# Optimizing a Trainium2 kernel written in Bass

```python
import jax, jax.numpy as jnp
from jax import lax
import numpy as np

D_MODEL = 1024
BATCH = 1
SEQ = 256
DEPTH = 2

HEAD_DIM = 64
BLOCK_Q = 128
ROPE_THETA = 10000.0
RMS_EPS = 1e-6
NEG_INF = -1e30
D_FF = 2816

NSA_HEADS = 8
NSA_KV_HEADS = 2
CMP_BLOCK = 32
CMP_STRIDE = 16
CMP_HIDDEN = 256
SLC_BLOCK = 64
N_SELECT = 16
NSA_WINDOW = 512
FORCE_SCORE = 1e9
SWA_HEADS = 8
SWA_KV_HEADS = 2
SWA_WINDOW = 128
FOX_HEADS = 8
MLA_HEADS = 8
MLA_Q_RANK = 256
MLA_KV_RANK = 128
MLA_NOPE_DIM = 64
MLA_ROPE_DIM = 32
MLA_V_DIM = 64

NSA_Q_COLS = NSA_HEADS * HEAD_DIM
NSA_KV_COLS = NSA_KV_HEADS * HEAD_DIM
NSA_GATE_COLS = 3 * NSA_HEADS
SWA_Q_COLS = SWA_HEADS * HEAD_DIM
SWA_KV_COLS = SWA_KV_HEADS * HEAD_DIM
EVEN_SPLITS = (NSA_Q_COLS,) + (NSA_KV_COLS,) * 6 + (NSA_GATE_COLS, SWA_Q_COLS, SWA_KV_COLS, SWA_KV_COLS)
EVEN_IN_COLS = sum(EVEN_SPLITS)
EVEN_OUT_COLS = NSA_Q_COLS + SWA_Q_COLS
FOX_COLS = FOX_HEADS * HEAD_DIM
ODD_SPLITS = (FOX_COLS, FOX_COLS, FOX_COLS, FOX_HEADS, MLA_Q_RANK, MLA_KV_RANK, MLA_ROPE_DIM)
ODD_IN_COLS = sum(ODD_SPLITS)
ODD_OUT_COLS = FOX_COLS + MLA_HEADS * MLA_V_DIM

kernel_name = 'hybrid_nsa_swa_fox_mla_macaron'

def rms_norm(x, g):
    xf = x.astype(jnp.float32)
    y = xf * lax.rsqrt(jnp.mean(xf * xf, axis=-1, keepdims=True) + RMS_EPS)
    return (y * g.astype(jnp.float32)).astype(x.dtype)

def rope_tables(seq, dim):
    inv_freq = 1.0 / (ROPE_THETA ** (jnp.arange(0, dim, 2, dtype=jnp.float32) / dim))
    ang = jnp.arange(seq, dtype=jnp.float32)[:, None] * inv_freq[None, :]
    return jnp.cos(ang), jnp.sin(ang)

def apply_rope(t, cos, sin):
    half = t.shape[-1] // 2
    t1, t2 = t[..., :half], t[..., half:]
    c = cos.astype(t.dtype)
    s = sin.astype(t.dtype)
    return jnp.concatenate([t1 * c - t2 * s, t2 * c + t1 * s], axis=-1)

def rope_tail(t, cos, sin):
    return jnp.concatenate([t[..., :-MLA_ROPE_DIM], apply_rope(t[..., -MLA_ROPE_DIM:], cos, sin)], axis=-1)

def masked_softmax(logits, mask):
    logits = jnp.where(mask, logits, NEG_INF)
    m = jnp.max(logits, axis=-1, keepdims=True)
    e = jnp.where(mask, jnp.exp(logits - m), 0.0)
    return e / jnp.maximum(jnp.sum(e, axis=-1, keepdims=True), 1e-30)

def swiglu(h, w_gate, w_up, w_down):
    return (jax.nn.silu(h @ w_gate) * (h @ w_up)) @ w_down

def split_cols(t, sizes):
    return jnp.split(t, np.cumsum(sizes)[:-1].tolist(), axis=-1)

def to_heads(t, n):
    B, S, C = t.shape
    return t.reshape(B, S, n, C // n).transpose(0, 2, 1, 3)

def merge_heads(t):
    B, H, S, D = t.shape
    return t.transpose(0, 2, 1, 3).reshape(B, S, H * D)

def banded_attention(q, k, v, window, sinks=None):
    B, Hk, G, S, D = q.shape
    Q = BLOCK_Q
    nb = -(-window // Q)
    nq = S // Q
    pad = ((0, 0), (0, 0), (nb * Q, 0), (0, 0))
    kp = jnp.pad(k, pad).reshape(B, Hk, nq + nb, Q, D)
    vp = jnp.pad(v, pad).reshape(B, Hk, nq + nb, Q, v.shape[-1])
    kb = jnp.concatenate([kp[:, :, j:j + nq] for j in range(nb + 1)], axis=3)
    vb = jnp.concatenate([vp[:, :, j:j + nq] for j in range(nb + 1)], axis=3)
    qb = q.reshape(B, Hk, G, nq, Q, D)
    logits = jnp.einsum('bhgnqd,bhnkd->bhgnqk', qb, kb).astype(jnp.float32) * (D ** -0.5)
    blk = jnp.arange(nq)[:, None, None] * Q
    t = blk + jnp.arange(Q)[None, :, None]
    s = blk - nb * Q + jnp.arange((nb + 1) * Q)[None, None, :]
    mask = (s >= 0) & (s <= t) & (t - s < window)
    logits = jnp.where(mask, logits, NEG_INF)
    m = jnp.max(logits, axis=-1, keepdims=True)
    if sinks is not None:
        sk = sinks.astype(jnp.float32).reshape(1, Hk, G, 1, 1, 1)
        m = jnp.maximum(m, sk)
    e = jnp.where(mask, jnp.exp(logits - m), 0.0)
    denom = jnp.sum(e, axis=-1, keepdims=True)
    if sinks is not None:
        denom = denom + jnp.exp(sk - m)
    p = (e / denom).astype(v.dtype)
    o = jnp.einsum('bhgnqk,bhnkd->bhgnqd', p, vb)
    return o.reshape(B, Hk, G, S, v.shape[-1])

def compress_blocks(t, pos_emb, w1, w2):
    B, Hk, S, D = t.shape
    ch = t.reshape(B, Hk, S // CMP_STRIDE, CMP_STRIDE, D)
    blocks = jnp.concatenate([ch[:, :, :-1], ch[:, :, 1:]], axis=3) + pos_emb
    flat = blocks.reshape(B, Hk, blocks.shape[2], CMP_BLOCK * D)
    return jax.nn.silu(flat @ w1) @ w2

def nsa_compressed_selected(q_cmp, q_slc, k_cmp, v_cmp, k_slc, v_slc):
    B, Hk, G, S, D = q_cmp.shape
    Q = BLOCK_Q
    nq = S // Q
    nc = k_cmp.shape[2]
    ns = S // SLC_BLOCK
    n_sel = min(N_SELECT, ns)
    scale = D ** -0.5
    c_start = jnp.arange(nc)[:, None] * CMP_STRIDE
    s_start = jnp.arange(ns)[None, :] * SLC_BLOCK
    overlap = jnp.maximum(jnp.minimum(c_start + CMP_BLOCK, s_start + SLC_BLOCK) - jnp.maximum(c_start, s_start), 0).astype(jnp.float32)
    cmp_end = jnp.arange(nc) * CMP_STRIDE + CMP_BLOCK - 1
    k_blocks = k_slc.reshape(B, Hk, ns, SLC_BLOCK * D)
    v_blocks = v_slc.reshape(B, Hk, ns, SLC_BLOCK * D)
    b_idx = jnp.arange(B)[:, None, None]
    h_idx = jnp.arange(Hk)[None, :, None]
    blk_ids = jnp.arange(ns)
    n_keys = n_sel * SLC_BLOCK

    def one_block(args):
        n, qc, qs = args
        t = n * Q + jnp.arange(Q)
        lc = jnp.einsum('bhgqd,bhcd->bhgqc', qc, k_cmp).astype(jnp.float32) * scale
        pc = masked_softmax(lc, cmp_end[None, :] <= t[:, None])
        o_c = jnp.einsum('bhgqc,bhcd->bhgqd', pc.astype(v_cmp.dtype), v_cmp)
        imp = jnp.einsum('bhgqc,cs->bhqs', pc, overlap)
        cur = (t // SLC_BLOCK)[:, None]
        forced = (blk_ids == 0) | (blk_ids == cur) | (blk_ids == cur - 1)
        score = jnp.where(forced, FORCE_SCORE, jnp.where(blk_ids <= cur, imp, NEG_INF))
        _, idx = lax.top_k(score, n_sel)
        flat = idx.reshape(B, Hk, Q * n_sel)
        ks = k_blocks[b_idx, h_idx, flat].reshape(B, Hk, Q, n_keys, D)
        vs = v_blocks[b_idx, h_idx, flat].reshape(B, Hk, Q, n_keys, D)
        kpos = (idx[..., None] * SLC_BLOCK + jnp.arange(SLC_BLOCK)).reshape(B, Hk, Q, n_keys)
        ls = jnp.einsum('bhgqd,bhqkd->bhgqk', qs, ks).astype(jnp.float32) * scale
        ps = masked_softmax(ls, (kpos <= t[:, None])[:, :, None])
        o_s = jnp.einsum('bhgqk,bhqkd->bhgqd', ps.astype(vs.dtype), vs)
        return o_c, o_s

    def to_blocks(a):
        return jnp.moveaxis(a.reshape(B, Hk, G, nq, Q, D), 3, 0)

    def from_blocks(a):
        return jnp.moveaxis(a, 0, 3).reshape(B, Hk, G, S, D)

    o_c, o_s = lax.map(one_block, (jnp.arange(nq), to_blocks(q_cmp), to_blocks(q_slc)))
    return from_blocks(o_c), from_blocks(o_s)

def causal_block_attention(q, k, v, decay_cum=None):
    B, H, S, Dk = q.shape
    Q = BLOCK_Q
    nq = S // Q
    scale = Dk ** -0.5
    key_pos = jnp.arange(S)
    qb = jnp.moveaxis(q.reshape(B, H, nq, Q, Dk), 2, 0)
    if decay_cum is None:
        xs = (jnp.arange(nq), qb)
    else:
        xs = (jnp.arange(nq), qb, jnp.moveaxis(decay_cum.reshape(B, H, nq, Q), 2, 0))

    def one_block(args):
        n, qi = args[0], args[1]
        t = n * Q + jnp.arange(Q)
        logits = jnp.einsum('bhqd,bhkd->bhqk', qi, k).astype(jnp.float32) * scale
        if decay_cum is not None:
            logits = logits + args[2][..., :, None] - decay_cum[:, :, None, :]
        p = masked_softmax(logits, key_pos[None, :] <= t[:, None])
        return jnp.einsum('bhqk,bhkd->bhqd', p.astype(v.dtype), v)

    o = lax.map(one_block, xs)
    return jnp.moveaxis(o, 0, 2).reshape(B, H, S, v.shape[-1])

def nsa_swa_mixer(h, w_in, nsa_gate_b, nsa_q_norm, nsa_kc_norm, nsa_ks_norm, nsa_kw_norm,
                  cmp_pos_k, cmp_pos_v, cmpk_w1, cmpk_w2, cmpv_w1, cmpv_w2,
                  swa_q_norm, swa_k_norm, swa_sinks, w_out):
    B, S, _ = h.shape
    (q_a, kc, vc, ks, vs, kw, vw, gate_logits, q_b, k_b, v_b) = split_cols(h @ w_in, EVEN_SPLITS)
    cos, sin = rope_tables(S, HEAD_DIM)
    ga = NSA_HEADS // NSA_KV_HEADS
    gb = SWA_HEADS // SWA_KV_HEADS
    qa = rms_norm(to_heads(q_a, NSA_HEADS), nsa_q_norm)
    qa_rot = apply_rope(qa, cos, sin)

    def grp(t):
        return t.reshape(B, NSA_KV_HEADS, ga, S, HEAD_DIM)

    k_cmp = rms_norm(compress_blocks(to_heads(kc, NSA_KV_HEADS), cmp_pos_k, cmpk_w1, cmpk_w2), nsa_kc_norm)
    v_cmp = compress_blocks(to_heads(vc, NSA_KV_HEADS), cmp_pos_v, cmpv_w1, cmpv_w2)
    k_slc = apply_rope(rms_norm(to_heads(ks, NSA_KV_HEADS), nsa_ks_norm), cos, sin)
    v_slc = to_heads(vs, NSA_KV_HEADS)
    k_win = apply_rope(rms_norm(to_heads(kw, NSA_KV_HEADS), nsa_kw_norm), cos, sin)
    v_win = to_heads(vw, NSA_KV_HEADS)
    o_cmp, o_slc = nsa_compressed_selected(grp(qa), grp(qa_rot), k_cmp, v_cmp, k_slc, v_slc)
    o_win = banded_attention(grp(qa_rot), k_win, v_win, NSA_WINDOW)
    gates = jax.nn.sigmoid(gate_logits + nsa_gate_b).reshape(B, S, NSA_HEADS, 3).transpose(0, 2, 1, 3)
    gates = gates.reshape(B, NSA_KV_HEADS, ga, S, 3)
    o_a = gates[..., 0:1] * o_cmp + gates[..., 1:2] * o_slc + gates[..., 2:3] * o_win
    o_a = o_a.reshape(B, NSA_HEADS, S, HEAD_DIM)
    qb = apply_rope(rms_norm(to_heads(q_b, SWA_HEADS), swa_q_norm), cos, sin)
    kb = apply_rope(rms_norm(to_heads(k_b, SWA_KV_HEADS), swa_k_norm), cos, sin)
    vb = to_heads(v_b, SWA_KV_HEADS)
    o_b = banded_attention(qb.reshape(B, SWA_KV_HEADS, gb, S, HEAD_DIM), kb, vb, SWA_WINDOW,
                           swa_sinks.reshape(SWA_KV_HEADS, gb))
    o_b = o_b.reshape(B, SWA_HEADS, S, HEAD_DIM)
    o = jnp.concatenate([merge_heads(o_a), merge_heads(o_b)], axis=-1)
    return o @ w_out

def fox_mla_mixer(h, w_in, fox_f_bias, fox_q_norm, fox_k_norm, mla_q_a_norm, mla_w_q_b,
                  mla_kv_a_norm, mla_w_kv_b, mla_q_norm, mla_k_norm, w_out):
    B, S, _ = h.shape
    q_c, k_c, v_c, f_c, c_q, c_kv, k_r = split_cols(h @ w_in, ODD_SPLITS)
    qf = rms_norm(to_heads(q_c, FOX_HEADS), fox_q_norm)
    kf = rms_norm(to_heads(k_c, FOX_HEADS), fox_k_norm)
    vf = to_heads(v_c, FOX_HEADS)
    log_f = jax.nn.log_sigmoid((f_c + fox_f_bias).astype(jnp.float32))
    decay_cum = jnp.cumsum(log_f, axis=1).transpose(0, 2, 1)
    o_fox = causal_block_attention(qf, kf, vf, decay_cum)
    qk_dim = MLA_NOPE_DIM + MLA_ROPE_DIM
    q = (rms_norm(c_q, mla_q_a_norm) @ mla_w_q_b).reshape(B, S, MLA_HEADS, qk_dim)
    kv = (rms_norm(c_kv, mla_kv_a_norm) @ mla_w_kv_b).reshape(B, S, MLA_HEADS, MLA_NOPE_DIM + MLA_V_DIM)
    k_nope, v_m = kv[..., :MLA_NOPE_DIM], kv[..., MLA_NOPE_DIM:]
    k_rope = jnp.broadcast_to(k_r[:, :, None, :], (B, S, MLA_HEADS, MLA_ROPE_DIM))
    k = jnp.concatenate([k_nope, k_rope], axis=-1)
    cos, sin = rope_tables(S, MLA_ROPE_DIM)
    q = rope_tail(rms_norm(q, mla_q_norm).transpose(0, 2, 1, 3), cos, sin)
    k = rope_tail(rms_norm(k, mla_k_norm).transpose(0, 2, 1, 3), cos, sin)
    o_mla = causal_block_attention(q, k, v_m.transpose(0, 2, 1, 3))
    o = jnp.concatenate([merge_heads(o_fox), merge_heads(o_mla)], axis=-1)
    return o @ w_out

def setup_inputs(seed: int = 0) -> dict:
    key = jax.random.key(seed)
    D, F, hd = D_MODEL, D_FF, HEAD_DIM

    def ffn(p):
        return [(p + 'norm', (D,), 'gain'), (p + 'w_gate', (D, F), 'w'),
                (p + 'w_up', (D, F), 'w'), (p + 'w_down', (F, D), 'w')]

    specs = [('x', (BATCH, SEQ, D), 'act')]
    specs += ffn('l0_ffn1_')
    specs += [('l0_mix_norm', (D,), 'gain'), ('l0_w_in', (D, EVEN_IN_COLS), 'w'),
              ('l0_nsa_gate_b', (NSA_GATE_COLS,), 'bias'),
              ('l0_nsa_q_norm', (hd,), 'gain'), ('l0_nsa_kc_norm', (hd,), 'gain'),
              ('l0_nsa_ks_norm', (hd,), 'gain'), ('l0_nsa_kw_norm', (hd,), 'gain'),
              ('l0_cmp_pos_k', (CMP_BLOCK, hd), 'bias'), ('l0_cmp_pos_v', (CMP_BLOCK, hd), 'bias'),
              ('l0_cmpk_w1', (CMP_BLOCK * hd, CMP_HIDDEN), 'w'), ('l0_cmpk_w2', (CMP_HIDDEN, hd), 'w'),
              ('l0_cmpv_w1', (CMP_BLOCK * hd, CMP_HIDDEN), 'w'), ('l0_cmpv_w2', (CMP_HIDDEN, hd), 'w'),
              ('l0_swa_q_norm', (hd,), 'gain'), ('l0_swa_k_norm', (hd,), 'gain'),
              ('l0_swa_sinks', (SWA_HEADS,), 'sink'), ('l0_w_out', (EVEN_OUT_COLS, D), 'w')]
    specs += ffn('l0_ffn2_')
    specs += ffn('l1_ffn1_')
    specs += [('l1_mix_norm', (D,), 'gain'), ('l1_w_in', (D, ODD_IN_COLS), 'w'),
              ('l1_fox_f_bias', (FOX_HEADS,), 'forget'),
              ('l1_fox_q_norm', (hd,), 'gain'), ('l1_fox_k_norm', (hd,), 'gain'),
              ('l1_mla_q_a_norm', (MLA_Q_RANK,), 'gain'),
              ('l1_mla_w_q_b', (MLA_Q_RANK, MLA_HEADS * (MLA_NOPE_DIM + MLA_ROPE_DIM)), 'w'),
              ('l1_mla_kv_a_norm', (MLA_KV_RANK,), 'gain'),
              ('l1_mla_w_kv_b', (MLA_KV_RANK, MLA_HEADS * (MLA_NOPE_DIM + MLA_V_DIM)), 'w'),
              ('l1_mla_q_norm', (MLA_NOPE_DIM + MLA_ROPE_DIM,), 'gain'),
              ('l1_mla_k_norm', (MLA_NOPE_DIM + MLA_ROPE_DIM,), 'gain'),
              ('l1_w_out', (ODD_OUT_COLS, D), 'w')]
    specs += ffn('l1_ffn2_')
    keys = jax.random.split(key, len(specs))
    out = {}
    for k, (name, shape, kind) in zip(keys, specs):
        if kind == 'act':
            val = jax.random.normal(k, shape, jnp.float32)
        elif kind == 'w':
            val = jax.random.normal(k, shape, jnp.float32) * (shape[0] ** -0.5)
        elif kind == 'gain':
            val = 1.0 + 0.02 * jax.random.normal(k, shape, jnp.float32)
        elif kind == 'bias':
            val = 0.02 * jax.random.normal(k, shape, jnp.float32)
        elif kind == 'sink':
            val = 0.5 * jax.random.normal(k, shape, jnp.float32)
        else:
            val = jax.random.uniform(k, shape, jnp.float32, minval=1.0, maxval=4.0)
        out[name] = val
    return out

def reference(x,
              l0_ffn1_norm, l0_ffn1_w_gate, l0_ffn1_w_up, l0_ffn1_w_down,
              l0_mix_norm, l0_w_in, l0_nsa_gate_b,
              l0_nsa_q_norm, l0_nsa_kc_norm, l0_nsa_ks_norm, l0_nsa_kw_norm,
              l0_cmp_pos_k, l0_cmp_pos_v, l0_cmpk_w1, l0_cmpk_w2, l0_cmpv_w1, l0_cmpv_w2,
              l0_swa_q_norm, l0_swa_k_norm, l0_swa_sinks, l0_w_out,
              l0_ffn2_norm, l0_ffn2_w_gate, l0_ffn2_w_up, l0_ffn2_w_down,
              l1_ffn1_norm, l1_ffn1_w_gate, l1_ffn1_w_up, l1_ffn1_w_down,
              l1_mix_norm, l1_w_in, l1_fox_f_bias, l1_fox_q_norm, l1_fox_k_norm,
              l1_mla_q_a_norm, l1_mla_w_q_b, l1_mla_kv_a_norm, l1_mla_w_kv_b,
              l1_mla_q_norm, l1_mla_k_norm, l1_w_out,
              l1_ffn2_norm, l1_ffn2_w_gate, l1_ffn2_w_up, l1_ffn2_w_down):
    ffn1 = [(l0_ffn1_norm, l0_ffn1_w_gate, l0_ffn1_w_up, l0_ffn1_w_down),
            (l1_ffn1_norm, l1_ffn1_w_gate, l1_ffn1_w_up, l1_ffn1_w_down)]
    ffn2 = [(l0_ffn2_norm, l0_ffn2_w_gate, l0_ffn2_w_up, l0_ffn2_w_down),
            (l1_ffn2_norm, l1_ffn2_w_gate, l1_ffn2_w_up, l1_ffn2_w_down)]
    mix_norms = [l0_mix_norm, l1_mix_norm]
    mix_params = [
        (l0_w_in, l0_nsa_gate_b, l0_nsa_q_norm, l0_nsa_kc_norm, l0_nsa_ks_norm, l0_nsa_kw_norm,
         l0_cmp_pos_k, l0_cmp_pos_v, l0_cmpk_w1, l0_cmpk_w2, l0_cmpv_w1, l0_cmpv_w2,
         l0_swa_q_norm, l0_swa_k_norm, l0_swa_sinks, l0_w_out),
        (l1_w_in, l1_fox_f_bias, l1_fox_q_norm, l1_fox_k_norm, l1_mla_q_a_norm, l1_mla_w_q_b,
         l1_mla_kv_a_norm, l1_mla_w_kv_b, l1_mla_q_norm, l1_mla_k_norm, l1_w_out)]
    mix_fns = (nsa_swa_mixer, fox_mla_mixer)
    for l in range(DEPTH):
        n1, g1, u1, d1 = ffn1[l]
        x = x + 0.5 * swiglu(rms_norm(x, n1), g1, u1, d1)
        x = x + mix_fns[l % 2](rms_norm(x, mix_norms[l]), *mix_params[l])
        n2, g2, u2, d2 = ffn2[l]
        x = x + 0.5 * swiglu(rms_norm(x, n2), g2, u2, d2)
    return x


_drawn_inputs = setup_inputs


def setup_inputs(seed=0):
    import zlib

    import numpy as np

    out = dict(_drawn_inputs(seed))
    spreads = {}
    factors = {'l0_ffn1_norm': 5.422,
     'l0_mix_norm': 7.042,
     'l0_nsa_gate_b': 8.0,
     'l0_nsa_q_norm': 8.0,
     'l0_nsa_kc_norm': 8.0,
     'l0_nsa_ks_norm': 8.0,
     'l0_nsa_kw_norm': 8.0,
     'l0_cmp_pos_k': 8.0,
     'l0_cmp_pos_v': 24.763,
     'l0_swa_q_norm': 8.0,
     'l0_swa_k_norm': 8.0,
     'l0_swa_sinks': 33.153,
     'l0_ffn2_norm': 6.605,
     'l1_ffn1_norm': 7.056,
     'l1_mix_norm': 6.705,
     'l1_fox_q_norm': 8.0,
     'l1_fox_k_norm': 21.944,
     'l1_mla_q_a_norm': 8.0,
     'l1_mla_kv_a_norm': 8.0,
     'l1_mla_q_norm': 8.0,
     'l1_mla_k_norm': 8.0,
     'l1_ffn2_norm': 24.449}
    for name, (base, spread) in spreads.items():
        noise = np.random.default_rng([zlib.crc32(name.encode()), seed]).standard_normal(out[name].shape)
        drawn = base * np.exp(spread * noise) if base else spread * noise
        out[name] = __import__('jax').numpy.asarray(drawn.astype(out[name].dtype))
    for name, factor in factors.items():
        out[name] = (out[name] * factor).astype(out[name].dtype)
    return out
```

```python
from contextlib import ExitStack

import numpy as np
import concourse.bass as bass
from concourse import mybir

F32 = mybir.dt.float32
F32R = mybir.dt.float32r
BF16 = mybir.dt.bfloat16
ALU = mybir.AluOpType
ACT = mybir.ActivationFunctionType
AX = mybir.AxisListType

P = 128
SEQ = 256
NT = SEQ // P
D = 1024
DC = D // P
FF = 2816
STEP = 256
NSTEP = FF // STEP
HD = 64
EPS = 1e-6
BIG = 1e30
NCMP = 15
CMPH = 256
CB, CS = 32, 16
UNIT = 2048
RAW, SPLIT = 3, 6
LEAD = 4

FFN_UNITS = 3 * NSTEP
M0_COLS = [(512, 256), (0, 256), (256, 256), (768, 256), (1024, 256), (1280, 24), (1304, 256), (1560, 256), (1816, 256)]
M1_COLS = [(1544, 256), (0, 256), (256, 256), (512, 256), (1800, 160), (768, 256), (1024, 256), (1280, 256), (1536, 8)]
NPROJ = 9
M0_UNITS = NPROJ + 4 + 4
M1_UNITS = NPROJ + 2 + 4
M0_SIZES = [DC * w for _, w in M0_COLS] + [UNIT] * 8
M1_SIZES = [DC * w for _, w in M1_COLS] + [2 * 768, 1024] + [UNIT] * 4
U_FFN = [0, FFN_UNITS + M0_UNITS, 2 * FFN_UNITS + M0_UNITS, 3 * FFN_UNITS + M0_UNITS + M1_UNITS]
U_M0 = FFN_UNITS
U_M1 = 3 * FFN_UNITS + M0_UNITS
U_END = 4 * FFN_UNITS + M0_UNITS + M1_UNITS
NORM_FFN = [0, 2, 3, 5]
NORM_M0, NORM_M1 = 1, 4

T_ID, T_TRI, T_CAUSAL, T_BAND = 0, 128, 384, 512
T_R64, T_R32, T_CNEG, T_C01, T_COLS = 640, 896, 1024, 1054, 1084
ROWS = {}
_at = 0
for _n, _w in (("l0_nsa_q_norm", 64), ("l0_nsa_kc_norm", 64), ("l0_nsa_ks_norm", 64), ("l0_nsa_kw_norm", 64),
               ("l0_swa_q_norm", 64), ("l0_swa_k_norm", 64), ("l0_swa_sinks", 8), ("l0_nsa_gate_b", 24),
               ("l1_fox_f_bias", 8), ("l1_fox_q_norm", 64), ("l1_fox_k_norm", 64),
               ("l1_mla_q_norm", 96), ("l1_mla_k_norm", 96)):
    ROWS[_n] = (_at, _w)
    _at += _w
ROWS_W = _at
COLS = {}
_at = 0
for _n, _w in (("l0_ffn1_norm", 8), ("l0_mix_norm", 8), ("l0_ffn2_norm", 8), ("l1_ffn1_norm", 8), ("l1_mix_norm", 8),
               ("l1_ffn2_norm", 8), ("l0_cmp_pos_k", 16), ("l0_cmp_pos_v", 16), ("l1_mla_q_a_norm", 2),
               ("l1_mla_kv_a_norm", 1)):
    COLS[_n] = (_at, _w)
    _at += _w
COLS_W = _at

A_M0, A_M1, A_END = 0, 6, 10
SLC, WIN, SWA, FOX, MLA = range(5)
ATT = [(SLC, 0), (SLC, 1), (WIN, 0), (WIN, 1), (SWA, 0), (SWA, 1), (FOX, 0), (FOX, 1), (MLA, 0), (MLA, 1)]
OUT_OF = {2: 0, 3: 1, 4: 2, 5: 3, 6: 4, 7: 5, 8: 6, 9: 7}
M0_TJOBS = [(1, "rot"), (1, "gain"), (2, "rot"), (2, "gain"), (3, "rot"), (4, "rot"), (6, "rot"), (7, "rot"), (8, "rot")]
M0_CHAINS = [1, 2, 3, 4, 6, 7, 8]
M1_CHAINS = [1, 2, 3, 5]


def trunk(nc, A, tables, out):
    ctx = ExitStack()
    with ctx:
        def sem(name):
            return ctx.enter_context(nc.semaphore(name))

        top = nc.sbuf_usable_end
        base = (nc.sbuf_base + 63) // 32 * 32
        slab = ctx.enter_context(nc.sbuf_tensor("slab", [P, (top - base) // 4 - 16], F32))
        place = [base]

        def at(name, shape, dt=F32, offset=None):
            size = int(np.prod(shape[1:])) * (2 if dt == BF16 else 4)
            here = place[0] if offset is None else offset
            if offset is None:
                place[0] = here + (size + 31) // 32 * 32
                assert place[0] <= top, (name, place[0] - top)
            return nc.alloc_sbuf_tensor_at(name, shape, dt, offset=here)

        raw = [at(f"raw{i}", [P, UNIT]) for i in range(RAW)]
        w_hi = [at(f"w_hi{i}", [P, UNIT], F32R) for i in range(SPLIT)]
        w_lo = [at(f"w_lo{i}", [P, UNIT], F32R) for i in range(SPLIT)]
        x = at("x_res", [P, NT, D])
        h_at = place[0]
        h_hi = at("h_hi", [P, DC, SEQ], F32R)
        h_lo = at("h_lo", [P, DC, SEQ], F32R)
        a_hi = at("a_hi", [P, 2, 2, SEQ], F32R)
        a_lo = at("a_lo", [P, 2, 2, SEQ], F32R)
        tab = at("tab", [P, T_COLS])
        rows = at("rows", [P, ROWS_W])
        cols = at("cols", [P, COLS_W])
        id_b = at("id_b", [P, P], BF16)
        zero_b = at("zero_b", [P, P], BF16)
        mask0 = at("mask0", [P, P], BF16)
        mask1 = at("mask1", [P, 2 * P], BF16)
        mask1w = at("mask1w", [P, 2 * P], BF16)
        ms = at("ms", [P, 6, NT])
        ms_eps = at("ms_eps", [P, 6, NT])
        rstd = at("rstd", [P, 6, NT])
        mhalf = at("mhalf", [P, 16])
        w2 = at("w2", [P, 2, 2, HD])
        arena = place[0]
        ident = tab[:, T_ID:T_ID + P]

        sg = at("sg", [P, 2 * SEQ])
        act_v = at("act_v", [P, 2 * SEQ])
        xn = at("xn", [P, NT, D])
        pstage = at("pstage", [COLS_W, P], offset=place[0])

        place[0] = arena
        p_at = arena
        prob = [at(f"prob{i}", [P, 4 * P + 4 * SEQ]) for i in range(2)]
        pT = at("pT", [P, 4 * SEQ + 4 * P])
        nmax = at("nmax", [P, 2, 8])
        nmax2 = at("nmax2", [P, 2, 8])
        den = at("den", [P, 2, 8])
        den2 = at("den2", [P, 2, 8])
        rden = at("rden", [P, 2, 8])
        gden = at("gden", [P, 2, 8])
        esink = at("esink", [P, 2, 8])
        zsink = at("zsink", [P, 2, 8])
        ssq = at("ssq", [P, 4, 8])
        ssq2 = at("ssq2", [P, 4, 8])
        srs = at("srs", [P, 4, 8])
        m_at = place[0]
        place[0] = p_at
        nat = [at(f"nat{i}", [P, NT, 256]) for i in range(2)]
        t1 = [at(f"t1_{i}", [P, NT, 256]) for i in range(2)]
        t2 = at("t2", [P, NT, 256])
        qg = at("qg", [P, NT, 256])
        flat = at("flat", [P, 2, CS, 30])
        glog = at("glog", [P, NT * 24])
        gden1 = at("gden1", [P, NT * 24])
        assert place[0] <= m_at
        place[0] = p_at
        nat1 = [at(f"nat1_{i}", [P, NT, 256]) for i in range(4)]
        sq1 = at("sq1", [P, NT, 4 * 96])
        natm = at("natm", [P, NT, 4 * 96])
        r1 = at("r1", [P, NT, 4 * 32])
        r2 = at("r2", [P, NT, 4 * 32])
        natkv = at("natkv", [P, NT, 160])
        assert place[0] <= m_at

        place[0] = m_at
        qaT = at("qaT", [P, 4, SEQ])
        qrT = at("qrT", [P, 4, SEQ])
        qbT = at("qbT", [P, 4, SEQ])
        kT = [at(f"kT{i}", [P, 2, SEQ]) for i in range(3)]
        vN = [at(f"vN{i}", [P, NT, 2 * HD]) for i in range(3)]
        rope_q = [at(f"rope_g{i}", [P, NT, P]) for i in range(5)]
        nsink = at("nsink", [P, 8])
        gate = at("gate", [P, NT * 24])
        place[0], m_end = h_at, place[0]
        pcT = at("pcT", [NCMP, 8, SEQ])
        hid = at("hid", [P, 2, 2, 30])
        kcv = at("kcv", [NCMP, 256])
        kc2 = at("kc2", [NCMP, P])
        kcd = at("kcd", [NCMP, 256])
        kcT = at("kcT", [P, 2, 16])
        lc = at("lc", [P, NT, 8, 16])
        lc_n = at("lc_n", [P, 16])
        lc_d = at("lc_d", [P, 16])
        lc_r = at("lc_r", [P, 16])
        assert place[0] <= h_at + 2 * DC * SEQ * 4
        place[0] = m_at
        qf_at = place[0]
        qfT = at("qfT", [P, 4, SEQ])
        kfT = at("kfT", [P, 4, SEQ])
        vf = at("vf", [P, NT, 512])
        negDT = at("negDT", [8, SEQ])
        dnat = at("dnat", [P, NT, 8])
        fz = at("fz", [P, 16])
        fa = at("fa", [P, 16])
        fe = at("fe", [P, 16])
        fl = at("fl", [P, 16])
        lf = at("lf", [P, NT, 8])
        vm = at("vm", [P, NT, 8, HD])
        kr = at("kr", [P, NT, 32])
        fgain = at("fgain", [P, 160])
        oA_hi = at("oA_hi", [P, 4, SEQ], F32R)
        oA_lo = at("oA_lo", [P, 4, SEQ], F32R)
        oB_hi = at("oB_hi", [P, 4, SEQ], F32R, offset=qf_at)
        oB_lo = at("oB_lo", [P, 4, SEQ], F32R, offset=qf_at + 4 * SEQ * 4)
        qmT = at("qmT", [96, 8, SEQ], offset=h_at)
        kmT = at("kmT", [96, 8, SEQ], offset=h_at + 8 * SEQ * 4)
        a_hi_flat = a_hi[:, :, :, :].rearrange("p a b c -> p (a b c)")
        a_lo_flat = a_lo[:, :, :, :].rearrange("p a b c -> p (a b c)")
        flat_hi, flat_lo = (v[:, 0:960].rearrange("p (m c b) -> p m c b", m=2, b=30) for v in (a_hi_flat, a_lo_flat))
        cq_hi, cq_lo = (v[:, 0:512].rearrange("p (c t) -> p c t", c=2) for v in (a_hi_flat, a_lo_flat))
        ckv_hi, ckv_lo = (v[:, 512:768] for v in (a_hi_flat, a_lo_flat))

        ps = ctx.enter_context(nc.psum_tensor("ps", [P, 8, 512], F32))

        x_loaded = sem("x_loaded")
        tab_loaded = sem("tab_loaded")
        par_loaded = sem("par_loaded")
        raw_loaded = [sem(f"raw_loaded{i}") for i in range(RAW)]
        hi_ready = sem("hi_ready")
        lo_ready = sem("lo_ready")
        unit_done = sem("unit_done")
        x_updated = sem("x_updated")
        sq_done = sem("sq_done")
        rstd_ready = sem("rstd_ready")
        xn_ready = sem("xn_ready")
        xT_ready = sem("xT_ready")
        hhi_ready = sem("hhi_ready")
        hlo_ready = sem("hlo_ready")
        silu_done = sem("silu_done")
        mul_done = sem("mul_done")
        ahi_ready = sem("ahi_ready")
        alo_ready = sem("alo_ready")
        acc_ready = sem("acc_ready")
        out_stored = sem("out_stored")
        const_ready = sem("const_ready")
        cast_ready = sem("cast_ready")
        parT_ready = sem("parT_ready")
        cols_ready = sem("cols_ready")
        pool_const = sem("pool_const")
        v_step = sem("v_step")
        g_step = sem("g_step")
        a_step = sem("a_step")
        nat_ready = sem("nat_ready")
        hsq_done = sem("hsq_done")
        hss_done = sem("hss_done")
        hrs_ready = sem("hrs_ready")
        hn_ready = sem("hn_ready")
        rot2_ready = sem("rot2_ready")
        rot_ready = sem("rot_ready")
        hT_done = sem("hT_done")
        hT_ready = sem("hT_ready")
        flat_built = sem("flat_built")
        flathi_ready = sem("flathi_ready")
        flatlo_ready = sem("flatlo_ready")
        hid_ready = sem("hid_ready")
        kcv_done = sem("kcv_done")
        kcv_ready = sem("kcv_ready")
        ksq_done = sem("ksq_done")
        kss_done = sem("kss_done")
        krs_ready = sem("krs_ready")
        kcn_ready = sem("kcn_ready")
        kcT_done = sem("kcT_done")
        kcT_ready = sem("kcT_ready")
        lc_done = sem("lc_done")
        lc_shift = sem("lc_shift")
        lc_exp = sem("lc_exp")
        pc_ready = sem("pc_ready")
        pcT_done = sem("pcT_done")
        pcT_ready = sem("pcT_ready")
        glog_ready = sem("glog_ready")
        gexp_ready = sem("gexp_ready")
        even_done = sem("even_done")
        qk_done = sem("qk_done")
        nmax_ready = sem("nmax_ready")
        zsink_ready = sem("zsink_ready")
        esink_ready = sem("esink_ready")
        exp_done = sem("exp_done")
        ps_ready = sem("ps_ready")
        pt_done = sem("pt_done")
        pTa_ready = sem("pTa_ready")
        pTb_ready = sem("pTb_ready")
        pv_done = sem("pv_done")
        ohi_ready = sem("ohi_ready")
        olo_ready = sem("olo_ready")
        cT_done = sem("cT_done")
        chi_ready = sem("chi_ready")
        clo_ready = sem("clo_ready")
        f_abs = sem("f_abs")
        f_ln = sem("f_ln")
        lf_ready = sem("lf_ready")
        dt_done = sem("dt_done")
        dt_ready = sem("dt_ready")
        natm_ready = sem("natm_ready")
        krep_ready = sem("krep_ready")
        msq_done = sem("msq_done")
        mss_done = sem("mss_done")
        mrs_ready = sem("mrs_ready")
        mg_ready = sem("mg_ready")
        mr2_ready = sem("mr2_ready")
        mrot_ready = sem("mrot_ready")
        mT_done = sem("mT_done")
        mT_ready = sem("mT_ready")

        block = ctx.enter_context(nc.Block())

        def row(name, scale_of=None):
            c, w = ROWS[name]
            return rows[:, c:c + w]

        def gain_col(norm, c):
            return cols[:, norm * 8 + c:norm * 8 + c + 1]

        ffn_names = [("l0_ffn1_", 0), ("l0_ffn2_", 1), ("l1_ffn1_", 2), ("l1_ffn2_", 3)]
        gates = [A[n + "w_gate"].rearrange("(k p) n -> p k n", p=P) for n, _ in ffn_names]
        ups = [A[n + "w_up"].rearrange("(k p) n -> p k n", p=P) for n, _ in ffn_names]
        downs = [A[n + "w_down"].rearrange("(c p) n -> p c n", p=P) for n, _ in ffn_names]

        def down_index(j):
            return 3 * j + 4 if j < NSTEP - 1 else 3 * NSTEP - 1

        def heads4(ap, h, w):
            return ap.rearrange("p t (h d) -> p t h d", d=w)[:, :, 0:h, :]

        @block.sync
        def _(sp):
            xv = A["x"][0, :, :].rearrange("(t p) d -> p t d", p=P)
            for t in range(NT):
                sp.dma_start(x[:, t, :], xv[:, t, :]).then_inc(x_loaded, 16)

            def load(u, dst, src):
                if not isinstance(u, int) or u >= RAW:
                    sp.wait_ge(lo_ready, u - (RAW - 1))
                return sp.dma_start(dst, src)

            def slot(u_static, size, inner):
                return raw[u_static % RAW][:, 0:size].rearrange("p (a b) -> p a b", b=inner)

            def ffn(f):
                u0 = U_FFN[f]

                def gate_up(u, us, c0):
                    for n, w in enumerate((gates[f], ups[f])):
                        load(u + n, slot(us + n, UNIT, STEP), w[:, :, bass.ds(c0, STEP)]).then_inc(raw_loaded[(us + n) % RAW], 16)

                gate_up(u0, u0, 0)
                with sp.Fori(0, (NSTEP - 1) // 2) as i:
                    for half in range(2):
                        us = u0 + 2 + 3 * half
                        gate_up(6 * i + us, us, (2 * i + 1 + half) * STEP)
                        load(6 * i + (us + 2), slot(us + 2, UNIT, D), downs[f][:, bass.ds((2 * i + half) * 2, 2), :])\
                            .then_inc(raw_loaded[(us + 2) % RAW], 16)
                u = u0 + FFN_UNITS - 1
                load(u, slot(u, UNIT, D), downs[f][:, 2 * NSTEP - 2:2 * NSTEP, :]).then_inc(raw_loaded[u % RAW], 16)

            def mixer(u0, w_in, spans, others, w_out):
                w = w_in.rearrange("(k p) n -> p k n", p=P)
                parts = [(w[:, :, c:c + n], n) for c, n in spans] + others
                wo = w_out.rearrange("(c p) n -> p c n", p=P)
                parts += [(wo[:, 2 * e:2 * e + 2, :], D) for e in range(4)]
                for n, (src, inner) in enumerate(parts):
                    u = u0 + n
                    load(u, slot(u, src.shape[1] * inner, inner), src).then_inc(raw_loaded[u % RAW], 16)

            ffn(0)
            w1k, w1v = (A[n].rearrange("(c p) n -> p c n", p=P) for n in ("l0_cmpk_w1", "l0_cmpv_w1"))
            mixer(U_M0, A["l0_w_in"], M0_COLS, [(w1[:, 8 * n:8 * n + 8, :], CMPH) for w1 in (w1k, w1v) for n in range(2)], A["l0_w_out"])
            ffn(1)
            ffn(2)
            mixer(U_M1, A["l1_w_in"], M1_COLS,
                  [(A["l1_mla_w_q_b"].rearrange("(c p) n -> p c n", p=P), 768),
                   (A["l1_mla_w_kv_b"].rearrange("(c p) n -> p c n", p=P), 1024)], A["l1_w_out"])
            ffn(3)
            ov = out[0, :, :].rearrange("(t p) d -> p t d", p=P)
            for t in range(NT):
                sp.wait_ge(x_updated, 10 + t + 1)
                sp.dma_start(ov[:, t, :], x[:, t, :]).then_inc(out_stored, 16)
            sp.wait_ge(out_stored, 16 * NT)

        @block.gpsimd
        def _(pool):
            steps = [0]

            def link(ins):
                steps[0] += 1
                ins.then_inc(g_step, 1)
                pool.wait_ge(g_step, steps[0])

            def norm(m):
                for t in range(NT):
                    pool.wait_ge(sq_done, NT * m + t + 1)
                    link(nc.gpsimd.tensor_scalar(ms_eps[:, m, t:t + 1], ms[:, m, t:t + 1], 1.0, EPS, ALU.mult, ALU.add))
                    nc.gpsimd.tensor_tensor(rstd[:, m, t:t + 1], ms_eps[:, m, t:t + 1], mhalf[:, 0:1], ALU.pow)\
                        .then_inc(rstd_ready, 1)

            def inverse_rms(dst, tmp, src, width, n, signal, parts=P):
                link(nc.gpsimd.tensor_scalar(tmp[0:parts, 0:n], src[0:parts, 0:n], 1.0 / width, EPS, ALU.mult, ALU.add))
                nc.gpsimd.tensor_tensor(dst[0:parts, 0:n], tmp[0:parts, 0:n], mhalf[0:parts, 0:n], ALU.pow).then_inc(signal, 1)

            def chain_squares(n, src, dst):
                nc.gpsimd.tensor_tensor(dst, src, src, ALU.mult).then_inc(hsq_done, 1)

            def mixer0():
                for n, u in enumerate(M0_CHAINS):
                    h = 4 if u in (1, 2, 6, 7) else 2
                    w = h * HD
                    src = nat[u % 2][:, :, 0:w]
                    pool.wait_ge(nat_ready, u if u < 5 else u - 1)
                    if n:
                        pool.wait_ge(rot_ready, n)
                    nc.gpsimd.tensor_tensor(t2[:, :, 0:w], src, src, ALU.mult).then_inc(hsq_done, 1)
                    pool.wait_ge(hss_done, n + 1)
                    inverse_rms(srs[:, n % 4, :], ssq2[:, n % 4, :], ssq[:, n % 4, :], HD, NT * h, hrs_ready)
                    pool.wait_ge(hn_ready, n + 1)
                    table = rope_q[{1: 0, 2: 0, 3: 1, 4: 2, 6: 3, 7: 3, 8: 4}[u]]
                    for half in range(2):
                        a, b = (32 * half, 32 - 32 * half)
                        z = heads4(nat[u % 2][:, :, :], h, HD)[:, :, :, b:b + 32]
                        s = table[:, :, None, HD + a:HD + a + 32].to_broadcast([P, NT, h, 32])
                        ins = nc.gpsimd.tensor_tensor(heads4(t2[:, :, :], h, HD)[:, :, :, a:a + 32], z, s, ALU.mult)
                    ins.then_inc(rot2_ready, 1)
                pool.wait_ge(kcv_ready, 1)
                nc.gpsimd.tensor_tensor(kc2[:, :], kcv[:, 0:P], kcv[:, 0:P], ALU.mult).then_inc(ksq_done, 1)
                pool.wait_ge(kss_done, 1)
                inverse_rms(srs[:, 3, :], ssq2[:, 3, :], ssq[:, 3, :], HD, 2, krs_ready, parts=NCMP)

            def mixer1():
                c0 = len(M0_CHAINS)
                for n, u in enumerate((0, 1, 2, 3, 4, 5)):
                    pool.wait_ge(nat_ready, len(M0_CHAINS) + u + 1)
                    if n:
                        pool.wait_ge(rot_ready, c0 + n)
                    w = {0: 256, 4: 128}.get(u, 256)
                    src = natkv[:, :, 0:w] if u == 4 else nat1[u % 4][:, :, 0:w]
                    nc.gpsimd.tensor_tensor(sq1[:, :, 0:w], src, src, ALU.mult).then_inc(hsq_done, 1)
                    pool.wait_ge(hss_done, c0 + n + 1)
                    width, cnt = {0: (256, 2), 4: (128, 2)}.get(u, (HD, 8))
                    inverse_rms(srs[:, n % 4, :], ssq2[:, n % 4, :], ssq[:, n % 4, :], width, cnt, hrs_ready)
                for n in range(4):
                    pool.wait_ge(natm_ready, n + 1)
                    if n >= 2:
                        link(nc.gpsimd.tensor_copy(heads4(natm[:, :, :], 4, 96)[:, :, :, 64:96],
                                                   kr[:, :, None, :].to_broadcast([P, NT, 4, 32])))
                    nc.gpsimd.tensor_tensor(sq1[:, :, :], natm[:, :, :], natm[:, :, :], ALU.mult).then_inc(msq_done, 1)
                    pool.wait_ge(mss_done, n + 1)
                    inverse_rms(srs[:, n % 4, :], ssq2[:, n % 4, :], ssq[:, n % 4, :], 96, 8, mrs_ready)
                    pool.wait_ge(mg_ready, n + 1)
                    for half in range(2):
                        a, b = (16 * half, 16 - 16 * half)
                        z = heads4(natm[:, :, :], 4, 96)[:, :, :, 64 + b:80 + b]
                        s = tab[:, T_R32:T_R32 + 128].rearrange("p (t c) -> p t c", t=NT)[:, :, None, 32 + a:48 + a]\
                            .to_broadcast([P, NT, 4, 16])
                        ins = nc.gpsimd.tensor_tensor(heads4(r2[:, :, :], 4, 32)[:, :, :, a:a + 16], z, s, ALU.mult)
                    ins.then_inc(mr2_ready, 1)

            nc.gpsimd.memset(mhalf[:, :], -0.5).then_inc(pool_const, 1)
            pool.wait_ge(pool_const, 1)
            norm(0)
            norm(1)
            mixer0()
            norm(2)
            norm(3)
            norm(4)
            mixer1()
            norm(5)

        @block.scalar
        def _(act):
            def split(u, us, size=UNIT):
                s = us % RAW
                act.wait_ge(raw_loaded[s], 16 * bass_div(u, us, s) + 16)
                if not isinstance(u, int) or u >= SPLIT:
                    act.wait_ge(unit_done, u - (SPLIT - 1))
                nc.scalar.activation(w_hi[us % SPLIT][:, 0:size], raw[s][:, 0:size], ACT.Copy).then_inc(hi_ready, 1)

            def bass_div(u, us, s):
                if isinstance(u, int):
                    return (u - s) // RAW
                return u.over_raw

            def split_list(u0, sizes, n):
                if n < len(sizes):
                    split(u0 + n, u0 + n, sizes[n])
                elif u0 + n < U_END:
                    split(u0 + n, u0 + n)

            def norm(m):
                for t in range(NT):
                    if m == 0:
                        act.wait_ge(x_loaded, 16 * NT)
                    else:
                        act.wait_ge(x_updated, NT * (m - 1) + t + 1)
                    nc.scalar.activation(xn[:, t, :], x[:, t, :], ACT.Square, scale=D ** -0.5,
                                         accum_out=ms[:, m, t:t + 1]).then_inc(sq_done, 1)
                if m == 0:
                    act.wait_ge(parT_ready, 1)
                    nc.scalar.activation(cols[:, :], ps[:, 5, 0:COLS_W], ACT.Copy).then_inc(cols_ready, 1)
                    act.wait_ge(cols_ready, 1)
                for c in range(DC):
                    if c % 2 == 0:
                        act.wait_ge(xT_ready, 4 * m + c // 2 + 1)
                    src = ps[:, 6 + c // 2 % 2, (c % 2) * SEQ:(c % 2 + 1) * SEQ]
                    nc.scalar.activation(h_hi[:, c, :], src, ACT.Copy, scale=gain_col(m, c)).then_inc(hhi_ready, 1)

            def ffn(f, last):
                u0 = U_FFN[f]

                def step(j, js):
                    for n in range(3):
                        u = 3 * js + 4 + n
                        if isinstance(j, int):
                            if u0 + u < U_END:
                                split(u0 + u, u0 + u)
                        else:
                            i = j
                            us = u0 + u
                            s = us % RAW
                            act.wait_ge(raw_loaded[s], 32 * i + (16 * ((us - s) // RAW) + 16))
                            act.wait_ge(unit_done, 6 * i + (us - (SPLIT - 1)))
                            nc.scalar.activation(w_hi[us % SPLIT][:, :], raw[s][:, :], ACT.Copy).then_inc(hi_ready, 1)
                    bank = 4 + 2 * (js % 2)
                    up = u0 + (3 * js + 1 if js else 2)
                    done = 11 * f + js + 1
                    if not isinstance(j, int):
                        up, done = 6 * j + up, 2 * j + done
                    act.wait_ge(unit_done, up)
                    nc.scalar.activation(sg[:, :].rearrange("p (b n) -> p b n", b=2), ps[:, bank:bank + 2, 0:SEQ],
                                         ACT.Silu).then_inc(silu_done, 1)
                    act.wait_ge(mul_done, done)
                    nc.scalar.activation(a_hi[:, js % 2, :, :].rearrange("p b n -> p (b n)"), act_v[:, :],
                                         ACT.Copy).then_inc(ahi_ready, 1)

                step(0, 0)
                n_loop = (NSTEP - 1) // 2 - (1 if last else 0)
                with act.Fori(0, n_loop) as i:
                    for half in range(2):
                        step(i, 1 + half)
                if last:
                    step(NSTEP - 2, NSTEP - 2)
                    step(NSTEP - 1, NSTEP - 1)

            def att_exp(a):
                kind, g = ATT[a]
                act.wait_ge(nmax_ready, a + 1)
                if a >= 2:
                    act.wait_ge(pt_done, a - 1)
                pr = prob[a % 2]
                s = a % 2
                if kind == SWA:
                    nc.scalar.activation(esink[:, s, :], zsink[:, s, :], ACT.Exp).then_inc(esink_ready, 1)
                for h in range(4):
                    nc.scalar.activation(pr[:, h * P:(h + 1) * P], ps[:, 2, h * P:(h + 1) * P], ACT.Exp,
                                         bias=nmax[:, s, h:h + 1], accum_out=den[:, s, h:h + 1])
                for h in range(4):
                    ins = nc.scalar.activation(pr[:, 4 * P + h * SEQ:4 * P + (h + 1) * SEQ],
                                               ps[:, 3 + h % 2, (h // 2) * SEQ:(h // 2 + 1) * SEQ], ACT.Exp,
                                               bias=nmax[:, s, 4 + h:5 + h], accum_out=den[:, s, 4 + h:5 + h])
                ins.then_inc(exp_done, 1)

            def att_evac(a):
                act.wait_ge(pt_done, a + 1)
                if a:
                    act.wait_ge(pv_done, a)
                dst = pT[:, 0:4 * SEQ].rearrange("p (h b q) -> p b h q", h=4, b=2)
                src = ps[:, 5:7, :].rearrange("p b (h q) -> p b h q", h=4)
                for b in range(2):
                    ins = nc.scalar.activation(dst[:, b, :, :], src[:, b, :, :], ACT.Copy)
                ins.then_inc(pTa_ready, 1)

            def o_parts(e):
                if e < 4:
                    return h_hi[:, 2 * e:2 * e + 2, :], h_lo[:, 2 * e:2 * e + 2, :]
                hi, lo = (oA_hi, oA_lo) if e < 6 else (oB_hi, oB_lo)
                c = 2 * (e % 2)
                return hi[:, c:c + 2, :], lo[:, c:c + 2, :]

            def att_out(a):
                if a in OUT_OF:
                    e = OUT_OF[a]
                    act.wait_ge(pv_done, a + 1)
                    if e == 6:
                        act.wait_ge(qk_done, 8)
                    hi, _ = o_parts(e)
                    nc.scalar.activation(hi.rearrange("p c t -> p (c t)"), ps[:, e % 2, :], ACT.Copy).then_inc(ohi_ready, 1)

            def attention(a0, a1):
                att_exp(a0)
                for a in range(a0, a1):
                    if a + 1 < a1:
                        att_exp(a + 1)
                    att_evac(a)
                    att_out(a)

            def copy_T(job_bank, dst):
                nc.scalar.activation(dst, ps[:, job_bank, :], ACT.Copy).then_inc(hT_ready, 1)

            def mixer0():
                u0 = U_M0
                job_dst = [qrT[:, 0:2, :], qaT[:, 0:2, :], qrT[:, 2:4, :], qaT[:, 2:4, :], kT[0][:, :, :], kT[1][:, :, :],
                           qbT[:, 0:2, :], qbT[:, 2:4, :], kT[2][:, :, :]]

                def t_evac(j):
                    act.wait_ge(hT_done, j + 1)
                    copy_T(5 + j % 3, job_dst[j].rearrange("p c t -> p (c t)"))

                def nat_evac(u):
                    act.wait_ge(unit_done, u0 + u + 1)
                    src = ps[:, (u - 1) % 4, :].rearrange("p (t n) -> p t n", t=NT)
                    if u >= 3:
                        act.wait_ge(rot_ready, {3: 1, 4: 2, 6: 4, 7: 4, 8: 5}[u])
                    if u in (3, 4, 8):
                        nc.scalar.activation(nat[u % 2][:, :, 0:P], src[:, :, 0:P], ACT.Copy)
                        nc.scalar.activation(vN[{3: 0, 4: 1, 8: 2}[u]][:, :, :], src[:, :, P:2 * P], ACT.Copy).then_inc(nat_ready, 1)
                    else:
                        nc.scalar.activation(nat[u % 2][:, :, :], src, ACT.Copy).then_inc(nat_ready, 1)

                split_list(u0, M0_SIZES, 4)
                act.wait_ge(flat_built, 1)
                nc.scalar.activation(flat_hi, flat[:, :, :, :], ACT.Copy).then_inc(flathi_ready, 1)
                after = {3: (0, 1), 4: (2, 3), 6: (4, 5), 7: (), 8: (6,)}
                for u in range(1, NPROJ):
                    split_list(u0, M0_SIZES, u + 4)
                    if u == 5:
                        act.wait_ge(glog_ready, 1)
                        nc.scalar.activation(gden1[:, :], glog[:, :], ACT.Exp, scale=-1.0).then_inc(gexp_ready, 1)
                    else:
                        nat_evac(u)
                    for j in after.get(u, ()):
                        t_evac(j)
                for n in (13, 14):
                    split_list(u0, M0_SIZES, n)
                t_evac(7)
                t_evac(8)
                for m in range(2):
                    act.wait_ge(unit_done, u0 + 9 + 2 * m + 2)
                    nc.scalar.activation(hid[:, m, :, :], ps[:, 2 * m:2 * m + 2, 0:30], ACT.Silu).then_inc(hid_ready, 1)
                for n in (15, 16, 17, 18):
                    split_list(u0, M0_SIZES, n)
                act.wait_ge(kcv_done, 1)
                nc.scalar.activation(kcv[:, :], ps[0:NCMP, 4, 0:256], ACT.Copy).then_inc(kcv_ready, 1)
                act.wait_ge(kcT_done, 1)
                nc.scalar.activation(kcT[:, :, 0:NCMP], ps[:, 5, 0:32].rearrange("p (g c) -> p g c", g=2)[:, :, 0:NCMP],
                                     ACT.Copy).then_inc(kcT_ready, 1)
                act.wait_ge(lc_shift, 1)
                nc.scalar.activation(lc[:, :, :, 0:NCMP].rearrange("p t h c -> p (t h) c"),
                                     lc[:, :, :, 0:NCMP].rearrange("p t h c -> p (t h) c"), ACT.Exp).then_inc(lc_exp, 1)
                act.wait_ge(pcT_done, 1)
                for b in range(4):
                    ins = nc.scalar.activation(pcT[:, 2 * b:2 * b + 2, :].rearrange("p h t -> p (h t)"), ps[0:NCMP, 4 + b, :], ACT.Copy)
                ins.then_inc(pcT_ready, 1)
                attention(A_M0, A_M1)
                for n in (19, 20):
                    split_list(u0, M0_SIZES, n)

            def mixer1():
                u0 = U_M1
                o0 = len(M0_TJOBS)

                def t_evac(j):
                    act.wait_ge(hT_done, o0 + j + 1)
                    dst = (qfT[:, 0:2, :], qfT[:, 2:4, :], kfT[:, 0:2, :], kfT[:, 2:4, :])[j]
                    copy_T(4 + j, dst.rearrange("p c t -> p (c t)"))

                def c_hi(n):
                    act.wait_ge(cT_done, n + 1)
                    if n == 0:
                        c = COLS["l1_mla_q_a_norm"][0]
                        for k in range(2):
                            ins = nc.scalar.activation(cq_hi[:, k, :], ps[:, 5, k * SEQ:(k + 1) * SEQ], ACT.Copy, scale=cols[:, c + k:c + k + 1])
                    else:
                        c = COLS["l1_mla_kv_a_norm"][0]
                        ins = nc.scalar.activation(ckv_hi, ps[:, 6, 0:SEQ], ACT.Copy, scale=cols[:, c:c + 1])
                    ins.then_inc(chi_ready, 1)

                for u in range(NPROJ):
                    split_list(u0, M1_SIZES, u + 4)
                    if u < 8:
                        act.wait_ge(unit_done, u0 + u + 1)
                    src = ps[:, u % 4, :].rearrange("p (t n) -> p t n", t=NT)
                    c0 = len(M0_CHAINS)
                    if u in (2, 3):
                        act.wait_ge(rot_ready, c0 + u - 1)
                    if u == 5:
                        act.wait_ge(rot_ready, c0 + 4)
                    if u in (0, 1, 2, 3, 5):
                        nc.scalar.activation(nat1[u % 4][:, :, :], src, ACT.Copy).then_inc(nat_ready, 1)
                    elif u == 4:
                        nc.scalar.activation(natkv[:, :, :], src[:, :, 0:160], ACT.Copy).then_inc(nat_ready, 1)
                        nc.scalar.activation(kr[:, :, :], src[:, :, P:160], ACT.Copy)
                    elif u in (6, 7):
                        nc.scalar.activation(vf[:, :, (u - 6) * 256:(u - 5) * 256], src, ACT.Copy).then_inc(nat_ready, 1)
                    if u == 2:
                        c_hi(0)
                    if u == 4:
                        t_evac(0)
                    if u == 5:
                        t_evac(1)
                    if u == 6:
                        t_evac(2)
                        c_hi(1)
                    if u == 8:
                        t_evac(3)
                act.wait_ge(f_abs, 1)
                nc.scalar.activation(fe[:, :], fa[:, :], ACT.Exp, scale=-1.0).then_inc(a_step, 1)
                act.wait_ge(a_step, 1)
                nc.scalar.activation(fl[:, :], fe[:, :], ACT.Ln, bias=1.0).then_inc(f_ln, 1)
                split_list(u0, M1_SIZES, 13)
                act.wait_ge(unit_done, u0 + 10)
                for n in range(4):
                    half = n % 2
                    if n == 2:
                        act.wait_ge(unit_done, u0 + 11)
                    if n:
                        act.wait_ge(mT_done, n)
                    else:
                        act.wait_ge(rot_ready, len(M0_CHAINS) + 6)
                    b = 2 * half
                    if n < 2:
                        nc.scalar.activation(natm[:, :, :], ps[:, b:b + 2, 0:384], ACT.Copy).then_inc(natm_ready, 1)
                    else:
                        kv = ps[:, b:b + 2, :].rearrange("p t (h d) -> p t h d", d=P)
                        for t in range(NT):
                            nc.scalar.activation(heads4(natm[:, :, :], 4, 96)[:, t, :, 0:HD], kv[:, t, :, 0:HD], ACT.Copy)
                            ins = nc.scalar.activation(vm[:, t, 4 * half:4 * half + 4, :], kv[:, t, :, HD:P], ACT.Copy)
                        ins.then_inc(natm_ready, 1)
                    if n:
                        m_evac(n - 1)
                m_evac(3)
                for n in (14, 15, 16):
                    split_list(u0, M1_SIZES, n)
                attention(A_M1, A_END)
                for n in (17, 18):
                    split_list(u0, M1_SIZES, n)

            def m_evac(n):
                act.wait_ge(mT_done, n + 1)
                dst = (qmT if n < 2 else kmT)[:, 4 * (n % 2):4 * (n % 2) + 4, :]
                b = 4 + 2 * (n % 2)
                for k in range(2):
                    ins = nc.scalar.activation(dst[:, 2 * k:2 * k + 2, :].rearrange("p h t -> p (h t)"), ps[0:96, b + k, :], ACT.Copy)
                ins.then_inc(mT_ready, 1)

            act.dma_start(tab[:, :], tables).then_inc(tab_loaded, 16)
            n_par = 0
            for name, (r, w) in COLS.items():
                src = A[name]
                src = src.rearrange("(a b) -> a b", b=P) if len(src.shape) == 1 else src.rearrange("(c j) d -> c (j d)", j=2)
                act.dma_start(pstage[r:r + w, :], src).then_inc(par_loaded, 16)
                n_par += 1
            for name, (c, w) in ROWS.items():
                act.dma_start(rows[:, c:c + w], A[name].partition_broadcast(P)).then_inc(par_loaded, 16)
                n_par += 1
            for m, name in enumerate(("l0_cmpk_w2", "l0_cmpv_w2")):
                act.dma_start(w2[:, m, :, :], A[name].rearrange("(c p) n -> p c n", p=P)).then_inc(par_loaded, 16)
                n_par += 1
            act.wait_ge(tab_loaded, 16)
            nc.scalar.activation(id_b[:, :], ident, ACT.Copy)
            nc.scalar.activation(mask0[:, :], tab[:, T_CAUSAL:T_CAUSAL + P], ACT.Copy)
            nc.scalar.activation(mask1[:, P:2 * P], tab[:, T_CAUSAL:T_CAUSAL + P], ACT.Copy)
            nc.scalar.activation(mask1w[:, P:2 * P], tab[:, T_CAUSAL:T_CAUSAL + P], ACT.Copy)
            nc.scalar.activation(mask1w[:, 0:P], tab[:, T_BAND:T_BAND + P], ACT.Copy).then_inc(cast_ready, 1)
            norm(0)
            for n in range(LEAD):
                split(n, n)
            ffn(0, False)
            norm(1)
            mixer0()
            norm(2)
            ffn(1, False)
            norm(3)
            ffn(2, False)
            norm(4)
            mixer1()
            norm(5)
            ffn(3, True)

        @block.vector
        def _(dve):
            steps = [0]

            def link(ins):
                steps[0] += 1
                ins.then_inc(v_step, 1)
                dve.wait_ge(v_step, steps[0])

            def split(u, us, size=UNIT):
                dve.wait_ge(hi_ready, u + 1)
                nc.vector.tensor_tensor(w_lo[us % SPLIT][:, 0:size], raw[us % RAW][:, 0:size],
                                        w_hi[us % SPLIT][:, 0:size].bitcast(F32), ALU.subtract).then_inc(lo_ready, 1)

            def split_list(u0, sizes, n):
                if n < len(sizes):
                    split(u0 + n, u0 + n, sizes[n])
                elif u0 + n < U_END:
                    split(u0 + n, u0 + n)

            def norm(m):
                for t in range(NT):
                    dve.wait_ge(rstd_ready, NT * m + t + 1)
                    nc.vector.tensor_scalar(xn[:, t, :], x[:, t, :], rstd[:, m, t:t + 1], None, ALU.mult).then_inc(xn_ready, 1)
                for c in range(DC):
                    dve.wait_ge(hhi_ready, DC * m + 2 * (c // 2) + 2)
                    src = ps[:, 6 + c // 2 % 2, (c % 2) * SEQ:(c % 2 + 1) * SEQ]
                    nc.vector.scalar_tensor_tensor(out=h_lo[:, c, :], in0=src, scalar=gain_col(m, c), in1=h_hi[:, c, :].bitcast(F32),
                                                   op0=ALU.mult, op1=ALU.subtract).then_inc(hlo_ready, 1)

            def add_to_x(m, bank, scale, last_unit):
                for t in range(NT):
                    if t == 0:
                        dve.wait_ge(acc_ready, m + 1)
                    else:
                        dve.wait_ge(unit_done, last_unit + 1)
                    b = bank + 2 * t
                    nc.vector.scalar_tensor_tensor(out=x[:, t, :], in0=ps[:, b:b + 2, :].rearrange("p b n -> p (b n)"), scalar=scale,
                                                   in1=x[:, t, :], op0=ALU.mult, op1=ALU.add).then_inc(x_updated, 1)

            def ffn(f, last):
                u0 = U_FFN[f]

                def step(j, js):
                    loop = not isinstance(j, int)
                    for n in range(3):
                        us = u0 + 3 * js + 4 + n
                        if loop:
                            split(6 * j + us, us)
                        elif us < U_END:
                            split(us, us)
                    bank = 4 + 2 * (js % 2)
                    done = 11 * f + js + 1
                    if loop:
                        done = 2 * j + done
                    if loop or done > 1:
                        dve.wait_ge(alo_ready, done - 1)
                    dve.wait_ge(silu_done, done)
                    nc.vector.tensor_tensor(act_v[:, :].rearrange("p (b n) -> p b n", b=2), sg[:, :].rearrange("p (b n) -> p b n", b=2),
                                            ps[:, bank:bank + 2, SEQ:2 * SEQ], ALU.mult).then_inc(mul_done, 1)
                    dve.wait_ge(ahi_ready, done)
                    nc.vector.tensor_tensor(a_lo[:, js % 2, :, :].rearrange("p b n -> p (b n)"), act_v[:, :],
                                            a_hi[:, js % 2, :, :].rearrange("p b n -> p (b n)").bitcast(F32),
                                            ALU.subtract).then_inc(alo_ready, 1)

                step(0, 0)
                with dve.Fori(0, (NSTEP - 1) // 2 - (1 if last else 0)) as i:
                    for half in range(2):
                        step(i, 1 + half)
                if last:
                    step(NSTEP - 2, NSTEP - 2)
                    step(NSTEP - 1, NSTEP - 1)
                add_to_x(NORM_FFN[f], 0, 0.5, u0 + FFN_UNITS - 1)

            def att_max(a):
                kind, g = ATT[a]
                s = a % 2
                dve.wait_ge(qk_done, a + 1)
                if a >= 2:
                    dve.wait_ge(exp_done, a - 1)
                first = nmax2 if kind in (SWA, FOX) else nmax
                nc.vector.tensor_reduce(first[:, s, 0:4], ps[:, 2, :].rearrange("p (h k) -> p h k", h=4), AX.X, ALU.max, negate=True)\
                    .then_inc(v_step, 1)
                steps[0] += 1
                ins = nc.vector.tensor_reduce(first[:, s, 4:8].rearrange("p (i b) -> p b i", b=2), ps[:, 3:5, :].rearrange("p b (i k) -> p b i k", i=2),
                                              AX.X, ALU.max, negate=True)
                if kind in (SLC, WIN, MLA):
                    ins.then_inc(nmax_ready, 1)
                    return
                link(ins)
                two = lambda ap: ap.rearrange("p (b h) -> p b h", b=2)
                if kind == SWA:
                    sk = ROWS["l0_swa_sinks"][0] + 4 * g
                    link(nc.vector.tensor_tensor(two(nmax[:, s, :]), two(nmax2[:, s, :]),
                                                 nsink[:, None, 4 * g:4 * g + 4].to_broadcast([P, 2, 4]), ALU.min))
                    nc.vector.tensor_tensor(two(zsink[:, s, :]), two(nmax[:, s, :]),
                                            rows[:, None, sk:sk + 4].to_broadcast([P, 2, 4]), ALU.add).then_inc(nmax_ready, 1)
                else:
                    dn = dnat[:, :, 4 * g:4 * g + 4]
                    link(nc.vector.tensor_tensor(two(nmax2[:, s, :]), two(nmax2[:, s, :]), dn, ALU.subtract))
                    nc.vector.tensor_tensor(two(nmax[:, s, :]), two(nmax2[:, s, :]), dn, ALU.add).then_inc(nmax_ready, 1)

            def att_scale(a):
                kind, g = ATT[a]
                s = a % 2
                dve.wait_ge(exp_done, a + 1)
                d = den
                if kind == SWA:
                    dve.wait_ge(esink_ready, a - 3)
                    link(nc.vector.tensor_tensor(den2[:, s, :], den[:, s, :], esink[:, s, :], ALU.add))
                    d = den2
                link(nc.vector.reciprocal(rden[:, s, :], d[:, s, :]))
                r = rden
                if kind in (SLC, WIN):
                    gv = gate[:, :].rearrange("p (t h b) -> p t h b", t=NT, b=3)[:, :, 4 * g:4 * g + 4, 1 if kind == SLC else 2]
                    link(nc.vector.tensor_tensor(gden[:, s, :].rearrange("p (t h) -> p t h", t=NT),
                                                 rden[:, s, :].rearrange("p (t h) -> p t h", t=NT), gv, ALU.mult))
                    r = gden
                pr = prob[a % 2]
                p0 = pr[:, 0:4 * P].rearrange("p (h k) -> p h k", h=4)
                p1 = pr[:, 4 * P:4 * P + 4 * SEQ].rearrange("p (h k) -> p h k", h=4)
                nc.vector.tensor_tensor(p0, p0, r[:, s, 0:4, None].to_broadcast([P, 4, P]), ALU.mult)
                nc.vector.tensor_tensor(p1, p1, r[:, s, 4:8, None].to_broadcast([P, 4, SEQ]), ALU.mult).then_inc(ps_ready, 1)

            def att_evac(a):
                dve.wait_ge(pt_done, a + 1)
                if a:
                    dve.wait_ge(pv_done, a)
                nc.vector.tensor_copy(pT[:, 4 * SEQ:4 * SEQ + 4 * P], ps[:, 7, :]).then_inc(pTb_ready, 1)

            def att_out(a):
                if a in OUT_OF:
                    e = OUT_OF[a]
                    dve.wait_ge(ohi_ready, e + 1)
                    if e < 4:
                        hi, lo = h_hi[:, 2 * e:2 * e + 2, :], h_lo[:, 2 * e:2 * e + 2, :]
                    else:
                        c = 2 * (e % 2)
                        hi, lo = ((oA_hi, oA_lo) if e < 6 else (oB_hi, oB_lo))
                        hi, lo = hi[:, c:c + 2, :], lo[:, c:c + 2, :]
                    nc.vector.tensor_tensor(lo.rearrange("p c t -> p (c t)"), ps[:, e % 2, :],
                                            hi.rearrange("p c t -> p (c t)").bitcast(F32), ALU.subtract).then_inc(olo_ready, 1)

            def attention(a0, a1):
                att_max(a0)
                for a in range(a0, a1):
                    att_scale(a)
                    if a + 1 < a1:
                        att_max(a + 1)
                    att_evac(a)
                    att_out(a)

            def head_sums(n, src, h, w, signal, sqd, cnt, parts=P):
                pass

            def mixer0():
                u0 = U_M0
                link(nc.vector.tensor_scalar(row("l0_nsa_q_norm"), row("l0_nsa_q_norm"), 0.125, None, ALU.mult))
                r64 = tab[:, T_R64:T_R64 + 256].rearrange("p (t c) -> p t c", t=NT)
                for i, (name, scale) in enumerate((("l0_nsa_q_norm", 1.0), ("l0_nsa_ks_norm", 1.0), ("l0_nsa_kw_norm", 1.0),
                                                   ("l0_swa_q_norm", 0.125), ("l0_swa_k_norm", 1.0))):
                    g = row(name)
                    for a, b in ((0, 0), (HD, 32), (HD + 32, 0)):
                        w = HD if a == 0 else 32
                        nc.vector.scalar_tensor_tensor(out=rope_q[i][:, :, a:a + w], in0=g[:, None, b:b + w].to_broadcast([P, NT, w]), scalar=scale,
                                                       in1=r64[:, :, a:a + w], op0=ALU.mult, op1=ALU.mult)
                link(nc.vector.tensor_scalar(nsink[:, :], row("l0_swa_sinks"), -1.0, None, ALU.mult))

                def build_flat():
                    dve.wait_ge(unit_done, u0 + 1)
                    for m, name in enumerate(("l0_cmp_pos_k", "l0_cmp_pos_v")):
                        c0 = COLS[name][0]
                        for g in range(2):
                            tok = ps[g * HD:(g + 1) * HD, 4, m * SEQ:(m + 1) * SEQ].rearrange("p (b j) -> p j b", j=CS)
                            for jj in range(2):
                                for b0 in range(2):
                                    src = tok[:, jj:CS:2, b0:b0 + NCMP]
                                    pos = cols[jj * HD:(jj + 1) * HD, c0 + 8 * b0:c0 + 8 * b0 + 8]
                                    ins = nc.vector.tensor_tensor(flat[jj * HD:(jj + 1) * HD, m, 8 * b0:8 * b0 + 8, g * NCMP:(g + 1) * NCMP],
                                                                  src, pos[:, :, None].to_broadcast([HD, 8, NCMP]), ALU.add)
                    ins.then_inc(flat_built, 1)

                def chain(n):
                    u = M0_CHAINS[n]
                    h = 4 if u in (1, 2, 6, 7) else 2
                    dve.wait_ge(hsq_done, n + 1)
                    w = h * HD
                    nc.vector.tensor_reduce(ssq[:, n % 4, 0:NT * h].rearrange("p (t h) -> p t h", t=NT), heads4(t2[:, :, :], h, HD), AX.X, ALU.add)\
                        .then_inc(hss_done, 1)
                    dve.wait_ge(hrs_ready, n + 1)
                    rs = srs[:, n % 4, 0:NT * h].rearrange("p (t h) -> p t h", t=NT)[:, :, :, None].to_broadcast([P, NT, h, HD])
                    z = heads4(nat[u % 2][:, :, :], h, HD)
                    nc.vector.tensor_tensor(z, z, rs, ALU.mult).then_inc(hn_ready, 1)
                    dve.wait_ge(hn_ready, n + 1)
                    if n >= 2:
                        dve.wait_ge(hT_done, {2: 2, 3: 4, 4: 5, 5: 6, 6: 7}[n])
                    table = rope_q[{1: 0, 2: 0, 3: 1, 4: 2, 6: 3, 7: 3, 8: 4}[u]]
                    dst = heads4(t1[n % 2][:, :, :], h, HD)
                    link(nc.vector.tensor_tensor(dst, z, table[:, :, None, 0:HD].to_broadcast([P, NT, h, HD]), ALU.mult))
                    if n < 2:
                        if n == 1:
                            dve.wait_ge(hT_done, 2)
                        link(nc.vector.tensor_tensor(heads4(qg[:, :, :], h, HD), z,
                                                     row("l0_nsa_q_norm")[:, None, None, :].to_broadcast([P, NT, h, HD]), ALU.mult))
                    dve.wait_ge(rot2_ready, n + 1)
                    if h == 2:
                        dve.wait_ge(hT_done, {2: 4, 3: 5, 6: 6}[n])
                        for t in range(NT):
                            a, b = (v[:, t, 0:P].rearrange("p (g d) -> p g d", g=2)[:, :, None, :].to_broadcast([P, 2, 2, HD]) for v in (t1[n % 2], t2))
                            ins = nc.vector.tensor_tensor(qg[:, t, :].rearrange("p (g two d) -> p g two d", g=2, two=2), a, b, ALU.add)
                        ins.then_inc(rot_ready, 1)
                        return
                    nc.vector.tensor_tensor(t1[n % 2][:, :, 0:w], t1[n % 2][:, :, 0:w], t2[:, :, 0:w], ALU.add).then_inc(rot_ready, 1)

                split_list(u0, M0_SIZES, 4)
                build_flat()
                dve.wait_ge(flathi_ready, 1)
                nc.vector.tensor_tensor(flat_lo, flat[:, :, :, :], flat_hi.bitcast(F32), ALU.subtract).then_inc(flatlo_ready, 1)
                for u in range(1, NPROJ):
                    split_list(u0, M0_SIZES, u + 4)
                    if u == 5:
                        dve.wait_ge(unit_done, u0 + 6)
                        gb = row("l0_nsa_gate_b")[:, None, :].to_broadcast([P, NT, 24])
                        nc.vector.tensor_tensor(glog[:, :].rearrange("p (t c) -> p t c", t=NT),
                                                ps[:, 0, :].rearrange("p (t n) -> p t n", t=NT)[:, :, 0:24], gb, ALU.add).then_inc(glog_ready, 1)
                        dve.wait_ge(gexp_ready, 1)
                        link(nc.vector.tensor_scalar(gden1[:, :], gden1[:, :], 1.0, None, ALU.add))
                        link(nc.vector.reciprocal(gate[:, :], gden1[:, :]))
                    else:
                        chain(M0_CHAINS.index(u))
                for n in (13, 14):
                    split_list(u0, M0_SIZES, n)
                for n in (15, 16, 17, 18):
                    split_list(u0, M0_SIZES, n)
                dve.wait_ge(ksq_done, 1)
                nc.vector.tensor_reduce(ssq[0:NCMP, 3, 0:2], kc2[:, :].rearrange("p (g d) -> p g d", g=2), AX.X, ALU.add).then_inc(kss_done, 1)
                dve.wait_ge(krs_ready, 1)
                kn = kcv[:, 0:P].rearrange("p (g d) -> p g d", g=2)
                link(nc.vector.tensor_tensor(kn, kn, srs[0:NCMP, 3, 0:2, None].to_broadcast([NCMP, 2, HD]), ALU.mult))
                c = ROWS["l0_nsa_kc_norm"][0]
                nc.vector.tensor_tensor(kcd[:, :].rearrange("p (g two d) -> p g two d", g=2, two=2), kn[:, :, None, :].to_broadcast([NCMP, 2, 2, HD]),
                                        rows[0:NCMP, None, None, c:c + HD].to_broadcast([NCMP, 2, 2, HD]), ALU.mult).then_inc(kcn_ready, 1)
                dve.wait_ge(lc_done, 1)
                v3 = lc[:, :, :, 0:NCMP]
                flat3 = v3.rearrange("p t h c -> p (t h) c")

                def blk(c0, heads):
                    return tab[:, c0:c0 + 30].rearrange("p (t c) -> p t c", t=NT)[:, :, None, :].to_broadcast([P, NT, heads, NCMP])

                for par in range(2):
                    sc = ps[:, 6 + par, 0:128].rearrange("p (t h c) -> p t h c", t=NT, h=4)[:, :, :, 0:NCMP]
                    link(nc.vector.tensor_tensor(v3[:, :, par:8:2, :], sc, blk(T_CNEG, 4), ALU.add))
                link(nc.vector.tensor_reduce(lc_n[:, :], flat3, AX.X, ALU.max, negate=True))
                nc.vector.tensor_tensor(flat3, flat3, lc_n[:, :, None].to_broadcast([P, 16, NCMP]), ALU.add).then_inc(lc_shift, 1)
                dve.wait_ge(lc_exp, 1)
                link(nc.vector.tensor_tensor(v3, v3, blk(T_C01, 8), ALU.mult))
                link(nc.vector.tensor_reduce(lc_d[:, :], flat3, AX.X, ALU.add))
                link(nc.vector.tensor_scalar(lc_d[:, :], lc_d[:, :], 1e-30, None, ALU.max))
                link(nc.vector.reciprocal(lc_r[:, :], lc_d[:, :]))
                g0 = gate[:, :].rearrange("p (t h b) -> p (t h) b", t=NT, b=3)[:, :, 0]
                link(nc.vector.tensor_tensor(lc_r[:, :], lc_r[:, :], g0, ALU.mult))
                nc.vector.tensor_tensor(flat3, flat3, lc_r[:, :, None].to_broadcast([P, 16, NCMP]), ALU.mult).then_inc(pc_ready, 1)
                attention(A_M0, A_M1)
                for n in (19, 20):
                    split_list(u0, M0_SIZES, n)
                add_to_x(NORM_M0, 4, 1.0, u0 + M0_UNITS - 1)

            def mixer1():
                u0 = U_M1
                c0 = len(M0_CHAINS)
                c = ROWS["l1_mla_q_norm"][0]
                nc.vector.tensor_scalar(fgain[:, 0:HD], row("l1_fox_q_norm"), 0.125, None, ALU.mult)
                link(nc.vector.tensor_scalar(fgain[:, HD:160], row("l1_mla_q_norm"), 96.0 ** -0.5, None, ALU.mult))

                def chain(n):
                    u = n
                    dve.wait_ge(hsq_done, c0 + n + 1)
                    if u in (0, 4):
                        w = 256 if u == 0 else 128
                        z = nat1[0][:, :, 0:w] if u == 0 else natkv[:, :, 0:w]
                        nc.vector.tensor_reduce(ssq[:, n % 4, 0:NT], sq1[:, :, 0:w], AX.X, ALU.add).then_inc(hss_done, 1)
                        dve.wait_ge(hrs_ready, c0 + n + 1)
                        nc.vector.tensor_tensor(z, z, srs[:, n % 4, 0:NT, None].to_broadcast([P, NT, w]), ALU.mult).then_inc(rot_ready, 1)
                        return
                    z = heads4(nat1[u % 4][:, :, :], 4, HD)
                    nc.vector.tensor_reduce(ssq[:, n % 4, :].rearrange("p (t h) -> p t h", t=NT), heads4(sq1[:, :, 0:256], 4, HD), AX.X, ALU.add)\
                        .then_inc(hss_done, 1)
                    dve.wait_ge(hrs_ready, c0 + n + 1)
                    rs = srs[:, n % 4, :].rearrange("p (t h) -> p t h", t=NT)[:, :, :, None].to_broadcast([P, NT, 4, HD])
                    link(nc.vector.tensor_tensor(z, z, rs, ALU.mult))
                    g = fgain[:, 0:HD] if u in (1, 2) else row("l1_fox_k_norm")
                    nc.vector.tensor_tensor(z, z, g[:, None, None, :].to_broadcast([P, NT, 4, HD]), ALU.mult).then_inc(rot_ready, 1)

                def c_lo(n):
                    dve.wait_ge(chi_ready, n + 1)
                    if n == 0:
                        cc = COLS["l1_mla_q_a_norm"][0]
                        for k in range(2):
                            ins = nc.vector.scalar_tensor_tensor(out=cq_lo[:, k, :], in0=ps[:, 5, k * SEQ:(k + 1) * SEQ], scalar=cols[:, cc + k:cc + k + 1],
                                                                 in1=cq_hi[:, k, :].bitcast(F32), op0=ALU.mult, op1=ALU.subtract)
                    else:
                        cc = COLS["l1_mla_kv_a_norm"][0]
                        ins = nc.vector.scalar_tensor_tensor(out=ckv_lo, in0=ps[:, 6, 0:SEQ], scalar=cols[:, cc:cc + 1],
                                                             in1=ckv_hi.bitcast(F32), op0=ALU.mult, op1=ALU.subtract)
                    ins.then_inc(clo_ready, 1)

                for u in range(NPROJ):
                    split_list(u0, M1_SIZES, u + 4)
                    if u < 6:
                        chain(u)
                    if u == 2:
                        c_lo(0)
                    if u == 6:
                        c_lo(1)
                dve.wait_ge(unit_done, u0 + 9)
                fb = row("l1_fox_f_bias")[:, None, :].to_broadcast([P, NT, 8])
                link(nc.vector.tensor_tensor(fz[:, :].rearrange("p (t h) -> p t h", t=NT),
                                             ps[:, 0, :].rearrange("p (t n) -> p t n", t=NT)[:, :, 0:8], fb, ALU.add))
                nc.vector.scalar_tensor_tensor(out=fa[:, :], in0=fz[:, :], scalar=-1.0, in1=fz[:, :], op0=ALU.mult, op1=ALU.max).then_inc(f_abs, 1)
                dve.wait_ge(f_ln, 1)
                nc.vector.scalar_tensor_tensor(out=lf[:, :, :].rearrange("p t h -> p (t h)"), in0=fz[:, :], scalar=0.0, in1=fl[:, :],
                                               op0=ALU.min, op1=ALU.subtract).then_inc(lf_ready, 1)
                split_list(u0, M1_SIZES, 13)
                dve.wait_ge(dt_done, 1)
                nc.vector.tensor_scalar(negDT[:, :], ps[0:8, 4, 0:SEQ], -1.0, None, ALU.mult)
                nc.vector.tensor_copy(dnat[:, :, :].rearrange("p t h -> p (t h)"), ps[:, 4, SEQ:SEQ + 16]).then_inc(dt_ready, 1)
                for n in range(4):
                    dve.wait_ge(msq_done, n + 1)
                    z = heads4(natm[:, :, :], 4, 96)
                    nc.vector.tensor_reduce(ssq[:, n % 4, :].rearrange("p (t h) -> p t h", t=NT), heads4(sq1[:, :, :], 4, 96), AX.X, ALU.add)\
                        .then_inc(mss_done, 1)
                    dve.wait_ge(mrs_ready, n + 1)
                    rs = srs[:, n % 4, :].rearrange("p (t h) -> p t h", t=NT)[:, :, :, None].to_broadcast([P, NT, 4, 96])
                    link(nc.vector.tensor_tensor(z, z, rs, ALU.mult))
                    g = fgain[:, HD:160] if n < 2 else row("l1_mla_k_norm")
                    nc.vector.tensor_tensor(z, z, g[:, None, None, :].to_broadcast([P, NT, 4, 96]), ALU.mult).then_inc(mg_ready, 1)
                    dve.wait_ge(mg_ready, n + 1)
                    tail = z[:, :, :, HD:96]
                    cs = tab[:, T_R32:T_R32 + 128].rearrange("p (t c) -> p t c", t=NT)[:, :, None, 0:32].to_broadcast([P, NT, 4, 32])
                    link(nc.vector.tensor_tensor(heads4(r1[:, :, :], 4, 32), tail, cs, ALU.mult))
                    dve.wait_ge(mr2_ready, n + 1)
                    nc.vector.tensor_tensor(tail, heads4(r1[:, :, :], 4, 32), heads4(r2[:, :, :], 4, 32), ALU.add).then_inc(mrot_ready, 1)
                for n in (14, 15, 16):
                    split_list(u0, M1_SIZES, n)
                attention(A_M1, A_END)
                for n in (17, 18):
                    split_list(u0, M1_SIZES, n)
                add_to_x(NORM_M1, 4, 1.0, u0 + M1_UNITS - 1)

            nc.vector.memset(zero_b[:, :], 0.0)
            nc.vector.memset(mask1[:, 0:P], 0.0).then_inc(const_ready, 1)
            norm(0)
            for n in range(LEAD):
                split(n, n)
            ffn(0, False)
            norm(1)
            mixer0()
            norm(2)
            ffn(1, False)
            norm(3)
            ffn(2, False)
            norm(4)
            mixer1()
            norm(5)
            ffn(3, True)

        @block.tensor
        def _(pe):
            def passes(dst, lhs, rhs, start, stop):
                nc.tensor.matmul(dst, lhs[0], rhs[0], start=start, stop=False)
                nc.tensor.matmul(dst, lhs[0], rhs[1], start=False, stop=False)
                return nc.tensor.matmul(dst, lhs[1], rhs[0], start=False, stop=stop)

            def wslot(us, size, inner):
                return tuple(w[us % SPLIT][:, 0:size].rearrange("p (a b) -> p a b", b=inner) for w in (w_hi, w_lo))

            def norm(m, zero):
                def tr(q, t):
                    for c in range(2):
                        ins = nc.tensor.transpose(ps[:, 6 + q % 2, c * SEQ + t * P:c * SEQ + (t + 1) * P],
                                                  xn[:, t, (2 * q + c) * P:(2 * q + c + 1) * P], ident)
                    return ins

                pe.wait_ge(xn_ready, NT * m + 1)
                tr(0, 0)
                tr(1, 0)
                pe.wait_ge(xn_ready, NT * m + 2)
                tr(0, 1).then_inc(xT_ready, 1)
                tr(1, 1).then_inc(xT_ready, 1)
                for q in (2, 3):
                    pe.wait_ge(hlo_ready, DC * m + 2 * (q - 1))
                    tr(q, 0)
                    tr(q, 1).then_inc(xT_ready, 1)
                if zero:
                    for b in range(4):
                        nc.tensor.matmul(ps[:, b, :], zero_b[:, :], zero_b[:, 0:1].to_broadcast([P, 512]), start=True, stop=False)

            def down(us, lhs, last, bank, start=False):
                w = wslot(us, UNIT, D)
                for t in range(NT):
                    for half in range(2):
                        for c in range(2):
                            ins = passes(ps[:, bank + 2 * t + half, :], tuple(v[:, c, t * P:(t + 1) * P] for v in lhs),
                                         tuple(v[:, c, half * 512:(half + 1) * 512] for v in w),
                                         start and c == 0, last and c == 1)
                    if last and t == 0:
                        ins.then_inc(acc_ready, 1)
                return ins

            def ffn(f):
                u0 = U_FFN[f]
                m = NORM_FFN[f]

                def gate_up(j, js):
                    bank = 4 + 2 * (js % 2)
                    u = u0 + (3 * js - 1 if js else 0)
                    loop = not isinstance(j, int)
                    if js >= 1 and (loop or j >= 2):
                        pass
                    if loop:
                        pe.wait_ge(mul_done, 2 * j + (11 * f + js - 1) if 11 * f + js - 1 > 0 else 2 * j + 1)
                    for n in range(2):
                        us = u + n
                        pe.wait_ge(lo_ready, (6 * j if loop else 0) + us + 1)
                        w = wslot(us, UNIT, STEP)
                        for b in range(2):
                            for k in range(DC):
                                if js == 0 and n == 0 and b == 0:
                                    pe.wait_ge(hlo_ready, DC * m + k + 1)
                                ins = passes(ps[:, bank + b, n * SEQ:(n + 1) * SEQ], tuple(v[:, k, b * P:(b + 1) * P] for v in w),
                                             (h_hi[:, k, :], h_lo[:, k, :]), k == 0, k == DC - 1)
                        ins.then_inc(unit_done, 1)

                def down_step(j, js):
                    us = u0 + down_index(js)
                    loop = not isinstance(j, int)
                    pe.wait_ge(lo_ready, (6 * j if loop else 0) + us + 1)
                    pe.wait_ge(alo_ready, (2 * j if loop else 0) + (11 * f + js + 1))
                    lhs = (a_hi[:, js % 2, :, :], a_lo[:, js % 2, :, :])
                    down(us, lhs, js == NSTEP - 1 and not loop, 0).then_inc(unit_done, 1)

                gate_up(0, 0)
                with pe.Fori(0, (NSTEP - 1) // 2) as i:
                    for half in range(2):
                        gate_up(i, 1 + half)
                        down_step(i, half)
                down_step(NSTEP - 1, NSTEP - 1)

            def att_qk(a):
                kind, g = ATT[a]
                if a:
                    pe.wait_ge(exp_done, a)
                mk = mask1w if kind == SWA else mask1
                nc.tensor.matmul(ps[:, 2, :], id_b[:, :], mask0[:, None, :].to_broadcast([P, 4, P]), start=True, stop=False)
                for b in range(2):
                    nc.tensor.matmul(ps[:, 3 + b, :], id_b[:, :], mk[:, None, :].to_broadcast([P, 2, SEQ]), start=True, stop=False)

                def head(qt, i, end):
                    h = 4 * g + i
                    keys = P * (qt + 1)
                    dst = ps[:, 2, i * P:(i + 1) * P] if qt == 0 else ps[:, 3 + i % 2, (i // 2) * SEQ:(i // 2 + 1) * SEQ]
                    r = slice((h % 2) * HD, (h % 2 + 1) * HD)
                    if kind == MLA:
                        q, k = qmT[:, h, qt * P:(qt + 1) * P], kmT[:, h, 0:keys]
                    elif kind == FOX:
                        q, k = qfT[r, h // 2, qt * P:(qt + 1) * P], kfT[r, h // 2, 0:keys]
                    else:
                        q = (qbT if kind == SWA else qrT)[r, h // 2, qt * P:(qt + 1) * P]
                        k = kT[{SLC: 0, WIN: 1, SWA: 2}[kind]][r, g, 0:keys]
                    if kind == FOX:
                        nc.tensor.matmul(dst, ident[0:8, h:h + 1].to_broadcast([8, P]), negDT[:, 0:keys], start=False, stop=False)
                    return nc.tensor.matmul(dst, q, k, start=False, stop=end)

                head(0, 0, False)
                head(0, 2, False).then_inc(even_done, 1)
                head(1, 0, False)
                head(1, 2, True)
                head(1, 1, False)
                head(1, 3, True)
                pe.wait_ge(even_done, a + 1)
                head(0, 1, False)
                ins = head(0, 3, True)
                ins.then_inc(qk_done, 1)

            def att_pT(a):
                pe.wait_ge(ps_ready, a + 1)
                if a:
                    pe.wait_ge(pTa_ready, a)
                    pe.wait_ge(pTb_ready, a)
                pr = prob[a % 2]
                for h in range(4):
                    nc.tensor.transpose(ps[:, 5, h * P:(h + 1) * P], pr[:, h * P:(h + 1) * P], ident)
                for kc in range(2):
                    for h in range(4):
                        at_ = 4 * P + h * SEQ + kc * P
                        ins = nc.tensor.transpose(ps[:, 6 + kc, h * P:(h + 1) * P], pr[:, at_:at_ + P], ident)
                ins.then_inc(pt_done, 1)

            def att_pv(a):
                kind, g = ATT[a]
                pe.wait_ge(pTa_ready, a + 1)
                pe.wait_ge(pTb_ready, a + 1)
                if a in (4, 5):
                    pe.wait_ge(olo_ready, a - 3)
                if a in (8, 9):
                    pe.wait_ge(olo_ready, a - 3)
                k0 = pT[:, 0:4 * SEQ].rearrange("p (h q) -> p h q", h=4)
                k1 = pT[:, 4 * SEQ:4 * SEQ + 4 * P].rearrange("p (h q) -> p h q", h=4)
                bank = ps[:, g, :].rearrange("p (c t) -> p c t", c=2)
                if kind in (SLC, WIN, SWA):
                    v = vN[{SLC: 0, WIN: 1, SWA: 2}[kind]]
                    for par in range(2):
                        r = slice(par * HD, (par + 1) * HD)
                        nc.tensor.matmul(bank[r, :, :], v[:, 0, g * HD:(g + 1) * HD], k0[:, par:4:2, :], start=kind == SWA, stop=False)
                        ins = nc.tensor.matmul(bank[r, :, P:SEQ], v[:, 1, g * HD:(g + 1) * HD], k1[:, par:4:2, :], start=False, stop=kind != SLC)
                else:
                    for i in range(4):
                        h = 4 * g + i
                        r = slice((h % 2) * HD, (h % 2 + 1) * HD)
                        if kind == FOX:
                            v0, v1 = vf[:, 0, h * HD:(h + 1) * HD], vf[:, 1, h * HD:(h + 1) * HD]
                        else:
                            v0, v1 = vm[:, 0, h, :], vm[:, 1, h, :]
                        nc.tensor.matmul(bank[r, i // 2, :], v0, k0[:, i, :], start=True, stop=False)
                        ins = nc.tensor.matmul(bank[r, i // 2, P:SEQ], v1, k1[:, i, :], start=False, stop=True)
                ins.then_inc(pv_done, 1)

            def attention(a0, a1):
                att_qk(a0)
                for a in range(a0, a1):
                    if a + 1 < a1:
                        att_qk(a + 1)
                    att_pT(a)
                    att_pv(a)

            def project(u0, n, width, bank):
                us = u0 + n
                pe.wait_ge(lo_ready, us + 1)
                w = wslot(us, DC * width, width)
                for t in range(NT):
                    for k in range(DC):
                        ins = passes(ps[:, bank, t * 256:t * 256 + width], tuple(v[:, k, t * P:(t + 1) * P] for v in (h_hi, h_lo)),
                                     tuple(v[:, k, :] for v in w), k == 0, k == DC - 1)
                ins.then_inc(unit_done, 1)

            def out_proj(u0, first, e0, parts):
                for e in range(4):
                    us = u0 + first + e
                    pe.wait_ge(lo_ready, us + 1)
                    pe.wait_ge(olo_ready, e0 + e + 1)
                    down(us, parts(e), e == 3, 4, start=e == 0).then_inc(unit_done, 1)

            def mixer0():
                u0 = U_M0

                def tjob(j):
                    u, what = M0_TJOBS[j]
                    n = M0_CHAINS.index(u)
                    pe.wait_ge(rot_ready, n + 1)
                    if j >= 3:
                        pe.wait_ge(hT_ready, j - 2)
                    src = t1[n % 2] if what == "rot" and u in (1, 2, 6, 7) else qg
                    for c in range(2):
                        for t in range(NT):
                            ins = nc.tensor.transpose(ps[:, 5 + j % 3, c * SEQ + t * P:c * SEQ + (t + 1) * P],
                                                      src[:, t, c * P:(c + 1) * P], ident)
                    ins.then_inc(hT_done, 1)

                pe.wait_ge(lo_ready, u0 + 1)
                w = wslot(u0, UNIT, 256)
                for m in range(2):
                    for k in range(DC):
                        pe.wait_ge(hlo_ready, DC * NORM_M0 + k + 1)
                        ins = passes(ps[:, 4, m * SEQ:(m + 1) * SEQ], tuple(v[:, k, m * P:(m + 1) * P] for v in w),
                                     (h_hi[:, k, :], h_lo[:, k, :]), k == 0, k == DC - 1)
                ins.then_inc(unit_done, 1)
                before = {3: (0, 1), 4: (2, 3), 6: (4, 5), 8: (6,)}
                for u in range(1, NPROJ):
                    if u >= 5:
                        pe.wait_ge(nat_ready, {5: 1, 6: 2, 7: 3, 8: 4}[u])
                    project(u0, u, M0_COLS[u][1], (u - 1) % 4)
                    for j in before.get(u, ()):
                        tjob(j)
                pe.wait_ge(glog_ready, 1)
                pe.wait_ge(nat_ready, 7)
                pe.wait_ge(flatlo_ready, 1)
                for m in range(2):
                    for n in range(2):
                        us = u0 + NPROJ + 2 * m + n
                        pe.wait_ge(lo_ready, us + 1)
                        w = wslot(us, UNIT, CMPH)
                        for c in range(8):
                            for half in range(2):
                                ins = passes(ps[:, 2 * m + half, 0:30], tuple(v[:, c, half * P:(half + 1) * P] for v in w),
                                             (flat_hi[:, m, 8 * n + c, :], flat_lo[:, m, 8 * n + c, :]), n == 0 and c == 0, n == 1 and c == 7)
                        ins.then_inc(unit_done, 1)
                    if m == 0:
                        tjob(7)
                tjob(8)
                for m in range(2):
                    pe.wait_ge(hid_ready, m + 1)
                    for g in range(2):
                        for half in range(2):
                            ins = nc.tensor.matmul(ps[0:NCMP, 4, m * P + g * HD:m * P + (g + 1) * HD], hid[:, m, half, g * NCMP:(g + 1) * NCMP],
                                                   w2[:, m, half, :], start=half == 0, stop=half == 1)
                ins.then_inc(kcv_done, 1)
                pe.wait_ge(kcn_ready, 1)
                pe.wait_ge(hT_ready, 9)
                for g in range(2):
                    ins = nc.tensor.transpose(ps[:, 5, g * 16:g * 16 + NCMP], kcd[:, g * P:(g + 1) * P],
                                              ident[0:NCMP, 0:NCMP])
                ins.then_inc(kcT_done, 1)
                pe.wait_ge(kcT_ready, 1)
                for t in range(NT):
                    for h in range(8):
                        r = slice((h % 2) * HD, (h % 2 + 1) * HD)
                        c = (t * 4 + h // 2) * 16
                        ins = nc.tensor.matmul(ps[:, 6 + h % 2, c:c + NCMP], qaT[r, h // 2, t * P:(t + 1) * P],
                                               kcT[r, h // 4, 0:NCMP], start=True, stop=True)
                ins.then_inc(lc_done, 1)
                pe.wait_ge(pc_ready, 1)
                for h in range(8):
                    for t in range(NT):
                        ins = nc.tensor.transpose(ps[0:NCMP, 4 + h // 2, (h % 2) * SEQ + t * P:(h % 2) * SEQ + (t + 1) * P],
                                                  lc[:, t, h, 0:NCMP], ident)
                ins.then_inc(pcT_done, 1)
                pe.wait_ge(pcT_ready, 1)
                for g in range(2):
                    for par in range(2):
                        nc.tensor.matmul(ps[par * HD:(par + 1) * HD, g, :].rearrange("p (c t) -> p c t", c=2), kcv[:, P + g * HD:P + (g + 1) * HD],
                                         pcT[:, 4 * g + par:4 * g + 4:2, :], start=True, stop=False)
                attention(A_M0, A_M1)
                out_proj(u0, NPROJ + 4, 0, lambda e: (h_hi[:, 2 * e:2 * e + 2, :], h_lo[:, 2 * e:2 * e + 2, :]))

            def mixer1():
                u0 = U_M1
                c0 = len(M0_CHAINS)
                o0 = len(M0_TJOBS)

                def tjob(j):
                    u = M1_CHAINS[j]
                    pe.wait_ge(rot_ready, c0 + u + 1)
                    if j == 1:
                        pe.wait_ge(clo_ready, 1)
                    if j == 2:
                        pe.wait_ge(hlo_ready, DC * (NORM_M1 + 1))
                    for c in range(2):
                        for t in range(NT):
                            ins = nc.tensor.transpose(ps[:, 4 + j, c * SEQ + t * P:c * SEQ + (t + 1) * P], nat1[u % 4][:, t, c * P:(c + 1) * P], ident)
                    ins.then_inc(hT_done, 1)

                def c_T(n):
                    pe.wait_ge(rot_ready, c0 + (1 if n == 0 else 5))
                    if n == 1:
                        pe.wait_ge(hT_ready, o0 + 3)
                    for c in range(2 - n):
                        for t in range(NT):
                            src = nat1[0][:, t, c * P:(c + 1) * P] if n == 0 else natkv[:, t, 0:P]
                            ins = nc.tensor.transpose(ps[:, 5 + n, c * SEQ + t * P:c * SEQ + (t + 1) * P], src, ident)
                    ins.then_inc(cT_done, 1)

                for u in range(NPROJ):
                    if u >= 4:
                        pe.wait_ge(nat_ready, 7 + u - 3)
                    if u == 0:
                        pe.wait_ge(hlo_ready, DC * NORM_M1 + DC)
                    project(u0, u, M1_COLS[u][1], u % 4)
                    if u == 1:
                        c_T(0)
                    if u == 3:
                        tjob(0)
                    if u == 4:
                        tjob(1)
                    if u == 5:
                        tjob(2)
                    if u == 6:
                        c_T(1)
                    if u == 7:
                        tjob(3)
                pe.wait_ge(clo_ready, 2)
                pe.wait_ge(nat_ready, 7 + 8)
                pe.wait_ge(lo_ready, u0 + 10)
                pe.wait_ge(f_abs, 1)
                w = wslot(u0 + 9, 1536, 768)
                for half in range(2):
                    for t in range(NT):
                        for c in range(2):
                            ins = passes(ps[:, 2 * half + t, 0:384], tuple(v[:, c, t * P:(t + 1) * P] for v in (cq_hi, cq_lo)),
                                         tuple(v[:, c, half * 384:(half + 1) * 384] for v in w), c == 0, c == 1)
                ins.then_inc(unit_done, 1)
                pe.wait_ge(lf_ready, 1)
                pe.wait_ge(hT_ready, o0 + 4)
                tri, ones = tab[:, T_TRI:T_TRI + P], tab[:, T_TRI + P:T_TRI + 2 * P]
                nc.tensor.matmul(ps[0:8, 4, 0:SEQ], lf[:, 0, :], tab[:, T_TRI:T_TRI + SEQ], start=True, stop=False)
                nc.tensor.matmul(ps[0:8, 4, P:SEQ], lf[:, 1, :], tri, start=False, stop=True)
                nc.tensor.matmul(ps[:, 4, SEQ:SEQ + 8], tri, lf[:, 0, :], start=True, stop=True)
                nc.tensor.matmul(ps[:, 4, SEQ + 8:SEQ + 16], ones, lf[:, 0, :], start=True, stop=False)
                nc.tensor.matmul(ps[:, 4, SEQ + 8:SEQ + 16], tri, lf[:, 1, :], start=False, stop=True).then_inc(dt_done, 1)

                def m_T(n):
                    pe.wait_ge(mrot_ready, n + 1)
                    if n == 0:
                        pe.wait_ge(dt_ready, 1)
                    if n >= 2:
                        pe.wait_ge(mT_ready, n - 1)
                    b = 4 + 2 * (n % 2)
                    for h in range(4):
                        for t in range(NT):
                            ins = nc.tensor.transpose(ps[0:96, b + h // 2, (h % 2) * SEQ + t * P:(h % 2) * SEQ + (t + 1) * P],
                                                      natm[:, t, h * 96:(h + 1) * 96], ident)
                    ins.then_inc(mT_done, 1)

                m_T(0)
                m_T(1)
                pe.wait_ge(lo_ready, u0 + 11)
                w = wslot(u0 + 10, 1024, 1024)
                for half in range(2):
                    for t in range(NT):
                        ins = passes(ps[:, 2 * half + t, :], (ckv_hi[:, t * P:(t + 1) * P], ckv_lo[:, t * P:(t + 1) * P]),
                                     tuple(v[:, 0, half * 512:(half + 1) * 512] for v in w), True, True)
                ins.then_inc(unit_done, 1)
                m_T(2)
                m_T(3)
                pe.wait_ge(mT_ready, 4)
                attention(A_M1, A_END)
                out_proj(u0, NPROJ + 2, 4, lambda e: tuple(v[:, 2 * (e % 2):2 * (e % 2) + 2, :] for v in ((oA_hi, oA_lo) if e < 2 else (oB_hi, oB_lo))))

            pe.wait_ge(tab_loaded, 16)
            pe.wait_ge(par_loaded, 16 * (len(COLS) + len(ROWS) + 2))
            pe.wait_ge(const_ready, 1)
            pe.wait_ge(cast_ready, 1)
            nc.tensor.transpose(ps[:, 5, 0:COLS_W], pstage[:, :], ident[0:COLS_W, 0:COLS_W]).then_inc(parT_ready, 1)
            norm(0, True)
            ffn(0)
            norm(1, False)
            mixer0()
            norm(2, True)
            ffn(1)
            norm(3, True)
            ffn(2)
            norm(4, False)
            mixer1()
            norm(5, True)
            ffn(3)


def shape_tables():
    i = np.arange(P)
    t = np.zeros((P, T_COLS), np.float32)
    t[:, T_ID:T_ID + P] = np.eye(P)
    t[:, T_TRI:T_TRI + P] = i[None, :] >= i[:, None]
    t[:, T_TRI + P:T_TRI + 2 * P] = 1.0
    t[:, T_CAUSAL:T_CAUSAL + P] = np.where(i[None, :] <= i[:, None], 0.0, -BIG)
    t[:, T_BAND:T_BAND + P] = np.where(i[None, :] > i[:, None], 0.0, -BIG)
    for tile in range(NT):
        pos = (tile * P + i).astype(np.float32)[:, None]
        for at_, dim in ((T_R64 + tile * P, 64), (T_R32 + tile * 64, 32)):
            inv = (1.0 / (np.float32(10000.0) ** (np.arange(0, dim, 2, dtype=np.float32) / np.float32(dim)))).astype(np.float32)
            ang = (pos * inv[None, :]).astype(np.float32)
            c, s = np.cos(ang), np.sin(ang)
            t[:, at_:at_ + 2 * dim] = np.concatenate([c, c, -s, s], 1)
        seen = (np.arange(NCMP) * CS + CB - 1)[None, :] <= pos
        t[:, T_CNEG + tile * NCMP:T_CNEG + (tile + 1) * NCMP] = np.where(seen, 0.0, -BIG)
        t[:, T_C01 + tile * NCMP:T_C01 + (tile + 1) * NCMP] = seen
    return t


def kernel(**inputs):
    import concourse.bacc as bacc
    from concourse.bass_utils import run_bass_kernel_spmd

    nc = bacc.Bacc("TRN2", target_bir_lowering=False, num_devices=1)
    arrays = {name: np.ascontiguousarray(a) for name, a in inputs.items()}
    arrays["shape_tables"] = shape_tables()
    A = {}
    for name, a in arrays.items():
        A[name] = nc.dram_tensor(name, a.shape, mybir.dt.from_np(a.dtype), kind="ExternalInput").ap()
    out = nc.dram_tensor("out", (1, SEQ, D), F32, kind="ExternalOutput").ap()
    trunk(nc, A, A["shape_tables"], out)
    r = run_bass_kernel_spmd(nc, [arrays], core_ids=[0])
    return r.results[0]["out"]
```

```python
from contextlib import ExitStack

import numpy as np
import concourse.bass as bass
from concourse import mybir

F32 = mybir.dt.float32
F32R = mybir.dt.float32r
BF16 = mybir.dt.bfloat16
ALU = mybir.AluOpType
ACT = mybir.ActivationFunctionType
AX = mybir.AxisListType

P = 128
SEQ = 256
NT = SEQ // P
D = 1024
DC = D // P
FF = 2816
STEP = 256
NSTEP = FF // STEP
HD = 64
EPS = 1e-6
BIG = 1e30
NCMP = 15
CMPH = 256
CB, CS = 32, 16
UNIT = 2048
RAW, SPLIT = 3, 6
LEAD = 4

FFN_UNITS = 3 * NSTEP
M0_COLS = [(512, 256), (0, 256), (256, 256), (1280, 24), (768, 256), (1024, 256), (1304, 256), (1560, 256), (1816, 256)]
M0_PROJ = [0, 1, 2, 7, 8, 9, 10, 11, 12]
M1_COLS = [(1544, 256), (1800, 160), (0, 256), (256, 256), (512, 256), (768, 256), (1536, 8), (1024, 256), (1280, 256)]
M1_PROJ = [0, 1, 2, 4, 6, 7, 8, 9, 10]
NPROJ = 9
M0_UNITS = NPROJ + 4 + 4
M1_UNITS = NPROJ + 2 + 4
M0_SIZES = {u: DC * w for u, (_, w) in zip(M0_PROJ, M0_COLS)} | {u: UNIT for u in (3, 4, 5, 6, *range(NPROJ + 4, M0_UNITS))}
M1_SIZES = {u: DC * w for u, (_, w) in zip(M1_PROJ, M1_COLS)} | {3: 2 * 768, 5: 1024} | {u: UNIT for u in range(NPROJ + 2, M1_UNITS)}
U_FFN = [0, FFN_UNITS + M0_UNITS, 2 * FFN_UNITS + M0_UNITS, 3 * FFN_UNITS + M0_UNITS + M1_UNITS]
U_M0 = FFN_UNITS
U_M1 = 3 * FFN_UNITS + M0_UNITS
U_END = 4 * FFN_UNITS + M0_UNITS + M1_UNITS
NORM_FFN = [0, 2, 3, 5]
NORM_M0, NORM_M1 = 1, 4

T_ID, T_TRI, T_CAUSAL, T_BAND = 0, 128, 384, 512
T_R64, T_R32, T_CNEG, T_C01, T_COLS = 640, 896, 1024, 1054, 1084
ROWS = {}
_at = 0
for _n, _w in (("l0_nsa_q_norm", 64), ("l0_nsa_kc_norm", 64), ("l0_nsa_ks_norm", 64), ("l0_nsa_kw_norm", 64),
               ("l0_swa_q_norm", 64), ("l0_swa_k_norm", 64), ("l0_swa_sinks", 8), ("l0_nsa_gate_b", 24),
               ("l1_fox_f_bias", 8), ("l1_fox_q_norm", 64), ("l1_fox_k_norm", 64),
               ("l1_mla_q_norm", 96), ("l1_mla_k_norm", 96)):
    ROWS[_n] = (_at, _w)
    _at += _w
ROWS_W = _at
COLS = {}
_at = 0
for _n, _w in (("l0_ffn1_norm", 8), ("l0_mix_norm", 8), ("l0_ffn2_norm", 8), ("l1_ffn1_norm", 8), ("l1_mix_norm", 8),
               ("l1_ffn2_norm", 8), ("l0_cmp_pos_k", 16), ("l0_cmp_pos_v", 16), ("l1_mla_q_a_norm", 2),
               ("l1_mla_kv_a_norm", 1)):
    COLS[_n] = (_at, _w)
    _at += _w
COLS_W = _at

A_M0, A_M1, A_END = 0, 6, 10
SLC, WIN, SWA, FOX, MLA = range(5)
ATT = [(SLC, 0), (SLC, 1), (WIN, 0), (WIN, 1), (SWA, 0), (SWA, 1), (MLA, 0), (MLA, 1), (FOX, 0), (FOX, 1)]
FOX_T_BANK = (6, 7, 0, 3)
JOBS = 3
QK_RING, T_RING, PT_RING = 4, 2, 5
OUT_OF = {2: 0, 3: 1, 4: 2, 5: 3, 6: 4, 7: 5, 8: 6, 9: 7}
M0_CHAINS = [(1, 0, 4, 0, None), (2, 1, 4, 0, None), (8, 1, 2, 1, 0), (9, 2, 2, 2, 1), (10, 3, 4, 3, None), (11, 0, 4, 3, None), (12, 1, 2, 4, 2)]
M0_TJOBS = [(0, "rot"), (0, "gain"), (1, "rot"), (1, "gain"), (2, "rot"), (3, "rot"), (4, "rot"), (5, "rot"), (6, "rot")]
M1_CHAINS = [("cq", 0, 0), ("ckv", 0, 1), ("q", 0, 2), ("mq", 0, 3), ("mq", 1, 3), ("q", 1, 4), ("mk", 0, 5), ("k", 0, 6), ("mk", 1, 5), ("k", 1, 7)]


def trunk(nc, A, out):
    ctx = ExitStack()
    with ctx:
        def sem(name):
            return ctx.enter_context(nc.semaphore(name))

        top = nc.sbuf_usable_end
        base = (nc.sbuf_base + 63) // 32 * 32
        slab = ctx.enter_context(nc.sbuf_tensor("slab", [P, (top - base) // 4 - 16], F32))
        place = [base]

        def at(name, shape, dt=F32, offset=None):
            size = int(np.prod(shape[1:])) * (2 if dt == BF16 else 4)
            here = place[0] if offset is None else offset
            if offset is None:
                place[0] = here + (size + 31) // 32 * 32
                assert place[0] <= top, (name, place[0] - top)
            return nc.alloc_sbuf_tensor_at(name, shape, dt, offset=here)

        raw = [at(f"raw{i}", [P, UNIT]) for i in range(RAW)]
        w_hi = [at(f"w_hi{i}", [P, UNIT], F32R) for i in range(SPLIT)]
        w_lo = [at(f"w_lo{i}", [P, UNIT], F32R) for i in range(SPLIT)]
        x = at("x_res", [P, NT, D])
        h_at = place[0]
        h_hi = at("h_hi", [P, DC, SEQ], F32R)
        h_lo = at("h_lo", [P, DC, SEQ], F32R)
        a_at = place[0]
        a_hi = at("a_hi", [P, 2, 2, SEQ], F32R)
        a_lo = at("a_lo", [P, 2, 2, SEQ], F32R)
        tab = at("tab", [P, T_COLS])
        rows = at("rows", [P, ROWS_W])
        par = at("par", [P, COLS_W + 4 * HD])
        id_b = at("id_b", [P, P], BF16)
        zero_b = at("zero_b", [P, P], BF16)
        mask0 = at("mask0", [P, P], BF16)
        mask1 = at("mask1", [P, 2 * P], BF16)
        mask1w = at("mask1w", [P, 2 * P], BF16)
        ms = at("ms", [P, 6, NT])
        ms_eps = at("ms_eps", [P, 6, NT])
        rstd = at("rstd", [P, 6, NT])
        mhalf = at("mhalf", [P, 16])
        arena = place[0]
        ident = tab[:, T_ID:T_ID + P]
        cols = par[:, 0:COLS_W]
        w2 = par[:, COLS_W:COLS_W + 4 * HD].rearrange("p (m c n) -> p m c n", m=2, c=2)

        sg = at("sg", [P, 2 * SEQ])
        act_v = at("act_v", [P, 2 * SEQ])
        xn = at("xn", [P, NT, D])

        place[0] = arena
        p_at = arena
        prob = [at(f"prob{i}", [P, 512]) for i in range(QK_RING)]
        pT = [at(f"pT{i}", [P, 512]) for i in range(PT_RING)]
        nmax = at("nmax", [P, QK_RING, 4])
        nmax2 = at("nmax2", [P, QK_RING, 4])
        den = at("den", [P, QK_RING, 4])
        den2 = at("den2", [P, QK_RING, 4])
        rden = at("rden", [P, QK_RING, 4])
        gden = at("gden", [P, QK_RING, 4])
        esink = at("esink", [P, QK_RING, 4])
        zsink = at("zsink", [P, QK_RING, 4])
        ssq = at("ssq", [P, 4, 8])
        ssq2 = at("ssq2", [P, 4, 8])
        srs = at("srs", [P, 4, 8])
        m_at = place[0]
        place[0] = p_at
        nat = [at(f"nat{i}", [P, NT, 256]) for i in range(2)]
        t1 = [at(f"t1_{i}", [P, NT, 256]) for i in range(2)]
        t2 = at("t2", [P, NT, 256])
        qg = at("qg", [P, NT, 256])
        flat_at = place[0]
        flat = at("flat", [P, 2, CS, 30])
        glog = at("glog", [P, NT * 24])
        gden1 = at("gden1", [P, NT * 24])
        kcv = at("kcv", [NCMP, 256])
        lc_n = at("lc_n", [P, 16])
        lc_d = at("lc_d", [P, 16])
        lc_r = at("lc_r", [P, 16])
        assert place[0] <= m_at
        place[0] = flat_at
        hid = at("hid", [P, 2, 2, 30])
        kc2 = at("kc2", [NCMP, P])
        kcd = at("kcd", [NCMP, 256])
        kcT = at("kcT", [P, 2, 16])
        lc = at("lc", [P, NT, 8, 16])
        assert place[0] <= flat_at + 2 * CS * 30 * 4
        place[0] = p_at
        nat1 = [at(f"nat1_{i}", [P, NT, 256]) for i in range(4)]
        sq1 = at("sq1", [P, NT, 4 * 96])
        natm = [at(f"natm{i}", [P, NT, 4 * 96]) for i in range(2)]
        r2 = at("r2", [P, NT, 4 * 32])
        assert place[0] <= m_at

        place[0] = m_at
        qaT = at("qaT", [P, 4, SEQ])
        qrT = at("qrT", [P, 4, SEQ])
        qbT = at("qbT", [P, 4, SEQ])
        kT = [at(f"kT{i}", [P, 2, SEQ]) for i in range(3)]
        vN = [at(f"vN{i}", [P, NT, 2 * HD]) for i in range(3)]
        rope_q = [at(f"rope_g{i}", [P, NT, P]) for i in range(5)]
        nsink = at("nsink", [P, 8])
        gate = at("gate", [P, NT * 24])
        pcT = at("pcT", [NCMP, 8, SEQ], offset=h_at)
        place[0] = m_at
        qmT = at("qmT", [96, 8, SEQ])
        kmT = at("kmT", [96, 8, SEQ])
        vf = at("vf", [P, NT, 512])
        negDT = at("negDT", [8, SEQ])
        dnat = at("dnat", [P, NT, 8])
        fz = at("fz", [P, 16])
        fa = at("fa", [P, 16])
        fe = at("fe", [P, 16])
        fl = at("fl", [P, 16])
        lf = at("lf", [P, NT, 8])
        vm = at("vm", [P, NT, 8, HD])
        kr = at("kr", [P, NT, 32])
        fgain = at("fgain", [P, HD])
        qfT = at("qfT", [P, 4, SEQ], offset=h_at)
        kfT = at("kfT", [P, 4, SEQ], offset=h_at + 4 * SEQ * 4)
        oB_hi = at("oB_hi", [P, 4, SEQ], F32R, offset=h_at + 8 * SEQ * 4)
        oB_lo = at("oB_lo", [P, 4, SEQ], F32R, offset=h_at + 12 * SEQ * 4)
        oA_hi = at("oA_hi", [P, 4, SEQ], F32R, offset=a_at)
        oA_lo = at("oA_lo", [P, 4, SEQ], F32R, offset=a_at + 4 * SEQ * 4)
        mtab = [at(f"mtab{i}", [P, NT, P], offset=a_at + (4 * i + 3) * SEQ * 4) for i in range(2)]
        a_hi_flat = a_hi[:, :, :, :].rearrange("p a b c -> p (a b c)")
        a_lo_flat = a_lo[:, :, :, :].rearrange("p a b c -> p (a b c)")
        flat_hi, flat_lo = (v[:, 0:960].rearrange("p (m c b) -> p m c b", m=2, b=30) for v in (a_hi_flat, a_lo_flat))
        cq_hi, cq_lo = (v[:, 0:512].rearrange("p (c t) -> p c t", c=2) for v in (a_hi_flat, a_lo_flat))
        ckv_hi, ckv_lo = (v[:, 512:768] for v in (a_hi_flat, a_lo_flat))

        ps = ctx.enter_context(nc.psum_tensor("ps", [P, 8, 512], F32))

        x_loaded = [sem(f"x_loaded{t}") for t in range(NT)]
        ident_loaded = sem("ident_loaded")
        par_loaded = sem("par_loaded")
        rows_loaded = sem("rows_loaded")
        raw_loaded = [sem(f"raw_loaded{i}") for i in range(RAW)]
        hi_ready = sem("hi_ready")
        lo_ready = sem("lo_ready")
        unit_done = sem("unit_done")
        x_updated = sem("x_updated")
        sq_done = sem("sq_done")
        rstd_ready = sem("rstd_ready")
        xn_ready = sem("xn_ready")
        xT_ready = sem("xT_ready")
        hhi_ready = sem("hhi_ready")
        hlo_ready = sem("hlo_ready")
        silu_done = sem("silu_done")
        mul_done = sem("mul_done")
        ahi_ready = sem("ahi_ready")
        alo_ready = sem("alo_ready")
        acc_ready = sem("acc_ready")
        out_stored = sem("out_stored")
        const_ready = sem("const_ready")
        cast_ready = sem("cast_ready")
        pool_const = sem("pool_const")
        v_step = sem("v_step")
        g_step = sem("g_step")
        a_step = sem("a_step")
        nat_ready = sem("nat_ready")
        hsq_done = sem("hsq_done")
        hss_done = sem("hss_done")
        hrs_ready = sem("hrs_ready")
        hn_ready = sem("hn_ready")
        rot2_ready = sem("rot2_ready")
        rot_ready = sem("rot_ready")
        hT_done = sem("hT_done")
        hT_ready = sem("hT_ready")
        flat_built = sem("flat_built")
        flathi_ready = sem("flathi_ready")
        flatlo_ready = sem("flatlo_ready")
        hid_ready = sem("hid_ready")
        kcv_done = sem("kcv_done")
        kcv_ready = sem("kcv_ready")
        ksq_done = sem("ksq_done")
        kss_done = sem("kss_done")
        krs_ready = sem("krs_ready")
        kcn_ready = sem("kcn_ready")
        kcT_done = sem("kcT_done")
        kcT_ready = sem("kcT_ready")
        lc_done = sem("lc_done")
        lc_shift = sem("lc_shift")
        lc_exp = sem("lc_exp")
        pc_ready = sem("pc_ready")
        pcT_done = sem("pcT_done")
        pcT_ready = sem("pcT_ready")
        glog_ready = sem("glog_ready")
        gexp_ready = sem("gexp_ready")
        even_done = sem("even_done")
        qk_done = sem("qk_done")
        nmax_ready = sem("nmax_ready")
        zsink_ready = sem("zsink_ready")
        esink_ready = sem("esink_ready")
        exp_done = sem("exp_done")
        ps_ready = sem("ps_ready")
        pt_done = sem("pt_done")
        pT_ready = sem("pT_ready")
        pv_done = sem("pv_done")
        ohi_ready = sem("ohi_ready")
        olo_ready = sem("olo_ready")
        cT_done = sem("cT_done")
        chi_ready = sem("chi_ready")
        clo_ready = sem("clo_ready")
        f_abs = sem("f_abs")
        f_ln = sem("f_ln")
        lf_ready = sem("lf_ready")
        dt_done = sem("dt_done")
        dt_ready = sem("dt_ready")
        natm_ready = sem("natm_ready")
        krep_ready = sem("krep_ready")
        msq_done = sem("msq_done")
        mss_done = sem("mss_done")
        mrs_ready = sem("mrs_ready")
        mg_ready = sem("mg_ready")
        mr2_ready = sem("mr2_ready")
        mrot_ready = sem("mrot_ready")
        mT_done = sem("mT_done")
        mT_ready = sem("mT_ready")

        block = ctx.enter_context(nc.Block())

        def row(name):
            c, w = ROWS[name]
            return rows[:, c:c + w]

        def gain_col(norm, c):
            return cols[:, norm * 8 + c:norm * 8 + c + 1]

        def job_heads(j):
            b = j % JOBS
            return j // JOBS, int(b > 0), slice(0, 4) if b == 0 else slice(b - 1, 4, 2)

        def of_heads(sl, g):
            return slice(4 * g + sl.start, 4 * g + 4, sl.step or 1)

        def ends_output(j):
            return OUT_OF.get(j // JOBS) if j % JOBS == JOBS - 1 else None

        def o_parts(e):
            if e < 4:
                return h_hi[:, 2 * e:2 * e + 2, :], h_lo[:, 2 * e:2 * e + 2, :]
            hi, lo = (oA_hi, oA_lo) if e < 6 else (oB_hi, oB_lo)
            c = 2 * (e % 2)
            return hi[:, c:c + 2, :], lo[:, c:c + 2, :]

        ffn_names = [("l0_ffn1_", 0), ("l0_ffn2_", 1), ("l1_ffn1_", 2), ("l1_ffn2_", 3)]
        gates = [A[n + "w_gate"].rearrange("(k p) n -> p k n", p=P) for n, _ in ffn_names]
        ups = [A[n + "w_up"].rearrange("(k p) n -> p k n", p=P) for n, _ in ffn_names]
        downs = [A[n + "w_down"].rearrange("(c p) n -> p c n", p=P) for n, _ in ffn_names]

        def down_index(j):
            return 3 * j + 4 if j < NSTEP - 1 else 3 * NSTEP - 1

        def heads4(ap, h, w):
            return ap.rearrange("p t (h d) -> p t h d", d=w)[:, :, 0:h, :]

        @block.sync
        def _(sp):
            xv = A["x"][0, :, :].rearrange("(t p) d -> p t d", p=P)
            for t in range(NT):
                sp.dma_start(x[:, t, :], xv[:, t, :]).then_inc(x_loaded[t], 16)

            def load(u, dst, src):
                if not isinstance(u, int) or u >= RAW:
                    sp.wait_ge(lo_ready, u - (RAW - 1))
                return sp.dma_start(dst, src)

            def slot(u_static, size, inner):
                return raw[u_static % RAW][:, 0:size].rearrange("p (a b) -> p a b", b=inner)

            def ffn(f):
                u0 = U_FFN[f]

                def gate_up(u, us, c0):
                    for n, w in enumerate((gates[f], ups[f])):
                        load(u + n, slot(us + n, UNIT, STEP), w[:, :, bass.ds(c0, STEP)]).then_inc(raw_loaded[(us + n) % RAW], 16)

                gate_up(u0, u0, 0)
                with sp.Fori(0, (NSTEP - 1) // 2) as i:
                    for half in range(2):
                        us = u0 + 2 + 3 * half
                        gate_up(6 * i + us, us, (2 * i + 1 + half) * STEP)
                        load(6 * i + (us + 2), slot(us + 2, UNIT, D), downs[f][:, bass.ds((2 * i + half) * 2, 2), :])\
                            .then_inc(raw_loaded[(us + 2) % RAW], 16)
                u = u0 + FFN_UNITS - 1
                load(u, slot(u, UNIT, D), downs[f][:, 2 * NSTEP - 2:2 * NSTEP, :]).then_inc(raw_loaded[u % RAW], 16)

            def mixer(u0, w_in, spans, others, w_out, order):
                w = w_in.rearrange("(k p) n -> p k n", p=P)
                parts = [(w[:, :, c:c + n], n) for c, n in spans]
                for n, other in others:
                    parts.insert(n, other)
                wo = w_out.rearrange("(c p) n -> p c n", p=P)
                parts += [(wo[:, 2 * e:2 * e + 2, :], D) for e in order]
                for n, (src, inner) in enumerate(parts):
                    u = u0 + n
                    load(u, slot(u, src.shape[1] * inner, inner), src).then_inc(raw_loaded[u % RAW], 16)

            ffn(0)
            w1k, w1v = (A[n].rearrange("(c p) n -> p c n", p=P) for n in ("l0_cmpk_w1", "l0_cmpv_w1"))
            mixer(U_M0, A["l0_w_in"], M0_COLS,
                  [(3 + 2 * m + n, (w1[:, 8 * n:8 * n + 8, :], CMPH)) for m, w1 in enumerate((w1k, w1v)) for n in range(2)],
                  A["l0_w_out"], range(4))
            ffn(1)
            ffn(2)
            mixer(U_M1, A["l1_w_in"], M1_COLS,
                  [(3, (A["l1_mla_w_q_b"].rearrange("(c p) n -> p c n", p=P), 768)),
                   (5, (A["l1_mla_w_kv_b"].rearrange("(c p) n -> p c n", p=P), 1024))], A["l1_w_out"], (2, 3, 0, 1))
            ffn(3)
            ov = out[0, :, :].rearrange("(t p) d -> p t d", p=P)
            for t in range(NT):
                sp.wait_ge(x_updated, 10 + t + 1)
                sp.dma_start(ov[:, t, :], x[:, t, :]).then_inc(out_stored, 16)
            sp.wait_ge(out_stored, 16 * NT)

        @block.gpsimd
        def _(pool):
            steps = [0]

            def link(ins):
                steps[0] += 1
                ins.then_inc(g_step, 1)
                pool.wait_ge(g_step, steps[0])

            def norm(m):
                for t in range(NT):
                    pool.wait_ge(sq_done, NT * m + t + 1)
                    link(nc.gpsimd.tensor_scalar(ms_eps[:, m, t:t + 1], ms[:, m, t:t + 1], 1.0, EPS, ALU.mult, ALU.add))
                    nc.gpsimd.tensor_tensor(rstd[:, m, t:t + 1], ms_eps[:, m, t:t + 1], mhalf[:, 0:1], ALU.pow)\
                        .then_inc(rstd_ready, 1)

            def inverse_rms(dst, tmp, src, width, n, signal, parts=P):
                link(nc.gpsimd.tensor_scalar(tmp[0:parts, 0:n], src[0:parts, 0:n], 1.0 / width, EPS, ALU.mult, ALU.add))
                nc.gpsimd.tensor_tensor(dst[0:parts, 0:n], tmp[0:parts, 0:n], mhalf[0:parts, 0:n], ALU.pow).then_inc(signal, 1)

            def mixer0():
                for n, (u, bank, h, rope, value) in enumerate(M0_CHAINS):
                    if n == 2:
                        compressed_keys()
                    w = h * HD
                    src = nat[n % 2][:, :, 0:w]
                    pool.wait_ge(nat_ready, n + 1)
                    if n:
                        pool.wait_ge(rot_ready, n)
                    nc.gpsimd.tensor_tensor(t2[:, :, 0:w], src, src, ALU.mult).then_inc(hsq_done, 1)
                    pool.wait_ge(hss_done, n + 1)
                    inverse_rms(srs[:, n % 4, :], ssq2[:, n % 4, :], ssq[:, n % 4, :], HD, NT * h, hrs_ready)
                    pool.wait_ge(hn_ready, n + 1)
                    for half in range(2):
                        a, b = (32 * half, 32 - 32 * half)
                        z = heads4(nat[n % 2][:, :, :], h, HD)[:, :, :, b:b + 32]
                        sine = rope_q[rope][:, :, None, HD + a:HD + a + 32].to_broadcast([P, NT, h, 32])
                        ins = nc.gpsimd.tensor_tensor(heads4(t2[:, :, :], h, HD)[:, :, :, a:a + 32], z, sine, ALU.mult)
                    ins.then_inc(rot2_ready, 1)

            def compressed_keys():
                pool.wait_ge(kcv_ready, 1)
                nc.gpsimd.tensor_tensor(kc2[:, :], kcv[:, 0:P], kcv[:, 0:P], ALU.mult).then_inc(ksq_done, 1)
                pool.wait_ge(kss_done, 1)
                inverse_rms(srs[:, 3, :], ssq2[:, 3, :], ssq[:, 3, :], HD, 2, krs_ready, parts=NCMP)

            def mixer1():
                c0 = len(M0_CHAINS)
                m = 0
                for n, (what, part, _) in enumerate(M1_CHAINS):
                    width, cnt = {"cq": (256, 2), "ckv": (P, 2), "q": (HD, 8), "k": (HD, 8), "mq": (96, 8), "mk": (96, 8)}[what]
                    pool.wait_ge(hss_done, c0 + n + 1)
                    inverse_rms(srs[:, n % 4, :], ssq2[:, n % 4, :], ssq[:, n % 4, :], width, cnt, hrs_ready)
                    if what in ("mq", "mk"):
                        m += 1
                        pool.wait_ge(hn_ready, c0 + m)
                        if m > 1:
                            pool.wait_ge(mrot_ready, m - 1)
                        z4 = heads4(natm[part][:, :, :], 4, 96)
                        for half in range(2):
                            a, b = (16 * half, 16 - 16 * half)
                            sine = mtab[int(what == "mk")][:, :, None, 96 + a:112 + a].to_broadcast([P, NT, 4, 16])
                            ins = nc.gpsimd.tensor_tensor(heads4(r2[:, :, :], 4, 32)[:, :, :, a:a + 16], z4[:, :, :, 64 + b:80 + b], sine, ALU.mult)
                        ins.then_inc(rot2_ready, 1)

            nc.gpsimd.memset(mhalf[:, :], -0.5).then_inc(pool_const, 1)
            pool.wait_ge(pool_const, 1)
            norm(0)
            norm(1)
            mixer0()
            norm(2)
            norm(3)
            norm(4)
            mixer1()
            norm(5)

        @block.scalar
        def _(act):
            def split(u, us, size=UNIT, i=0):
                s = us % RAW
                act.wait_ge(raw_loaded[s], 32 * i + (16 * ((u - s) // RAW) + 16))
                if u >= SPLIT:
                    act.wait_ge(unit_done, 6 * i + (u - (SPLIT - 1)))
                nc.scalar.activation(w_hi[us % SPLIT][:, 0:size], raw[s][:, 0:size], ACT.Copy).then_inc(hi_ready, 1)

            def split_list(u0, sizes, n):
                if n < len(sizes):
                    split(u0 + n, u0 + n, sizes[n])
                elif u0 + n < U_END:
                    split(u0 + n, u0 + n)

            steps = [0]

            def link(ins):
                steps[0] += 1
                ins.then_inc(a_step, 1)
                act.wait_ge(a_step, steps[0])

            def norm(m):
                for t in range(NT):
                    if m == 0:
                        act.wait_ge(x_loaded[t], 16)
                    else:
                        act.wait_ge(x_updated, NT * (m - 1) + t + 1)
                    nc.scalar.activation(xn[:, t, :], x[:, t, :], ACT.Square, scale=D ** -0.5,
                                         accum_out=ms[:, m, t:t + 1]).then_inc(sq_done, 1)
                if m == 0:
                    act.wait_ge(par_loaded, 16)
                for c in range(DC):
                    if c % 2 == 0:
                        act.wait_ge(xT_ready, 4 * m + c // 2 + 1)
                    src = ps[:, 6 + c // 2 % 2, (c % 2) * SEQ:(c % 2 + 1) * SEQ]
                    nc.scalar.activation(h_hi[:, c, :], src, ACT.Copy, scale=gain_col(m, c)).then_inc(hhi_ready, 1)

            def ffn(f, last):
                u0 = U_FFN[f]

                def step(j, js):
                    def next_split(n):
                        us = u0 + 3 * js + 4 + n
                        if not isinstance(j, int):
                            split(us, us, i=j)
                        elif us < U_END:
                            split(us, us)

                    next_split(0)
                    next_split(1)
                    bank = 4 + 2 * (js % 2)
                    up = u0 + (3 * js + 1 if js else 2)
                    done = 11 * f + js + 1
                    if not isinstance(j, int):
                        up, done = 6 * j + up, 2 * j + done
                    act.wait_ge(unit_done, up)
                    nc.scalar.activation(sg[:, :].rearrange("p (b n) -> p b n", b=2), ps[:, bank:bank + 2, 0:SEQ],
                                         ACT.Silu).then_inc(silu_done, 1)
                    next_split(2)
                    act.wait_ge(mul_done, done)
                    nc.scalar.activation(a_hi[:, js % 2, :, :].rearrange("p b n -> p (b n)"), act_v[:, :],
                                         ACT.Copy).then_inc(ahi_ready, 1)

                step(0, 0)
                n_loop = (NSTEP - 1) // 2 - (1 if last else 0)
                with act.Fori(0, n_loop) as i:
                    for half in range(2):
                        step(i, 1 + half)
                if last:
                    step(NSTEP - 2, NSTEP - 2)
                    step(NSTEP - 1, NSTEP - 1)

            def att_exp(j):
                a, qt, hs = job_heads(j)
                kind, g = ATT[a]
                s = j % QK_RING
                act.wait_ge(nmax_ready, j + 1)
                if j >= QK_RING:
                    act.wait_ge(pt_done, j - QK_RING + 1)
                n, keys = (4, P) if qt == 0 else (2, SEQ)
                if kind == SWA:
                    nc.scalar.activation(esink[:, s, 0:n], zsink[:, s, 0:n], ACT.Exp).then_inc(esink_ready, 1)
                for i in range(n):
                    ins = nc.scalar.activation(prob[s][:, i * keys:(i + 1) * keys], ps[:, 2 + s, i * keys:(i + 1) * keys], ACT.Exp,
                                               bias=nmax[:, s, i:i + 1], accum_out=den[:, s, i:i + 1])
                ins.then_inc(exp_done, 1)

            def att_evac(j):
                act.wait_ge(pt_done, j + 1)
                if j >= PT_RING:
                    act.wait_ge(pv_done, j - PT_RING + 1)
                nc.scalar.activation(pT[j % PT_RING][:, :], ps[:, 6 + j % T_RING, :], ACT.Copy).then_inc(pT_ready, 1)

            def att_out(j):
                e = ends_output(j)
                if e is not None:
                    act.wait_ge(pv_done, j + 1)
                    nc.scalar.activation(o_parts(e)[0].rearrange("p c t -> p (c t)"), ps[:, e % 2, :], ACT.Copy).then_inc(ohi_ready, 1)

            def attention(a0, a1):
                j0, j1 = JOBS * a0, JOBS * a1
                for j in range(j0, j0 + 3):
                    att_exp(j)
                for j in range(j0, j1):
                    att_evac(j)
                    if j > j0:
                        att_out(j - 1)
                    if j + 3 < j1:
                        att_exp(j + 3)
                att_out(j1 - 1)

            def copy_T(job_bank, dst):
                nc.scalar.activation(dst, ps[:, job_bank, :], ACT.Copy).then_inc(hT_ready, 1)

            def mixer0():
                u0 = U_M0
                job_dst = [qrT[:, 0:2, :], qaT[:, 0:2, :], qrT[:, 2:4, :], qaT[:, 2:4, :], kT[0][:, :, :], kT[1][:, :, :],
                           qbT[:, 0:2, :], qbT[:, 2:4, :], kT[2][:, :, :]]

                def t_evac(j):
                    act.wait_ge(hT_done, j + 1)
                    copy_T(5 + j % 2, job_dst[j].rearrange("p c t -> p (c t)"))

                def rows_out(n):
                    u, bank, h, rope, value = M0_CHAINS[n]
                    act.wait_ge(unit_done, u0 + u + 1)
                    src = ps[:, bank, :].rearrange("p (t n) -> p t n", t=NT)
                    if n >= 2:
                        act.wait_ge(rot_ready, n - 1)
                    ins = nc.scalar.activation(nat[n % 2][:, :, 0:h * HD], src[:, :, 0:h * HD], ACT.Copy)
                    if value is not None:
                        ins = nc.scalar.activation(vN[value][:, :, :], src[:, :, P:2 * P], ACT.Copy)
                    ins.then_inc(nat_ready, 1)

                def w_split(n):
                    split_list(u0, M0_SIZES, n)

                w_split(4)
                act.wait_ge(flat_built, 1)
                nc.scalar.activation(flat_hi, flat[:, :, :, :], ACT.Copy).then_inc(flathi_ready, 1)
                w_split(5)
                rows_out(0)
                w_split(6)
                rows_out(1)
                t_evac(0)
                t_evac(1)
                w_split(7)
                w_split(8)
                t_evac(2)
                t_evac(3)
                w_split(9)
                w_split(10)
                act.wait_ge(unit_done, u0 + 7)
                act.wait_ge(flatlo_ready, 1)
                nc.scalar.activation(hid[:, :, :, :].rearrange("p m b n -> p b m n"),
                                     ps[:, 2:4, 0:64].rearrange("p b (m n) -> p b m n", m=2)[:, :, :, 0:30], ACT.Silu).then_inc(hid_ready, 1)
                w_split(11)
                act.wait_ge(glog_ready, 1)
                nc.scalar.activation(gden1[:, :], glog[:, :], ACT.Exp, scale=-1.0).then_inc(gexp_ready, 1)
                act.wait_ge(kcv_done, 1)
                nc.scalar.activation(kcv[:, :], ps[0:NCMP, 4, 0:256], ACT.Copy).then_inc(kcv_ready, 1)
                w_split(12)
                rows_out(2)
                act.wait_ge(kcT_done, 1)
                nc.scalar.activation(kcT[:, :, 0:NCMP], ps[:, 7, 0:32].rearrange("p (g c) -> p g c", g=2)[:, :, 0:NCMP],
                                     ACT.Copy).then_inc(kcT_ready, 1)
                w_split(13)
                rows_out(3)
                t_evac(4)
                w_split(14)
                rows_out(4)
                act.wait_ge(lc_shift, 1)
                nc.scalar.activation(lc[:, :, :, 0:NCMP].rearrange("p t h c -> p (t h) c"),
                                     lc[:, :, :, 0:NCMP].rearrange("p t h c -> p (t h) c"), ACT.Exp).then_inc(lc_exp, 1)
                t_evac(5)
                w_split(15)
                rows_out(5)
                t_evac(6)
                w_split(16)
                rows_out(6)
                t_evac(7)
                for b in range(4):
                    act.wait_ge(pcT_done, b + 1)
                    nc.scalar.activation(pcT[:, 2 * b:2 * b + 2, :].rearrange("p h t -> p (h t)"), ps[0:NCMP, (4, 7)[b % 2], :], ACT.Copy)\
                        .then_inc(pcT_ready, 1)
                t_evac(8)
                attention(A_M0, A_M1)
                for n in (17, 18, 19, 20):
                    w_split(n)

            def mixer1():
                u0 = U_M1
                o0 = len(M0_TJOBS)
                c0 = len(M0_CHAINS)

                def rows_out(n):
                    what, part, u = M1_CHAINS[n]
                    act.wait_ge(unit_done, u0 + u + 1)
                    if what in ("mq", "mk"):
                        z = natm[part]
                        if what == "mk":
                            act.wait_ge(mT_done, part + 1)
                            kv = ps[:, 4 + 2 * part:6 + 2 * part, :].rearrange("p t (h d) -> p t h d", d=P)
                            for t in range(NT):
                                nc.scalar.activation(heads4(z[:, :, :], 4, 96)[:, t, :, 0:HD], kv[:, t, :, 0:HD], ACT.Copy)
                                nc.scalar.activation(heads4(z[:, :, :], 4, 96)[:, t, :, HD:96], kr[:, t, None, :].to_broadcast([P, 4, 32]), ACT.Copy)
                                ins = nc.scalar.activation(vm[:, t, 4 * part:4 * part + 4, :], kv[:, t, :, HD:P], ACT.Copy)
                            link(ins)
                            src = z[:, :, :]
                        else:
                            src = ps[:, 4 + 2 * part:6 + 2 * part, 0:384]
                            nc.scalar.activation(z[:, :, :], src, ACT.Copy)
                        act.wait_ge(hss_done, c0 + n)
                        nc.scalar.activation(sq1[:, :, :], src, ACT.Square).then_inc(hsq_done, 1)
                        return
                    b = M1_PROJ.index(u) % 2
                    w = P if what == "ckv" else 256
                    src = ps[:, b, :].rearrange("p (t n) -> p t n", t=NT)
                    dst = nat1[{"cq": 3, "ckv": 2, "q": part, "k": 2 + part}[what]]
                    if what == "k":
                        act.wait_ge(cT_done, 2 - part)
                    nc.scalar.activation(dst[:, :, 0:w], src[:, :, 0:w], ACT.Copy)
                    if what == "ckv":
                        nc.scalar.activation(kr[:, :, :], src[:, :, P:160], ACT.Copy)
                    if n:
                        act.wait_ge(hss_done, c0 + n)
                    nc.scalar.activation(sq1[:, :, 0:w], src[:, :, 0:w], ACT.Square).then_inc(hsq_done, 1)

                def values_out(u):
                    act.wait_ge(unit_done, u0 + u + 1)
                    b = M1_PROJ.index(u) % 2
                    nc.scalar.activation(vf[:, :, (u - 9) * 256:(u - 8) * 256], ps[:, b, :].rearrange("p (t n) -> p t n", t=NT), ACT.Copy)\
                        .then_inc(nat_ready, 1)

                def c_hi(n):
                    act.wait_ge(cT_done, n + 1)
                    if n == 0:
                        c = COLS["l1_mla_q_a_norm"][0]
                        for k in range(2):
                            ins = nc.scalar.activation(cq_hi[:, k, :], ps[:, 2, k * SEQ:(k + 1) * SEQ], ACT.Copy, scale=cols[:, c + k:c + k + 1])
                    else:
                        c = COLS["l1_mla_kv_a_norm"][0]
                        ins = nc.scalar.activation(ckv_hi, ps[:, 3, 0:SEQ], ACT.Copy, scale=cols[:, c:c + 1])
                    ins.then_inc(chi_ready, 1)

                def m_evac(n):
                    act.wait_ge(mT_done, n + 1)
                    dst = (qmT if n < 2 else kmT)[:, 4 * (n % 2):4 * (n % 2) + 4, :]
                    nc.scalar.activation(dst.rearrange("p (b h) t -> p b (h t)", b=2), ps[0:96, 2:4, :], ACT.Copy).then_inc(mT_ready, 1)

                def w_split(n):
                    split_list(u0, M1_SIZES, n)

                w_split(4)
                rows_out(0)
                w_split(5)
                rows_out(1)
                c_hi(0)
                w_split(6)
                rows_out(2)
                c_hi(1)
                w_split(7)
                rows_out(3)
                rows_out(4)
                w_split(8)
                rows_out(5)
                w_split(9)
                rows_out(6)
                m_evac(0)
                w_split(10)
                rows_out(7)
                m_evac(1)
                rows_out(8)
                w_split(11)
                rows_out(9)
                m_evac(2)
                w_split(12)
                act.wait_ge(f_abs, 1)
                link(nc.scalar.activation(fe[:, :], fa[:, :], ACT.Exp, scale=-1.0))
                nc.scalar.activation(fl[:, :], fe[:, :], ACT.Ln, bias=1.0).then_inc(f_ln, 1)
                w_split(13)
                values_out(9)
                m_evac(3)
                w_split(14)
                values_out(10)
                for j in range(4):
                    act.wait_ge(hT_done, o0 + j + 1)
                    dst = (qfT[:, 0:2, :], qfT[:, 2:4, :], kfT[:, 0:2, :], kfT[:, 2:4, :])[j]
                    copy_T(FOX_T_BANK[j], dst.rearrange("p c t -> p (c t)"))
                attention(A_M1, A_END)
                for n in (15, 16, 17, 18):
                    w_split(n)

            act.dma_start(ident, A["shape_tables"][:, T_ID:T_ID + P]).then_inc(ident_loaded, 16)
            act.dma_start(par[:, :], A["columns"]).then_inc(par_loaded, 16)
            norm(0)
            act.dma_start(rows[:, :], A["rows"].partition_broadcast(P)).then_inc(rows_loaded, 16)
            act.dma_start(tab[:, P:T_COLS], A["shape_tables"][:, P:T_COLS]).then_inc(rows_loaded, 16)
            for n in range(LEAD):
                split(n, n)
            act.wait_ge(rows_loaded, 32)
            nc.scalar.activation(id_b[:, :], ident, ACT.Copy)
            nc.scalar.activation(mask0[:, :], tab[:, T_CAUSAL:T_CAUSAL + P], ACT.Copy)
            nc.scalar.activation(mask1[:, P:2 * P], tab[:, T_CAUSAL:T_CAUSAL + P], ACT.Copy)
            nc.scalar.activation(mask1w[:, P:2 * P], tab[:, T_CAUSAL:T_CAUSAL + P], ACT.Copy)
            nc.scalar.activation(mask1w[:, 0:P], tab[:, T_BAND:T_BAND + P], ACT.Copy).then_inc(cast_ready, 1)
            ffn(0, False)
            norm(1)
            mixer0()
            norm(2)
            ffn(1, False)
            norm(3)
            ffn(2, False)
            norm(4)
            mixer1()
            norm(5)
            ffn(3, True)

        @block.vector
        def _(dve):
            steps = [0]

            def link(ins):
                steps[0] += 1
                ins.then_inc(v_step, 1)
                dve.wait_ge(v_step, steps[0])

            def split(u, us, size=UNIT):
                dve.wait_ge(hi_ready, u + 1)
                nc.vector.tensor_tensor(w_lo[us % SPLIT][:, 0:size], raw[us % RAW][:, 0:size],
                                        w_hi[us % SPLIT][:, 0:size].bitcast(F32), ALU.subtract).then_inc(lo_ready, 1)

            def split_list(u0, sizes, n):
                if n < len(sizes):
                    split(u0 + n, u0 + n, sizes[n])
                elif u0 + n < U_END:
                    split(u0 + n, u0 + n)

            def norm(m):
                for t in range(NT):
                    dve.wait_ge(rstd_ready, NT * m + t + 1)
                    nc.vector.tensor_scalar(xn[:, t, :], x[:, t, :], rstd[:, m, t:t + 1], None, ALU.mult).then_inc(xn_ready, 1)
                for c in range(DC):
                    dve.wait_ge(hhi_ready, DC * m + 2 * (c // 2) + 2)
                    src = ps[:, 6 + c // 2 % 2, (c % 2) * SEQ:(c % 2 + 1) * SEQ]
                    nc.vector.scalar_tensor_tensor(out=h_lo[:, c, :], in0=src, scalar=gain_col(m, c), in1=h_hi[:, c, :].bitcast(F32),
                                                   op0=ALU.mult, op1=ALU.subtract).then_inc(hlo_ready, 1)

            def add_to_x(m, bank, scale, last_unit):
                for t in range(NT):
                    if t == 0:
                        dve.wait_ge(acc_ready, m + 1)
                    else:
                        dve.wait_ge(unit_done, last_unit + 1)
                    b = bank + 2 * t
                    nc.vector.scalar_tensor_tensor(out=x[:, t, :], in0=ps[:, b:b + 2, :].rearrange("p b n -> p (b n)"), scalar=scale,
                                                   in1=x[:, t, :], op0=ALU.mult, op1=ALU.add).then_inc(x_updated, 1)

            def ffn(f, last):
                u0 = U_FFN[f]

                def step(j, js):
                    loop = not isinstance(j, int)

                    def next_split(n):
                        us = u0 + 3 * js + 4 + n
                        if loop:
                            split(6 * j + us, us)
                        elif us < U_END:
                            split(us, us)

                    next_split(0)
                    next_split(1)
                    bank = 4 + 2 * (js % 2)
                    done = 11 * f + js + 1
                    if loop:
                        done = 2 * j + done
                    if loop or done > 1:
                        dve.wait_ge(alo_ready, done - 1)
                    dve.wait_ge(silu_done, done)
                    nc.vector.tensor_tensor(act_v[:, :].rearrange("p (b n) -> p b n", b=2), sg[:, :].rearrange("p (b n) -> p b n", b=2),
                                            ps[:, bank:bank + 2, SEQ:2 * SEQ], ALU.mult).then_inc(mul_done, 1)
                    next_split(2)
                    dve.wait_ge(ahi_ready, done)
                    nc.vector.tensor_tensor(a_lo[:, js % 2, :, :].rearrange("p b n -> p (b n)"), act_v[:, :],
                                            a_hi[:, js % 2, :, :].rearrange("p b n -> p (b n)").bitcast(F32),
                                            ALU.subtract).then_inc(alo_ready, 1)

                step(0, 0)
                with dve.Fori(0, (NSTEP - 1) // 2 - (1 if last else 0)) as i:
                    for half in range(2):
                        step(i, 1 + half)
                if last:
                    step(NSTEP - 2, NSTEP - 2)
                    step(NSTEP - 1, NSTEP - 1)
                add_to_x(NORM_FFN[f], 0, 0.5, u0 + FFN_UNITS - 1)

            def att_max(j):
                a, qt, hs = job_heads(j)
                kind, g = ATT[a]
                s = j % QK_RING
                n = 4 if qt == 0 else 2
                dve.wait_ge(qk_done, j + 1)
                if j >= QK_RING:
                    dve.wait_ge(exp_done, j - QK_RING + 1)
                first = nmax2 if kind in (SWA, FOX) else nmax
                ins = nc.vector.tensor_reduce(first[:, s, 0:n], ps[:, 2 + s, :].rearrange("p (h k) -> p h k", h=n), AX.X, ALU.max, negate=True)
                if kind in (SLC, WIN, MLA):
                    ins.then_inc(nmax_ready, 1)
                    return
                link(ins)
                if kind == SWA:
                    sinks = row("l0_swa_sinks")[:, of_heads(hs, g)]
                    link(nc.vector.tensor_tensor(nmax[:, s, 0:n], nmax2[:, s, 0:n], nsink[:, of_heads(hs, g)], ALU.min))
                    nc.vector.tensor_tensor(zsink[:, s, 0:n], nmax[:, s, 0:n], sinks, ALU.add).then_inc(nmax_ready, 1)
                else:
                    dn = dnat[:, qt, of_heads(hs, g)]
                    link(nc.vector.tensor_tensor(nmax2[:, s, 0:n], nmax2[:, s, 0:n], dn, ALU.subtract))
                    nc.vector.tensor_tensor(nmax[:, s, 0:n], nmax2[:, s, 0:n], dn, ALU.add).then_inc(nmax_ready, 1)

            def att_scale(j):
                a, qt, hs = job_heads(j)
                kind, g = ATT[a]
                s = j % QK_RING
                n = 4 if qt == 0 else 2
                dve.wait_ge(exp_done, j + 1)
                d = den
                if kind == SWA:
                    dve.wait_ge(esink_ready, j - 4 * JOBS + 1)
                    link(nc.vector.tensor_tensor(den2[:, s, 0:n], den[:, s, 0:n], esink[:, s, 0:n], ALU.add))
                    d = den2
                link(nc.vector.reciprocal(rden[:, s, 0:n], d[:, s, 0:n]))
                r = rden
                if kind in (SLC, WIN):
                    gv = gate[:, :].rearrange("p (t h b) -> p t h b", t=NT, b=3)[:, qt, of_heads(hs, g), 1 if kind == SLC else 2]
                    link(nc.vector.tensor_tensor(gden[:, s, 0:n], rden[:, s, 0:n], gv, ALU.mult))
                    r = gden
                pr = prob[s][:, :].rearrange("p (h k) -> p h k", h=n)
                nc.vector.tensor_tensor(pr, pr, r[:, s, 0:n, None].to_broadcast([P, n, 512 // n]), ALU.mult).then_inc(ps_ready, 1)

            def att_out(j):
                e = ends_output(j)
                if e is not None:
                    dve.wait_ge(ohi_ready, e + 1)
                    hi, lo = o_parts(e)
                    nc.vector.tensor_tensor(lo.rearrange("p c t -> p (c t)"), ps[:, e % 2, :],
                                            hi.rearrange("p c t -> p (c t)").bitcast(F32), ALU.subtract).then_inc(olo_ready, 1)

            def attention(a0, a1):
                j0, j1 = JOBS * a0, JOBS * a1
                for j in range(j0, j0 + 3):
                    att_max(j)
                for j in range(j0, j1):
                    att_scale(j)
                    if j + 3 < j1:
                        att_max(j + 3)
                    if j > j0:
                        att_out(j - 1)
                att_out(j1 - 1)

            def mixer0():
                u0 = U_M0
                dve.wait_ge(rows_loaded, 32)
                link(nc.vector.tensor_scalar(row("l0_nsa_q_norm"), row("l0_nsa_q_norm"), 0.125, None, ALU.mult))
                r64 = tab[:, T_R64:T_R64 + 256].rearrange("p (t c) -> p t c", t=NT)
                for i, (name, scale) in enumerate((("l0_nsa_q_norm", 1.0), ("l0_nsa_ks_norm", 1.0), ("l0_nsa_kw_norm", 1.0),
                                                   ("l0_swa_q_norm", 0.125), ("l0_swa_k_norm", 1.0))):
                    g = row(name)
                    for a, b in ((0, 0), (HD, 32), (HD + 32, 0)):
                        w = HD if a == 0 else 32
                        nc.vector.scalar_tensor_tensor(out=rope_q[i][:, :, a:a + w], in0=g[:, None, b:b + w].to_broadcast([P, NT, w]), scalar=scale,
                                                       in1=r64[:, :, a:a + w], op0=ALU.mult, op1=ALU.mult)
                link(nc.vector.tensor_scalar(nsink[:, :], row("l0_swa_sinks"), -1.0, None, ALU.mult))

                def build_flat():
                    dve.wait_ge(unit_done, u0 + 1)
                    for m, name in enumerate(("l0_cmp_pos_k", "l0_cmp_pos_v")):
                        c0 = COLS[name][0]
                        for g in range(2):
                            tok = ps[g * HD:(g + 1) * HD, 4, m * SEQ:(m + 1) * SEQ].rearrange("p (b j) -> p j b", j=CS)
                            for jj in range(2):
                                for b0 in range(2):
                                    src = tok[:, jj:CS:2, b0:b0 + NCMP]
                                    pos = cols[jj * HD:(jj + 1) * HD, c0 + 8 * b0:c0 + 8 * b0 + 8]
                                    ins = nc.vector.tensor_tensor(flat[jj * HD:(jj + 1) * HD, m, 8 * b0:8 * b0 + 8, g * NCMP:(g + 1) * NCMP],
                                                                  src, pos[:, :, None].to_broadcast([HD, 8, NCMP]), ALU.add)
                    ins.then_inc(flat_built, 1)

                def chain(n):
                    u, bank, h, rope, value = M0_CHAINS[n]
                    dve.wait_ge(hsq_done, n + 1)
                    w = h * HD
                    nc.vector.tensor_reduce(ssq[:, n % 4, 0:NT * h].rearrange("p (t h) -> p t h", t=NT), heads4(t2[:, :, :], h, HD), AX.X, ALU.add)\
                        .then_inc(hss_done, 1)
                    dve.wait_ge(hrs_ready, n + 1)
                    rs = srs[:, n % 4, 0:NT * h].rearrange("p (t h) -> p t h", t=NT)[:, :, :, None].to_broadcast([P, NT, h, HD])
                    z = heads4(nat[n % 2][:, :, :], h, HD)
                    nc.vector.tensor_tensor(z, z, rs, ALU.mult).then_inc(hn_ready, 1)
                    dve.wait_ge(hn_ready, n + 1)
                    if n >= 2:
                        dve.wait_ge(hT_done, {2: 2, 3: 4, 4: 5, 5: 6, 6: 7}[n])
                    dst = heads4(t1[n % 2][:, :, :], h, HD)
                    link(nc.vector.tensor_tensor(dst, z, rope_q[rope][:, :, None, 0:HD].to_broadcast([P, NT, h, HD]), ALU.mult))
                    if n < 2:
                        if n == 1:
                            dve.wait_ge(hT_done, 2)
                        link(nc.vector.tensor_tensor(heads4(qg[:, :, :], h, HD), z,
                                                     row("l0_nsa_q_norm")[:, None, None, :].to_broadcast([P, NT, h, HD]), ALU.mult))
                    dve.wait_ge(rot2_ready, n + 1)
                    if h == 2:
                        dve.wait_ge(hT_done, {2: 4, 3: 5, 6: 6}[n])
                        for t in range(NT):
                            a, b = (v[:, t, 0:P].rearrange("p (g d) -> p g d", g=2)[:, :, None, :].to_broadcast([P, 2, 2, HD]) for v in (t1[n % 2], t2))
                            ins = nc.vector.tensor_tensor(qg[:, t, :].rearrange("p (g two d) -> p g two d", g=2, two=2), a, b, ALU.add)
                        ins.then_inc(rot_ready, 1)
                        return
                    nc.vector.tensor_tensor(t1[n % 2][:, :, 0:w], t1[n % 2][:, :, 0:w], t2[:, :, 0:w], ALU.add).then_inc(rot_ready, 1)

                def compressed_keys():
                    dve.wait_ge(ksq_done, 1)
                    nc.vector.tensor_reduce(ssq[0:NCMP, 3, 0:2], kc2[:, :].rearrange("p (g d) -> p g d", g=2), AX.X, ALU.add).then_inc(kss_done, 1)
                    dve.wait_ge(krs_ready, 1)
                    kn = kcv[:, 0:P].rearrange("p (g d) -> p g d", g=2)
                    link(nc.vector.tensor_tensor(kn, kn, srs[0:NCMP, 3, 0:2, None].to_broadcast([NCMP, 2, HD]), ALU.mult))
                    c = ROWS["l0_nsa_kc_norm"][0]
                    nc.vector.tensor_tensor(kcd[:, :].rearrange("p (g two d) -> p g two d", g=2, two=2),
                                            kn[:, :, None, :].to_broadcast([NCMP, 2, 2, HD]),
                                            rows[0:NCMP, None, None, c:c + HD].to_broadcast([NCMP, 2, 2, HD]), ALU.mult).then_inc(kcn_ready, 1)

                lc4 = lc[:, :, :, 0:NCMP]
                lc3 = lc4.rearrange("p t h c -> p (t h) c")

                def block_table(c0, heads):
                    return tab[:, c0:c0 + 30].rearrange("p (t c) -> p t c", t=NT)[:, :, None, :].to_broadcast([P, NT, heads, NCMP])

                def compressed_shift():
                    dve.wait_ge(lc_done, 1)
                    for par, bank in enumerate((4, 7)):
                        sc = ps[:, bank, 0:128].rearrange("p (t h c) -> p t h c", t=NT, h=4)[:, :, :, 0:NCMP]
                        link(nc.vector.tensor_tensor(lc4[:, :, par:8:2, :], sc, block_table(T_CNEG, 4), ALU.add))
                    link(nc.vector.tensor_reduce(lc_n[:, :], lc3, AX.X, ALU.max, negate=True))
                    nc.vector.tensor_tensor(lc3, lc3, lc_n[:, :, None].to_broadcast([P, 16, NCMP]), ALU.add).then_inc(lc_shift, 1)

                def compressed_probabilities():
                    dve.wait_ge(lc_exp, 1)
                    link(nc.vector.tensor_tensor(lc4, lc4, block_table(T_C01, 8), ALU.mult))
                    link(nc.vector.tensor_reduce(lc_d[:, :], lc3, AX.X, ALU.add))
                    link(nc.vector.tensor_scalar(lc_d[:, :], lc_d[:, :], 1e-30, None, ALU.max))
                    link(nc.vector.reciprocal(lc_r[:, :], lc_d[:, :]))
                    g0 = gate[:, :].rearrange("p (t h b) -> p (t h) b", t=NT, b=3)[:, :, 0]
                    link(nc.vector.tensor_tensor(lc_r[:, :], lc_r[:, :], g0, ALU.mult))
                    nc.vector.tensor_tensor(lc3, lc3, lc_r[:, :, None].to_broadcast([P, 16, NCMP]), ALU.mult).then_inc(pc_ready, 1)

                def w_split(n):
                    split_list(u0, M0_SIZES, n)

                w_split(4)
                build_flat()
                dve.wait_ge(flathi_ready, 1)
                nc.vector.tensor_tensor(flat_lo, flat[:, :, :, :], flat_hi.bitcast(F32), ALU.subtract).then_inc(flatlo_ready, 1)
                w_split(5)
                chain(0)
                w_split(6)
                chain(1)
                for n in (7, 8, 9, 10, 11):
                    w_split(n)
                dve.wait_ge(unit_done, u0 + 8)
                gb = row("l0_nsa_gate_b")[:, None, :].to_broadcast([P, NT, 24])
                nc.vector.tensor_tensor(glog[:, :].rearrange("p (t c) -> p t c", t=NT),
                                        ps[:, 0, :].rearrange("p (t n) -> p t n", t=NT)[:, :, 0:24], gb, ALU.add).then_inc(glog_ready, 1)
                dve.wait_ge(gexp_ready, 1)
                link(nc.vector.tensor_scalar(gden1[:, :], gden1[:, :], 1.0, None, ALU.add))
                link(nc.vector.reciprocal(gate[:, :], gden1[:, :]))
                compressed_keys()
                w_split(12)
                chain(2)
                w_split(13)
                chain(3)
                compressed_shift()
                w_split(14)
                compressed_probabilities()
                chain(4)
                w_split(15)
                chain(5)
                w_split(16)
                chain(6)
                attention(A_M0, A_M1)
                for n in (17, 18, 19, 20):
                    w_split(n)
                add_to_x(NORM_M0, 4, 1.0, u0 + M0_UNITS - 1)

            def mixer1():
                u0 = U_M1
                c0 = len(M0_CHAINS)
                nc.vector.tensor_scalar(fgain[:, :], row("l1_fox_q_norm"), 0.125, None, ALU.mult)
                r32 = tab[:, T_R32:T_R32 + 128].rearrange("p (t c) -> p t c", t=NT)
                for i, (name, scale) in enumerate((("l1_mla_q_norm", 96.0 ** -0.5), ("l1_mla_k_norm", 1.0))):
                    g = row(name)
                    ins = nc.vector.tensor_scalar(mtab[i][:, :, 0:HD], g[:, None, 0:HD].to_broadcast([P, NT, HD]), scale, None, ALU.mult)
                    for a, b, w, r in ((HD, HD, 32, 0), (96, HD + 16, 16, 32), (112, HD, 16, 48)):
                        ins = nc.vector.scalar_tensor_tensor(out=mtab[i][:, :, a:a + w], in0=g[:, None, b:b + w].to_broadcast([P, NT, w]), scalar=scale,
                                                             in1=r32[:, :, r:r + w], op0=ALU.mult, op1=ALU.mult)
                link(ins)

                def chain_rows(n):
                    what, part, _ = M1_CHAINS[n]
                    return (natm[part] if what in ("mq", "mk") else nat1[{"cq": 3, "ckv": 2, "q": part, "k": 2 + part}[what]])

                def sums(n):
                    what, part, _ = M1_CHAINS[n]
                    dve.wait_ge(hsq_done, c0 + n + 1)
                    if what in ("cq", "ckv"):
                        w = 256 if what == "cq" else P
                        dst, src = ssq[:, n % 4, 0:NT], sq1[:, :, 0:w]
                    else:
                        w = 96 if what in ("mq", "mk") else HD
                        dst, src = ssq[:, n % 4, :].rearrange("p (t h) -> p t h", t=NT), heads4(sq1[:, :, 0:4 * w], 4, w)
                    nc.vector.tensor_reduce(dst, src, AX.X, ALU.add).then_inc(hss_done, 1)

                def scaled(n):
                    what, part, _ = M1_CHAINS[n]
                    dve.wait_ge(hrs_ready, c0 + n + 1)
                    if what in ("cq", "ckv"):
                        w = 256 if what == "cq" else P
                        z = chain_rows(n)[:, :, 0:w]
                        nc.vector.tensor_tensor(z, z, srs[:, n % 4, 0:NT, None].to_broadcast([P, NT, w]), ALU.mult).then_inc(rot_ready, 1)
                        return
                    w = 96 if what in ("mq", "mk") else HD
                    z = heads4(chain_rows(n)[:, :, :], 4, w)
                    rs = srs[:, n % 4, :].rearrange("p (t h) -> p t h", t=NT)[:, :, :, None].to_broadcast([P, NT, 4, w])
                    ins = nc.vector.tensor_tensor(z, z, rs, ALU.mult)
                    if w == 96:
                        ins.then_inc(hn_ready, 1)
                        return
                    link(ins)
                    g = fgain[:, :] if what == "q" else row("l1_fox_k_norm")
                    nc.vector.tensor_tensor(z, z, g[:, None, None, :].to_broadcast([P, NT, 4, HD]), ALU.mult).then_inc(rot_ready, 1)

                def rotated(n, m):
                    what, part, _ = M1_CHAINS[n]
                    z = heads4(natm[part][:, :, :], 4, 96)
                    dve.wait_ge(hn_ready, c0 + m + 1)
                    dve.wait_ge(rot2_ready, c0 + m + 1)
                    link(nc.vector.tensor_tensor(z, z, mtab[int(what == "mk")][:, :, None, 0:96].to_broadcast([P, NT, 4, 96]), ALU.mult))
                    nc.vector.tensor_tensor(z[:, :, :, HD:96], z[:, :, :, HD:96], heads4(r2[:, :, :], 4, 32), ALU.add).then_inc(mrot_ready, 1)

                def c_lo(n):
                    dve.wait_ge(chi_ready, n + 1)
                    if n == 0:
                        cc = COLS["l1_mla_q_a_norm"][0]
                        for k in range(2):
                            ins = nc.vector.scalar_tensor_tensor(out=cq_lo[:, k, :], in0=ps[:, 2, k * SEQ:(k + 1) * SEQ], scalar=cols[:, cc + k:cc + k + 1],
                                                                 in1=cq_hi[:, k, :].bitcast(F32), op0=ALU.mult, op1=ALU.subtract)
                    else:
                        cc = COLS["l1_mla_kv_a_norm"][0]
                        ins = nc.vector.scalar_tensor_tensor(out=ckv_lo, in0=ps[:, 3, 0:SEQ], scalar=cols[:, cc:cc + 1],
                                                             in1=ckv_hi.bitcast(F32), op0=ALU.mult, op1=ALU.subtract)
                    ins.then_inc(clo_ready, 1)

                def w_split(n):
                    split_list(u0, M1_SIZES, n)

                w_split(4)
                sums(0)
                w_split(5)
                scaled(0)
                sums(1)
                scaled(1)
                c_lo(0)
                w_split(6)
                sums(2)
                c_lo(1)
                scaled(2)
                w_split(7)
                sums(3)
                scaled(3)
                sums(4)
                rotated(3, 0)
                w_split(8)
                scaled(4)
                rotated(4, 1)
                sums(5)
                w_split(9)
                scaled(5)
                sums(6)
                w_split(10)
                scaled(6)
                rotated(6, 2)
                sums(7)
                scaled(7)
                sums(8)
                w_split(11)
                scaled(8)
                rotated(8, 3)
                sums(9)
                w_split(12)
                scaled(9)
                dve.wait_ge(unit_done, u0 + 9)
                fb = row("l1_fox_f_bias")[:, None, :].to_broadcast([P, NT, 8])
                link(nc.vector.tensor_tensor(fz[:, :].rearrange("p (t h) -> p t h", t=NT),
                                             ps[:, 0, :].rearrange("p (t n) -> p t n", t=NT)[:, :, 0:8], fb, ALU.add))
                nc.vector.scalar_tensor_tensor(out=fa[:, :], in0=fz[:, :], scalar=-1.0, in1=fz[:, :], op0=ALU.mult, op1=ALU.max).then_inc(f_abs, 1)
                w_split(13)
                dve.wait_ge(f_ln, 1)
                nc.vector.scalar_tensor_tensor(out=lf[:, :, :].rearrange("p t h -> p (t h)"), in0=fz[:, :], scalar=0.0, in1=fl[:, :],
                                               op0=ALU.min, op1=ALU.subtract).then_inc(lf_ready, 1)
                w_split(14)
                dve.wait_ge(dt_done, 1)
                nc.vector.tensor_scalar(negDT[:, :], ps[0:8, 1, 0:SEQ], -1.0, None, ALU.mult)
                nc.vector.tensor_copy(dnat[:, :, :].rearrange("p t h -> p (t h)"), ps[:, 1, SEQ:SEQ + 16]).then_inc(dt_ready, 1)
                attention(A_M1, A_END)
                for n in (15, 16, 17, 18):
                    w_split(n)
                add_to_x(NORM_M1, 4, 1.0, u0 + M1_UNITS - 1)

            nc.vector.memset(zero_b[:, :], 0.0)
            nc.vector.memset(mask1[:, 0:P], 0.0).then_inc(const_ready, 1)
            norm(0)
            for n in range(LEAD):
                split(n, n)
            ffn(0, False)
            norm(1)
            mixer0()
            norm(2)
            ffn(1, False)
            norm(3)
            ffn(2, False)
            norm(4)
            mixer1()
            norm(5)
            ffn(3, True)

        @block.tensor
        def _(pe):
            def passes(dst, lhs, rhs, start, stop):
                nc.tensor.matmul(dst, lhs[0], rhs[0], start=start, stop=False)
                nc.tensor.matmul(dst, lhs[0], rhs[1], start=False, stop=False)
                return nc.tensor.matmul(dst, lhs[1], rhs[0], start=False, stop=stop)

            def wslot(us, size, inner):
                return tuple(w[us % SPLIT][:, 0:size].rearrange("p (a b) -> p a b", b=inner) for w in (w_hi, w_lo))

            def norm(m, zero):
                def tr(q, t):
                    for c in range(2):
                        ins = nc.tensor.transpose(ps[:, 6 + q % 2, c * SEQ + t * P:c * SEQ + (t + 1) * P],
                                                  xn[:, t, (2 * q + c) * P:(2 * q + c + 1) * P], ident)
                    return ins

                pe.wait_ge(xn_ready, NT * m + 1)
                tr(0, 0)
                tr(1, 0)
                pe.wait_ge(xn_ready, NT * m + 2)
                tr(0, 1).then_inc(xT_ready, 1)
                tr(1, 1).then_inc(xT_ready, 1)
                for q in (2, 3):
                    pe.wait_ge(hlo_ready, DC * m + 2 * (q - 1))
                    tr(q, 0)
                    tr(q, 1).then_inc(xT_ready, 1)
                if zero:
                    for b in range(4):
                        nc.tensor.matmul(ps[:, b, :], zero_b[:, :], zero_b[:, 0:1].to_broadcast([P, 512]), start=True, stop=False)

            def down(us, lhs, last, bank, start=False):
                w = wslot(us, UNIT, D)
                for t in range(NT):
                    for half in range(2):
                        for c in range(2):
                            ins = passes(ps[:, bank + 2 * t + half, :], tuple(v[:, c, t * P:(t + 1) * P] for v in lhs),
                                         tuple(v[:, c, half * 512:(half + 1) * 512] for v in w),
                                         start and c == 0, last and c == 1)
                    if last and t == 0:
                        ins.then_inc(acc_ready, 1)
                return ins

            def ffn(f):
                u0 = U_FFN[f]
                m = NORM_FFN[f]

                def gate_up(j, js):
                    bank = 4 + 2 * (js % 2)
                    u = u0 + (3 * js - 1 if js else 0)
                    loop = not isinstance(j, int)
                    if loop:
                        pe.wait_ge(mul_done, 2 * j + (11 * f + js - 1) if 11 * f + js - 1 > 0 else 2 * j + 1)
                    for n in range(2):
                        us = u + n
                        pe.wait_ge(lo_ready, (6 * j if loop else 0) + us + 1)
                        w = wslot(us, UNIT, STEP)
                        for b in range(2):
                            for k in range(DC):
                                if js == 0 and n == 0 and b == 0:
                                    pe.wait_ge(hlo_ready, DC * m + k + 1)
                                ins = passes(ps[:, bank + b, n * SEQ:(n + 1) * SEQ], tuple(v[:, k, b * P:(b + 1) * P] for v in w),
                                             (h_hi[:, k, :], h_lo[:, k, :]), k == 0, k == DC - 1)
                        ins.then_inc(unit_done, 1)

                def down_step(j, js):
                    us = u0 + down_index(js)
                    loop = not isinstance(j, int)
                    pe.wait_ge(lo_ready, (6 * j if loop else 0) + us + 1)
                    pe.wait_ge(alo_ready, (2 * j if loop else 0) + (11 * f + js + 1))
                    lhs = (a_hi[:, js % 2, :, :], a_lo[:, js % 2, :, :])
                    down(us, lhs, js == NSTEP - 1 and not loop, 0).then_inc(unit_done, 1)

                gate_up(0, 0)
                with pe.Fori(0, (NSTEP - 1) // 2) as i:
                    for half in range(2):
                        gate_up(i, 1 + half)
                        down_step(i, half)
                down_step(NSTEP - 1, NSTEP - 1)

            def att_qk(j):
                a, qt, hs = job_heads(j)
                kind, g = ATT[a]
                if j >= QK_RING:
                    pe.wait_ge(exp_done, j - QK_RING + 1)
                mk = mask0 if qt == 0 else mask1w if kind == SWA else mask1
                n = 4 if qt == 0 else 2
                nc.tensor.matmul(ps[:, 2 + j % QK_RING, :], id_b[:, :], mk[:, None, :].to_broadcast([P, n, 512 // n]), start=True, stop=False)
                heads = range(0, 4, 2) if qt == 0 else range(hs.start, 4, 2)
                for n, i in enumerate(heads):
                    ins = att_head(j, i, n if qt else 2 * n, qt == 1 and n == 1)
                ins.then_inc(qk_done if qt else even_done, 1)

            def att_qk_odd(j):
                a, qt, hs = job_heads(j)
                if qt == 0:
                    pe.wait_ge(even_done, a + 1)
                    att_head(j, 1, 1, False)
                    att_head(j, 3, 3, True).then_inc(qk_done, 1)

            def att_head(j, i, n, end):
                a, qt, hs = job_heads(j)
                kind, g = ATT[a]
                h = 4 * g + i
                keys = P * (qt + 1)
                dst = ps[:, 2 + j % QK_RING, n * keys:(n + 1) * keys]
                r = slice((h % 2) * HD, (h % 2 + 1) * HD)
                if kind == MLA:
                    q, k = qmT[:, h, qt * P:(qt + 1) * P], kmT[:, h, 0:keys]
                elif kind == FOX:
                    q, k = qfT[r, h // 2, qt * P:(qt + 1) * P], kfT[r, h // 2, 0:keys]
                else:
                    q = (qbT if kind == SWA else qrT)[r, h // 2, qt * P:(qt + 1) * P]
                    k = kT[{SLC: 0, WIN: 1, SWA: 2}[kind]][r, g, 0:keys]
                if kind == FOX:
                    nc.tensor.matmul(dst, ident[0:8, h:h + 1].to_broadcast([8, P]), negDT[:, 0:keys], start=False, stop=False)
                return nc.tensor.matmul(dst, q, k, start=False, stop=end)

            def att_pT(j):
                pe.wait_ge(ps_ready, j + 1)
                if j >= T_RING:
                    pe.wait_ge(pT_ready, j - T_RING + 1)
                for c in range(4):
                    ins = nc.tensor.transpose(ps[:, 6 + j % T_RING, c * P:(c + 1) * P], prob[j % QK_RING][:, c * P:(c + 1) * P], ident)
                ins.then_inc(pt_done, 1)

            def att_pv(j):
                a, qt, hs = job_heads(j)
                kind, g = ATT[a]
                pe.wait_ge(pT_ready, j + 1)
                if a in (4, 5, 8, 9) and j % JOBS == 0:
                    pe.wait_ge(olo_ready, a - 3)
                bank = ps[:, g, :].rearrange("p (c t) -> p c t", c=2)
                pt = pT[j % PT_RING][:, :].rearrange("p (h q) -> p h q", h=4) if qt == 0 else \
                    pT[j % PT_RING][:, :].rearrange("p (h k q) -> p k h q", h=2, k=2)
                fresh = kind in (SWA, FOX, MLA)
                if kind in (SLC, WIN, SWA):
                    v = vN[{SLC: 0, WIN: 1, SWA: 2}[kind]]
                    if qt == 0:
                        for par in range(2):
                            r = slice(par * HD, (par + 1) * HD)
                            ins = nc.tensor.matmul(bank[r, :, 0:P], v[:, 0, g * HD:(g + 1) * HD], pt[:, par:4:2, :], start=fresh, stop=fresh)
                    else:
                        r = slice(hs.start * HD, (hs.start + 1) * HD)
                        for kc in range(2):
                            ins = nc.tensor.matmul(bank[r, :, P:SEQ], v[:, kc, g * HD:(g + 1) * HD], pt[:, kc, :, :], start=fresh and kc == 0,
                                                   stop=kind != SLC and kc == 1)
                else:
                    for n, i in enumerate(range(4)[hs]):
                        h = 4 * g + i
                        r = slice((h % 2) * HD, (h % 2 + 1) * HD)
                        for kc in range(qt + 1):
                            v = vf[:, kc, h * HD:(h + 1) * HD] if kind == FOX else vm[:, kc, h, :]
                            ins = nc.tensor.matmul(bank[r, i // 2, qt * P:(qt + 1) * P], v, pt[:, n, :] if qt == 0 else pt[:, kc, n, :],
                                                   start=kc == 0, stop=kc == qt)
                ins.then_inc(pv_done, 1)

            def attention(a0, a1, before_loop=None):
                j0, j1 = JOBS * a0, JOBS * a1
                for j in range(j0, j0 + 3):
                    att_qk(j)
                    att_qk_odd(j)
                if before_loop:
                    before_loop()
                for j in range(j0, j1):
                    if j + 3 < j1:
                        att_qk(j + 3)
                    att_pT(j)
                    if j + 3 < j1:
                        att_qk_odd(j + 3)
                    if j > j0:
                        att_pv(j - 1)
                att_pv(j1 - 1)

            def project(u0, n, width, bank):
                us = u0 + n
                pe.wait_ge(lo_ready, us + 1)
                w = wslot(us, DC * width, width)
                for t in range(NT):
                    for k in range(DC):
                        ins = passes(ps[:, bank, t * 256:t * 256 + width], tuple(v[:, k, t * P:(t + 1) * P] for v in (h_hi, h_lo)),
                                     tuple(v[:, k, :] for v in w), k == 0, k == DC - 1)
                ins.then_inc(unit_done, 1)

            def out_proj(u0, first, e0, parts):
                for e in range(4):
                    us = u0 + first + e
                    pe.wait_ge(lo_ready, us + 1)
                    pe.wait_ge(olo_ready, e0 + e + 1)
                    down(us, parts(e), e == 3, 4, start=e == 0).then_inc(unit_done, 1)

            def mixer0():
                u0 = U_M0

                def tjob(j):
                    n, what = M0_TJOBS[j]
                    pe.wait_ge(rot_ready, n + 1)
                    if j >= 2:
                        pe.wait_ge(hT_ready, j - 1)
                    src = t1[n % 2] if what == "rot" and M0_CHAINS[n][2] == 4 else qg
                    for c in range(2):
                        for t in range(NT):
                            ins = nc.tensor.transpose(ps[:, 5 + j % 2, c * SEQ + t * P:c * SEQ + (t + 1) * P],
                                                      src[:, t, c * P:(c + 1) * P], ident)
                    ins.then_inc(hT_done, 1)

                def proj(u):
                    if u in (7, 8):
                        pe.wait_ge(nat_ready, u - 6)
                    if u == 9:
                        pe.wait_ge(hid_ready, 1)
                    if u == 11:
                        pe.wait_ge(glog_ready, 1)
                    if u == 12:
                        pe.wait_ge(nat_ready, 3)
                    bank = 0 if u == 7 else [c[1] for c in M0_CHAINS if c[0] == u][0]
                    project(u0, u, M0_COLS[M0_PROJ.index(u)][1], bank)

                def hidden(u):
                    m, n = divmod(u - 3, 2)
                    pe.wait_ge(flatlo_ready, 1)
                    pe.wait_ge(lo_ready, u0 + u + 1)
                    w = wslot(u0 + u, UNIT, CMPH)
                    for half in range(2):
                        for c in range(8):
                            ins = passes(ps[:, 2 + half, m * 32:m * 32 + 30], tuple(v[:, c, half * P:(half + 1) * P] for v in w),
                                         (flat_hi[:, m, 8 * n + c, :], flat_lo[:, m, 8 * n + c, :]), n == 0 and c == 0, n == 1 and c == 7)
                    ins.then_inc(unit_done, 1)

                pe.wait_ge(cast_ready, 1)
                pe.wait_ge(lo_ready, u0 + 1)
                w = wslot(u0, UNIT, 256)
                for m in range(2):
                    for k in range(DC):
                        pe.wait_ge(hlo_ready, DC * NORM_M0 + k + 1)
                        ins = passes(ps[:, 4, m * SEQ:(m + 1) * SEQ], tuple(v[:, k, m * P:(m + 1) * P] for v in w),
                                     (h_hi[:, k, :], h_lo[:, k, :]), k == 0, k == DC - 1)
                ins.then_inc(unit_done, 1)
                proj(1)
                proj(2)
                tjob(0)
                tjob(1)
                hidden(3)
                hidden(4)
                tjob(2)
                tjob(3)
                hidden(5)
                hidden(6)
                proj(7)
                pe.wait_ge(hid_ready, 1)
                for m in range(2):
                    for g in range(2):
                        for half in range(2):
                            ins = nc.tensor.matmul(ps[0:NCMP, 4, m * P + g * HD:m * P + (g + 1) * HD], hid[:, m, half, g * NCMP:(g + 1) * NCMP],
                                                   w2[:, m, half, :], start=half == 0, stop=half == 1)
                ins.then_inc(kcv_done, 1)
                proj(8)
                pe.wait_ge(kcn_ready, 1)
                for g in range(2):
                    ins = nc.tensor.transpose(ps[:, 7, g * 16:g * 16 + NCMP], kcd[:, g * P:(g + 1) * P], ident[0:NCMP, 0:NCMP])
                ins.then_inc(kcT_done, 1)
                proj(9)
                pe.wait_ge(kcT_ready, 1)
                pe.wait_ge(hT_ready, 4)
                for t in range(NT):
                    for h in range(8):
                        r = slice((h % 2) * HD, (h % 2 + 1) * HD)
                        c = (t * 4 + h // 2) * 16
                        ins = nc.tensor.matmul(ps[:, (4, 7)[h % 2], c:c + NCMP], qaT[r, h // 2, t * P:(t + 1) * P],
                                               kcT[r, h // 4, 0:NCMP], start=True, stop=True)
                ins.then_inc(lc_done, 1)
                tjob(4)
                proj(10)
                tjob(5)
                proj(11)
                tjob(6)
                proj(12)
                tjob(7)
                pe.wait_ge(pc_ready, 1)
                for b in range(4):
                    if b >= 2:
                        pe.wait_ge(pcT_ready, b - 1)
                    for h in (2 * b, 2 * b + 1):
                        for t in range(NT):
                            ins = nc.tensor.transpose(ps[0:NCMP, (4, 7)[b % 2], (h % 2) * SEQ + t * P:(h % 2) * SEQ + (t + 1) * P],
                                                      lc[:, t, h, 0:NCMP], ident)
                    ins.then_inc(pcT_done, 1)

                def compressed_values():
                    tjob(8)
                    pe.wait_ge(nat_ready, len(M0_CHAINS))
                    pe.wait_ge(pcT_ready, 4)
                    for g in range(2):
                        for par in range(2):
                            nc.tensor.matmul(ps[par * HD:(par + 1) * HD, g, :].rearrange("p (c t) -> p c t", c=2), kcv[:, P + g * HD:P + (g + 1) * HD],
                                             pcT[:, 4 * g + par:4 * g + 4:2, :], start=True, stop=False)
                    pe.wait_ge(hT_ready, len(M0_TJOBS))

                compressed_values()
                attention(A_M0, A_M1)
                out_proj(u0, NPROJ + 4, 0, lambda e: (h_hi[:, 2 * e:2 * e + 2, :], h_lo[:, 2 * e:2 * e + 2, :]))

            def mixer1():
                u0 = U_M1
                c0 = len(M0_CHAINS)
                o0 = len(M0_TJOBS)

                def proj(u):
                    i = M1_PROJ.index(u)
                    if u == 0:
                        pe.wait_ge(hlo_ready, DC * NORM_M1 + DC)
                    elif u == 9:
                        pe.wait_ge(hsq_done, c0 + 10)
                    elif u == 10:
                        pe.wait_ge(f_abs, 1)
                    elif i >= 2:
                        last = M1_PROJ[i - 2]
                        pe.wait_ge(hsq_done, c0 + 1 + [c[2] for c in M1_CHAINS].index(last))
                    project(u0, u, M1_COLS[i][1], i % 2)

                def c_T(n):
                    pe.wait_ge(rot_ready, c0 + n + 1)
                    for c in range(2 - n):
                        for t in range(NT):
                            ins = nc.tensor.transpose(ps[:, 2 + n, c * SEQ + t * P:c * SEQ + (t + 1) * P], nat1[3 - n][:, t, c * P:(c + 1) * P], ident)
                    ins.then_inc(cT_done, 1)

                def m_T(n):
                    pe.wait_ge(mrot_ready, n + 1)
                    if n:
                        pe.wait_ge(mT_ready, n)
                    for h in range(4):
                        for t in range(NT):
                            ins = nc.tensor.transpose(ps[0:96, 2 + h // 2, (h % 2) * SEQ + t * P:(h % 2) * SEQ + (t + 1) * P],
                                                      natm[n % 2][:, t, h * 96:(h + 1) * 96], ident)
                    ins.then_inc(mT_done, 1)

                proj(0)
                proj(1)
                c_T(0)
                proj(2)
                c_T(1)
                pe.wait_ge(clo_ready, 1)
                pe.wait_ge(lo_ready, u0 + 4)
                w = wslot(u0 + 3, 1536, 768)
                for half in range(2):
                    for t in range(NT):
                        for c in range(2):
                            ins = passes(ps[:, 4 + 2 * half + t, 0:384], tuple(v[:, c, t * P:(t + 1) * P] for v in (cq_hi, cq_lo)),
                                         tuple(v[:, c, half * 384:(half + 1) * 384] for v in w), c == 0, c == 1)
                ins.then_inc(unit_done, 1)
                proj(4)
                pe.wait_ge(clo_ready, 2)
                pe.wait_ge(hsq_done, c0 + 5)
                pe.wait_ge(lo_ready, u0 + 6)
                w = wslot(u0 + 5, 1024, 1024)
                for half in range(2):
                    for t in range(NT):
                        ins = passes(ps[:, 4 + 2 * half + t, :], (ckv_hi[:, t * P:(t + 1) * P], ckv_lo[:, t * P:(t + 1) * P]),
                                     tuple(v[:, 0, half * 512:(half + 1) * 512] for v in w), True, True)
                ins.then_inc(unit_done, 1)
                m_T(0)
                proj(6)
                m_T(1)
                proj(7)
                m_T(2)
                proj(8)
                proj(9)
                m_T(3)
                proj(10)
                for j in range(4):
                    pe.wait_ge(rot_ready, c0 + 2 + j + 1)

                    if j == 2:
                        pe.wait_ge(nat_ready, c0 + 2)
                    if j == 3:
                        pe.wait_ge(mT_ready, 4)
                    for c in range(2):
                        for t in range(NT):
                            ins = nc.tensor.transpose(ps[:, FOX_T_BANK[j], c * SEQ + t * P:c * SEQ + (t + 1) * P],
                                                      nat1[j][:, t, c * P:(c + 1) * P], ident)
                    ins.then_inc(hT_done, 1)
                pe.wait_ge(lf_ready, 1)
                pe.wait_ge(nat_ready, c0 + 1)
                tri, ones = tab[:, T_TRI:T_TRI + P], tab[:, T_TRI + P:T_TRI + 2 * P]
                nc.tensor.matmul(ps[0:8, 1, 0:SEQ], lf[:, 0, :], tab[:, T_TRI:T_TRI + SEQ], start=True, stop=False)
                nc.tensor.matmul(ps[0:8, 1, P:SEQ], lf[:, 1, :], tri, start=False, stop=True)
                nc.tensor.matmul(ps[:, 1, SEQ:SEQ + 8], tri, lf[:, 0, :], start=True, stop=True)
                nc.tensor.matmul(ps[:, 1, SEQ + 8:SEQ + 16], ones, lf[:, 0, :], start=True, stop=False)
                nc.tensor.matmul(ps[:, 1, SEQ + 8:SEQ + 16], tri, lf[:, 1, :], start=False, stop=True).then_inc(dt_done, 1)

                def banks_free():
                    pe.wait_ge(hT_ready, o0 + 4)
                    pe.wait_ge(dt_ready, 1)

                pe.wait_ge(mT_ready, 4)
                attention(A_M1, A_END, banks_free)
                out_proj(u0, NPROJ + 2, 4, lambda e: tuple(v[:, 2 * (e % 2):2 * (e % 2) + 2, :] for v in ((oA_hi, oA_lo) if e < 2 else (oB_hi, oB_lo))))

            pe.wait_ge(ident_loaded, 16)
            pe.wait_ge(const_ready, 1)
            norm(0, True)
            ffn(0)
            norm(1, False)
            mixer0()
            norm(2, True)
            ffn(1)
            norm(3, True)
            ffn(2)
            norm(4, False)
            mixer1()
            norm(5, True)
            ffn(3)


def shape_tables():
    i = np.arange(P)
    t = np.zeros((P, T_COLS), np.float32)
    t[:, T_ID:T_ID + P] = np.eye(P)
    t[:, T_TRI:T_TRI + P] = i[None, :] >= i[:, None]
    t[:, T_TRI + P:T_TRI + 2 * P] = 1.0
    t[:, T_CAUSAL:T_CAUSAL + P] = np.where(i[None, :] <= i[:, None], 0.0, -BIG)
    t[:, T_BAND:T_BAND + P] = np.where(i[None, :] > i[:, None], 0.0, -BIG)
    for tile in range(NT):
        pos = (tile * P + i).astype(np.float32)[:, None]
        for at_, dim in ((T_R64 + tile * P, 64), (T_R32 + tile * 64, 32)):
            inv = (1.0 / (np.float32(10000.0) ** (np.arange(0, dim, 2, dtype=np.float32) / np.float32(dim)))).astype(np.float32)
            ang = (pos * inv[None, :]).astype(np.float32)
            c, s = np.cos(ang), np.sin(ang)
            t[:, at_:at_ + 2 * dim] = np.concatenate([c, c, -s, s], 1)
        seen = (np.arange(NCMP) * CS + CB - 1)[None, :] <= pos
        t[:, T_CNEG + tile * NCMP:T_CNEG + (tile + 1) * NCMP] = np.where(seen, 0.0, -BIG)
        t[:, T_C01 + tile * NCMP:T_C01 + (tile + 1) * NCMP] = seen
    return t


def kernel(**inputs):
    import concourse.bacc as bacc
    from concourse.bass_utils import run_bass_kernel_spmd

    nc = bacc.Bacc("TRN2", target_bir_lowering=False, num_devices=1)
    arrays = {name: np.ascontiguousarray(a) for name, a in inputs.items()}
    by_column = [arrays.pop(name).reshape(w, P).T for name, (_, w) in COLS.items()]
    by_column += [arrays.pop(name).reshape(2, P, HD).transpose(1, 0, 2).reshape(P, 2 * HD) for name in ("l0_cmpk_w2", "l0_cmpv_w2")]
    arrays["columns"] = np.ascontiguousarray(np.concatenate(by_column, 1))
    arrays["rows"] = np.concatenate([arrays.pop(name) for name in ROWS])
    arrays["shape_tables"] = shape_tables()
    A = {}
    for name, a in arrays.items():
        A[name] = nc.dram_tensor(name, a.shape, mybir.dt.from_np(a.dtype), kind="ExternalInput").ap()
    out = nc.dram_tensor("out", (1, SEQ, D), F32, kind="ExternalOutput").ap()
    trunk(nc, A, out)
    r = run_bass_kernel_spmd(nc, [arrays], core_ids=[0])
    return r.results[0]["out"]
```

```python
from contextlib import ExitStack

import numpy as np
import concourse.bass as bass
from concourse import mybir

F32 = mybir.dt.float32
F32R = mybir.dt.float32r
BF16 = mybir.dt.bfloat16
ALU = mybir.AluOpType
ACT = mybir.ActivationFunctionType
AX = mybir.AxisListType

P = 128
SEQ = 256
NT = SEQ // P
D = 1024
DC = D // P
FF = 2816
STEP = 256
NSTEP = FF // STEP
HD = 64
EPS = 1e-6
BIG = 1e30
NCMP = 15
CMPH = 256
CB, CS = 32, 16
UNIT = 2048
RAW, SPLIT = 3, 6
LEAD = 4

FFN_UNITS = 3 * NSTEP
M0_COLS = [(512, 256), (0, 256), (256, 256), (1280, 128), (768, 256), (1024, 256), (1304, 256), (1560, 256), (1816, 256)]
M0_PROJ = [0, 1, 2, 3, 5, 7, 10, 11, 12]
M1_COLS = [(1536, 256), (1704, 256), (0, 256), (256, 256), (512, 256), (768, 256), (1024, 256), (1280, 256)]
M1_PROJ = [0, 1, 2, 4, 6, 7, 8, 9]
NPROJ = len(M0_PROJ)
M0_OUT = NPROJ + 4
M0_UNITS = M0_OUT + 4
M1_OUT = len(M1_PROJ) + 2
M1_UNITS = M1_OUT + 4
M0_EXACT = (4, 6, 8, 9)
M0_SIZES = {u: DC * w for u, (_, w) in zip(M0_PROJ, M0_COLS)} | {u: UNIT for u in (*M0_EXACT, *range(M0_OUT, M0_UNITS))}
M1_SIZES = {u: DC * w for u, (_, w) in zip(M1_PROJ, M1_COLS)} | {3: 2 * 768, 5: 1024} | {u: UNIT for u in range(M1_OUT, M1_UNITS)}
U_FFN = [0, FFN_UNITS + M0_UNITS, 2 * FFN_UNITS + M0_UNITS, 3 * FFN_UNITS + M0_UNITS + M1_UNITS]
U_M0 = FFN_UNITS
U_M1 = 3 * FFN_UNITS + M0_UNITS
U_END = 4 * FFN_UNITS + M0_UNITS + M1_UNITS
NORM_FFN = [0, 2, 3, 5]
NORM_M0, NORM_M1 = 1, 4
X_PARTS = ((0, 0, D), (1, 0, D // 2), (1, D // 2, D))
N_PARTS = len(X_PARTS)
T_BANK = (4, 4, 0, 4, 4, 0)

T_ID, T_TRI, T_CAUSAL, T_BAND = 0, 128, 384, 512
T_R64, T_R32, T_CNEG, T_C01, T_COLS = 640, 896, 1024, 1054, 1084
ROWS = {}
_at = 0
for _n, _w in (("l0_nsa_q_norm", 64), ("l0_nsa_kc_norm", 64), ("l0_nsa_ks_norm", 64), ("l0_nsa_kw_norm", 64),
               ("l0_swa_q_norm", 64), ("l0_swa_k_norm", 64), ("l0_swa_sinks", 8), ("l0_nsa_gate_b", 24),
               ("l1_fox_f_bias", 8), ("l1_fox_q_norm", 64), ("l1_fox_k_norm", 64),
               ("l1_mla_q_norm", 96), ("l1_mla_k_norm", 96)):
    ROWS[_n] = (_at, _w)
    _at += _w
ROWS_W = _at
COLS = {}
_at = 0
for _n, _w in (("l0_ffn1_norm", 8), ("l0_mix_norm", 8), ("l0_ffn2_norm", 8), ("l1_ffn1_norm", 8), ("l1_mix_norm", 8),
               ("l1_ffn2_norm", 8), ("l0_cmp_pos_k", 16), ("l0_cmp_pos_v", 16), ("l1_mla_q_a_norm", 2),
               ("l1_mla_kv_a_norm", 1)):
    COLS[_n] = (_at, _w)
    _at += _w
COLS_W = _at

A_M0, A_M1, A_END = 0, 6, 10
SLC, WIN, SWA, FOX, MLA = range(5)
ATT = [(SLC, 0), (SLC, 1), (WIN, 0), (WIN, 1), (SWA, 0), (SWA, 1), (MLA, 0), (MLA, 1), (FOX, 0), (FOX, 1)]
M0_POOL, M1_POOL = 3, 3
POOL_UNITS = [*range(U_M0 + M0_OUT, U_M0 + M0_OUT + M0_POOL), *range(U_M1 + M1_OUT, U_M1 + M1_OUT + M1_POOL)]
FOX_T_BANK = (6, 7, 1, 3)
JOBS = 3
QK_RING, T_RING, PT_RING = 4, 2, 5
OUT_OF = {2: 0, 3: 1, 4: 2, 5: 3, 6: 4, 7: 5, 8: 6, 9: 7}
M0_CHAINS = [(1, 0, 4, 0, None), (2, 1, 4, 0, None), (5, 1, 2, 1, 0), (7, 0, 2, 2, 1), (10, 2, 4, 3, None), (11, 3, 4, 3, None), (12, 1, 2, 4, 2)]
M0_TJOBS = [(0, "rot"), (0, "gain"), (1, "rot"), (1, "gain"), (2, "rot"), (3, "rot"), (4, "rot"), (5, "rot"), (6, "rot")]
M1_CHAINS = [("cq", 0, 1), ("ckv", 0, 1), ("q", 0, 2), ("mq", 0, 3), ("mq", 1, 3), ("q", 1, 4), ("mk", 0, 5), ("k", 0, 6), ("mk", 1, 5), ("k", 1, 7)]


def trunk(nc, A, out):
    ctx = ExitStack()
    with ctx:
        def sem(name):
            return ctx.enter_context(nc.semaphore(name))

        top = nc.sbuf_usable_end
        base = (nc.sbuf_base + 63) // 32 * 32
        slab = ctx.enter_context(nc.sbuf_tensor("slab", [P, (top - base) // 4 - 16], F32))
        place = [base]

        def at(name, shape, dt=F32, offset=None):
            size = int(np.prod(shape[1:])) * (2 if dt == BF16 else 4)
            here = place[0] if offset is None else offset
            if offset is None:
                place[0] = here + (size + 31) // 32 * 32
                assert place[0] <= top, (name, place[0] - top)
            return nc.alloc_sbuf_tensor_at(name, shape, dt, offset=here)

        raw = [at(f"raw{i}", [P, UNIT]) for i in range(RAW)]
        w_at = place[0]
        w_hi = [at(f"w_hi{i}", [P, UNIT], F32R) for i in range(SPLIT)]
        w_lo = [at(f"w_lo{i}", [P, UNIT], F32R) for i in range(SPLIT)]
        w_half0, w_half1 = ([at(f"w_half{h}_{i}", [P, UNIT // 2], offset=w_at + (h * SPLIT + i) * UNIT * 4) for i in range(SPLIT)] for h in range(2))
        x = at("x_res", [P, NT, D])
        h_at = place[0]
        h_hi = at("h_hi", [P, DC, SEQ], F32R)
        h_lo = at("h_lo", [P, DC, SEQ], F32R)
        a_at = place[0]
        a_hi = at("a_hi", [P, 2, 2, SEQ], F32R)
        a_lo = at("a_lo", [P, 2, 2, SEQ], F32R)
        tab = at("tab", [P, T_COLS])
        rows = at("rows", [P, ROWS_W])
        par = at("par", [P, COLS_W + 4 * HD])
        id_b = at("id_b", [P, P], BF16)
        zero_b = at("zero_b", [P, P], BF16)
        mask0 = at("mask0", [P, P], BF16)
        mask1 = at("mask1", [P, 2 * P], BF16)
        mask1w = at("mask1w", [P, 2 * P], BF16)
        ms = at("ms", [P, 6, N_PARTS])
        ms_eps = at("ms_eps", [P, 6, NT])
        rstd = at("rstd", [P, 6, NT])
        mhalf = at("mhalf", [P, 16])
        arena = place[0]
        ident = tab[:, T_ID:T_ID + P]
        cols = par[:, 0:COLS_W]
        w2 = par[:, COLS_W:COLS_W + 4 * HD].rearrange("p (m c n) -> p m c n", m=2, c=2)

        sg = at("sg", [P, 2 * SEQ])
        act_v = at("act_v", [P, 2 * SEQ])
        xn = at("xn", [P, NT, D])

        place[0] = arena
        p_at = arena
        prob = [at(f"prob{i}", [P, 512]) for i in range(QK_RING)]
        pT = [at(f"pT{i}", [P, 512]) for i in range(PT_RING)]
        nmax = at("nmax", [P, QK_RING, 4])
        nmax2 = at("nmax2", [P, QK_RING, 4])
        den = at("den", [P, QK_RING, 4])
        den2 = at("den2", [P, QK_RING, 4])
        rden = at("rden", [P, QK_RING, 4])
        gden = at("gden", [P, QK_RING, 4])
        esink = at("esink", [P, QK_RING, 4])
        zsink = at("zsink", [P, QK_RING, 4])
        ssq = at("ssq", [P, 4, 8])
        ssq2 = at("ssq2", [P, 4, 8])
        srs = at("srs", [P, 4, 8])
        m_at = place[0]
        place[0] = p_at
        nat = [at(f"nat{i}", [P, NT, 256]) for i in range(2)]
        t1 = [at(f"t1_{i}", [P, NT, 256]) for i in range(2)]
        t2 = at("t2", [P, NT, 256])
        qg = at("qg", [P, NT, 256])
        flat_at = place[0]
        flat = at("flat", [P, 2, CS, 30])
        glog = at("glog", [P, NT * 24])
        gden1 = at("gden1", [P, NT * 24])
        kcv = at("kcv", [NCMP, 256])
        lc_n = at("lc_n", [P, 16])
        lc_d = at("lc_d", [P, 16])
        lc_r = at("lc_r", [P, 16])
        assert place[0] <= m_at
        place[0] = flat_at
        hid = at("hid", [P, 2, 2, 30])
        kc2 = at("kc2", [NCMP, P])
        kcd = at("kcd", [NCMP, 256])
        kcT = at("kcT", [P, 2, 16])
        lc = at("lc", [P, NT, 8, 16])
        assert place[0] <= flat_at + 2 * CS * 30 * 4
        place[0] = p_at
        nat1 = [at(f"nat1_{i}", [P, NT, 256]) for i in range(4)]
        sq1 = at("sq1", [P, NT, 4 * 96])
        natm = [at(f"natm{i}", [P, NT, 4 * 96]) for i in range(2)]
        r2 = at("r2", [P, NT, 4 * 32])
        assert place[0] <= m_at

        place[0] = m_at
        qaT = at("qaT", [P, 4, SEQ])
        qrT = at("qrT", [P, 4, SEQ])
        qbT = at("qbT", [P, 4, SEQ])
        k_even = [at(f"k_even{i}", [P, 2, SEQ]) for i in range(3)]
        k_odd = [at(f"k_odd{i}", [P, 2, SEQ], offset=a_at + 8 * SEQ * i) for i in range(3)]
        vN = [at(f"vN{i}", [P, NT, 2 * HD]) for i in range(3)]
        rope_q = [at(f"rope_g{i}", [P, NT, P]) for i in range(5)]
        nsink = at("nsink", [P, 8])
        gate = at("gate", [P, NT * 24])
        gateT = at("gateT", [24, SEQ], offset=a_at + 24 * SEQ)
        pcT = at("pcT", [NCMP, 8, SEQ], offset=h_at)
        place[0] = m_at
        qmT = at("qmT", [96, 8, SEQ])
        kmT = at("kmT", [96, 8, SEQ])
        vf = at("vf", [P, NT, 512])
        negDT = at("negDT", [8, SEQ])
        dnat = at("dnat", [P, NT, 8])
        f_raw = at("f_raw", [P, NT, 8])
        fz = at("fz", [P, 16])
        fa = at("fa", [P, 16])
        fe = at("fe", [P, 16])
        fl = at("fl", [P, 16])
        lf = at("lf", [P, NT, 8])
        vm = at("vm", [P, NT, 8, HD])
        kr = at("kr", [P, NT, 32])
        fgain = at("fgain", [P, HD])
        qfT = at("qfT", [P, 4, SEQ], offset=h_at)
        kf_even = at("kf_even", [P, 4, SEQ], offset=h_at + 4 * SEQ * 4)
        kf_odd = at("kf_odd", [P, 4, SEQ], offset=w_at + (U_M1 + M1_UNITS) % SPLIT * UNIT * 4)
        oB_hi = at("oB_hi", [P, 4, SEQ], F32R, offset=h_at + 8 * SEQ * 4)
        oB_lo = at("oB_lo", [P, 4, SEQ], F32R, offset=h_at + 12 * SEQ * 4)
        oA_hi = at("oA_hi", [P, 4, SEQ], F32R, offset=a_at)
        oA_lo = at("oA_lo", [P, 4, SEQ], F32R, offset=a_at + 4 * SEQ * 4)
        mtab = [at(f"mtab{i}", [P, NT, P], offset=a_at + (4 * i + 3) * SEQ * 4) for i in range(2)]
        a_hi_flat = a_hi[:, :, :, :].rearrange("p a b c -> p (a b c)")
        a_lo_flat = a_lo[:, :, :, :].rearrange("p a b c -> p (a b c)")
        cq_hi, cq_lo = (v[:, 0:512].rearrange("p (c t) -> p c t", c=2) for v in (a_hi_flat, a_lo_flat))
        ckv_hi, ckv_lo = (v[:, 512:768] for v in (a_hi_flat, a_lo_flat))

        ps = ctx.enter_context(nc.psum_tensor("ps", [P, 8, 512], F32))

        x_loaded = [sem(f"x_loaded{t}") for t in range(NT)]
        ident_loaded = sem("ident_loaded")
        par_loaded = sem("par_loaded")
        rows_loaded = sem("rows_loaded")
        raw_loaded = [sem(f"raw_loaded{i}") for i in range(RAW)]
        hi_ready = sem("hi_ready")
        lo_ready = sem("lo_ready")
        pool_split = sem("pool_split")
        unit_done = sem("unit_done")
        x_updated = sem("x_updated")
        sq_done = sem("sq_done")
        rstd_ready = sem("rstd_ready")
        xn_ready = sem("xn_ready")
        xT_ready = sem("xT_ready")
        hhi_ready = sem("hhi_ready")
        hlo_ready = sem("hlo_ready")
        silu_done = sem("silu_done")
        mul_done = sem("mul_done")
        ahi_ready = sem("ahi_ready")
        alo_ready = sem("alo_ready")
        acc_ready = sem("acc_ready")
        out_stored = sem("out_stored")
        const_ready = sem("const_ready")
        cast_ready = sem("cast_ready")
        pool_const = sem("pool_const")
        v_step = sem("v_step")
        g_step = sem("g_step")
        a_step = sem("a_step")
        nat_ready = sem("nat_ready")
        hsq_done = sem("hsq_done")
        hss_done = sem("hss_done")
        hrs_ready = sem("hrs_ready")
        hn_ready = sem("hn_ready")
        rot2_ready = sem("rot2_ready")
        rot_ready = sem("rot_ready")
        hT_done = sem("hT_done")
        hT_ready = sem("hT_ready")
        flat_built = sem("flat_built")
        gateT_ready = sem("gateT_ready")
        gate_done = sem("gate_done")
        hid_ready = sem("hid_ready")
        kcv_done = sem("kcv_done")
        kcv_ready = sem("kcv_ready")
        ksq_done = sem("ksq_done")
        kss_done = sem("kss_done")
        krs_ready = sem("krs_ready")
        kcn_ready = sem("kcn_ready")
        kcT_done = sem("kcT_done")
        kcT_ready = sem("kcT_ready")
        lc_done = sem("lc_done")
        lc_shift = sem("lc_shift")
        lc_exp = sem("lc_exp")
        pc_ready = sem("pc_ready")
        pcT_done = sem("pcT_done")
        pcT_ready = sem("pcT_ready")
        glog_ready = sem("glog_ready")
        gexp_ready = sem("gexp_ready")
        zeros_ready = sem("zeros_ready")
        qk_done = sem("qk_done")
        nmax_ready = sem("nmax_ready")
        esink_ready = sem("esink_ready")
        exp_done = sem("exp_done")
        ps_ready = sem("ps_ready")
        pt_done = sem("pt_done")
        pT_ready = sem("pT_ready")
        pv_done = sem("pv_done")
        ohi_ready = sem("ohi_ready")
        olo_ready = sem("olo_ready")
        cT_done = sem("cT_done")
        chi_ready = sem("chi_ready")
        clo_ready = sem("clo_ready")
        f_abs = sem("f_abs")
        f_ln = sem("f_ln")
        lf_ready = sem("lf_ready")
        dt_done = sem("dt_done")
        dt_ready = sem("dt_ready")
        natm_ready = sem("natm_ready")
        bank_free = sem("bank_free")
        mrot_ready = sem("mrot_ready")
        mT_done = sem("mT_done")
        mT_ready = sem("mT_ready")

        block = ctx.enter_context(nc.Block())

        def row(name):
            c, w = ROWS[name]
            return rows[:, c:c + w]

        def gain_col(norm, c):
            return cols[:, norm * 8 + c:norm * 8 + c + 1]

        def job_heads(j):
            b = j % JOBS
            return j // JOBS, int(b > 0), slice(0, 4) if b == 0 else slice(b - 1, 4, 2)

        def of_heads(sl, g):
            return slice(4 * g + sl.start, 4 * g + 4, sl.step or 1)

        def ends_output(j):
            return OUT_OF.get(j // JOBS) if j % JOBS == JOBS - 1 else None

        def after_mixer(m):
            return (U_FFN[1] if m == NORM_M0 + 1 else U_FFN[3]) + LEAD - 1

        def before(u):
            return u - sum(p < u for p in POOL_UNITS)

        def wait_unit(engine, u, more=0):
            if u in POOL_UNITS:
                engine.wait_ge(pool_split, POOL_UNITS.index(u) + 1)
            else:
                engine.wait_ge(lo_ready, more + (before(u) + 1))

        def o_parts(e):
            if e < 4:
                return h_hi[:, 2 * e:2 * e + 2, :], h_lo[:, 2 * e:2 * e + 2, :]
            hi, lo = (oA_hi, oA_lo) if e < 6 else (oB_hi, oB_lo)
            c = 2 * (e % 2)
            return hi[:, c:c + 2, :], lo[:, c:c + 2, :]

        ffn_names = [("l0_ffn1_", 0), ("l0_ffn2_", 1), ("l1_ffn1_", 2), ("l1_ffn2_", 3)]
        gates = [A[n + "w_gate"].rearrange("(k p) n -> p k n", p=P) for n, _ in ffn_names]
        ups = [A[n + "w_up"].rearrange("(k p) n -> p k n", p=P) for n, _ in ffn_names]
        downs = [A[n + "w_down"].rearrange("(c p) n -> p c n", p=P) for n, _ in ffn_names]

        def down_index(j):
            return 3 * j + 4 if j < NSTEP - 1 else 3 * NSTEP - 1

        def heads4(ap, h, w):
            return ap.rearrange("p t (h d) -> p t h d", d=w)[:, :, 0:h, :]

        @block.sync
        def _(sp):
            xv = A["x"][0, :, :].rearrange("(t p) d -> p t d", p=P)
            for t in range(NT):
                sp.dma_start(x[:, t, :], xv[:, t, :]).then_inc(x_loaded[t], 16)

            def load(u, dst, src, more=0):
                if not isinstance(more, int) or u + more >= RAW:
                    wait_unit(sp, u - RAW, more)
                return sp.dma_start(dst, src)

            def slot(u_static, size, inner):
                return raw[u_static % RAW][:, 0:size].rearrange("p (a b) -> p a b", b=inner)

            def ffn(f):
                u0 = U_FFN[f]

                def gate_up(us, c0, more=0):
                    for n, w in enumerate((gates[f], ups[f])):
                        load(us + n, slot(us + n, UNIT, STEP), w[:, :, bass.ds(c0, STEP)], more).then_inc(raw_loaded[(us + n) % RAW], 16)

                def steps(i):
                    for half in range(2):
                        us = u0 + 2 + 3 * half
                        gate_up(us, (2 * i + 1 + half) * STEP, 6 * i)
                        load(us + 2, slot(us + 2, UNIT, D), downs[f][:, bass.ds((2 * i + half) * 2, 2), :], 6 * i)\
                            .then_inc(raw_loaded[(us + 2) % RAW], 16)

                gate_up(u0, 0)
                if f == 0:
                    steps(0)
                with sp.Fori(int(f == 0), (NSTEP - 1) // 2) as i:
                    steps(i)
                u = u0 + FFN_UNITS - 1
                load(u, slot(u, UNIT, D), downs[f][:, 2 * NSTEP - 2:2 * NSTEP, :]).then_inc(raw_loaded[u % RAW], 16)

            def mixer(u0, w_in, spans, others, w_out, order):
                w = w_in.rearrange("(k p) n -> p k n", p=P)
                parts = [(w[:, :, c:c + n], n) for c, n in spans]
                for n, other in others:
                    parts.insert(n, other)
                wo = w_out.rearrange("(c p) n -> p c n", p=P)
                parts += [(wo[:, 2 * e:2 * e + 2, :], D) for e in order]
                for n, (src, inner) in enumerate(parts):
                    u = u0 + n
                    load(u, slot(u, src.shape[1] * inner, inner), src).then_inc(raw_loaded[u % RAW], 16)

            ffn(0)
            w1k, w1v = (A[n].rearrange("(c p) n -> p c n", p=P) for n in ("l0_cmpk_w1", "l0_cmpv_w1"))
            mixer(U_M0, A["l0_w_in"], M0_COLS,
                  [(M0_EXACT[2 * m + n], (w1[:, 8 * n:8 * n + 8, :], CMPH)) for m, w1 in enumerate((w1k, w1v)) for n in range(2)],
                  A["l0_w_out"], range(4))
            ffn(1)
            ffn(2)
            mixer(U_M1, A["l1_w_in"], M1_COLS,
                  [(3, (A["l1_mla_w_q_b"].rearrange("(c p) n -> p c n", p=P), 768)),
                   (5, (A["l1_mla_w_kv_b"].rearrange("(c p) n -> p c n", p=P), 1024))], A["l1_w_out"], (2, 3, 0, 1))
            ffn(3)
            ov = out[0, :, :].rearrange("(t p) d -> p t d", p=P)
            for i, (t, c0, c1) in enumerate(X_PARTS):
                sp.wait_ge(x_updated, 5 * N_PARTS + i + 1)
                sp.dma_start(ov[:, t, c0:c1], x[:, t, c0:c1]).then_inc(out_stored, 16)
            sp.wait_ge(out_stored, 16 * N_PARTS)

        @block.gpsimd
        def _(pool):
            steps = [0]

            def link(ins):
                steps[0] += 1
                ins.then_inc(g_step, 1)
                pool.wait_ge(g_step, steps[0])

            def norm(m):
                for t in range(NT):
                    pool.wait_ge(sq_done, N_PARTS * m + t + 1)
                    link(nc.gpsimd.tensor_scalar(ms_eps[:, m, t:t + 1], ms[:, m, t:t + 1], 1.0, EPS, ALU.mult, ALU.add))
                    if t == 1:
                        pool.wait_ge(sq_done, N_PARTS * m + 3)
                        link(nc.gpsimd.tensor_tensor(ms_eps[:, m, 1:2], ms_eps[:, m, 1:2], ms[:, m, 2:3], ALU.add))
                    nc.gpsimd.tensor_tensor(rstd[:, m, t:t + 1], ms_eps[:, m, t:t + 1], mhalf[:, 0:1], ALU.pow)\
                        .then_inc(rstd_ready, 1)

            def split(u):
                s = u % RAW
                pool.wait_ge(raw_loaded[s], 16 * (u // RAW) + 16)
                pool.wait_ge(unit_done, u - (SPLIT - 1))
                link(nc.gpsimd.tensor_copy(w_hi[u % SPLIT][:, :], raw[s][:, :]))
                nc.gpsimd.tensor_tensor(w_lo[u % SPLIT][:, :], raw[s][:, :], w_hi[u % SPLIT][:, :].bitcast(F32), ALU.subtract)\
                    .then_inc(pool_split, 1)

            def inverse_rms(dst, tmp, src, width, n, signal, parts=P):
                link(nc.gpsimd.tensor_scalar(tmp[0:parts, 0:n], src[0:parts, 0:n], 1.0 / width, EPS, ALU.mult, ALU.add))
                nc.gpsimd.tensor_tensor(dst[0:parts, 0:n], tmp[0:parts, 0:n], mhalf[0:parts, 0:n], ALU.pow).then_inc(signal, 1)

            zeroed = [0]

            def key_zeros(even, odd):
                for half in (even, odd):
                    zeroed[0] += 1
                    nc.gpsimd.memset(half, 0.0).then_inc(zeros_ready, 1)
                    pool.wait_ge(zeros_ready, zeroed[0])

            def mixer0():
                pool.wait_ge(hlo_ready, DC * (NORM_M0 + 1))
                for i in range(3):
                    key_zeros(k_even[i][HD:P, :, :], k_odd[i][0:HD, :, :])
                for n, (u, bank, h, rope, value) in enumerate(M0_CHAINS):
                    if n == 4:
                        compressed_keys()

                    def inverse():
                        pool.wait_ge(hss_done, n + 1)
                        inverse_rms(srs[:, n % 4, :], ssq2[:, n % 4, :], ssq[:, n % 4, :], HD, NT * h, hrs_ready)

                    if n < 2:
                        inverse()
                        pool.wait_ge(hn_ready, n + 1)
                        if n:
                            pool.wait_ge(rot_ready, n)
                    else:
                        pool.wait_ge(nat_ready, n + 1)
                        pool.wait_ge(rot_ready, 2)
                        pool.wait_ge(hn_ready, n)
                    for half in range(2):
                        a, b = (32 * half, 32 - 32 * half)
                        z = heads4(nat[n % 2][:, :, :], h, HD)[:, :, :, b:b + 32]
                        sine = rope_q[rope][:, :, None, HD + a:HD + a + 32].to_broadcast([P, NT, h, 32])
                        ins = nc.gpsimd.tensor_tensor(heads4(t2[:, :, :], h, HD)[:, :, :, a:a + 32], z, sine, ALU.mult)
                    ins.then_inc(rot2_ready, 1)
                    if n >= 2:
                        inverse()

            def compressed_keys():
                pool.wait_ge(kcv_ready, 1)
                nc.gpsimd.tensor_tensor(kc2[:, :], kcv[:, 0:P], kcv[:, 0:P], ALU.mult).then_inc(ksq_done, 1)
                pool.wait_ge(kss_done, 1)
                inverse_rms(srs[:, 3, :], ssq2[:, 3, :], ssq[:, 3, :], HD, 2, krs_ready, parts=NCMP)

            def mixer1():
                c0 = len(M0_CHAINS)
                m = 0
                for n, (what, part, _) in enumerate(M1_CHAINS):
                    width, cnt = {"cq": (256, 2), "ckv": (P, 2), "q": (HD, 8), "k": (HD, 8), "mq": (96, 8), "mk": (96, 8)}[what]
                    if what in ("mq", "mk"):
                        m += 1
                        pool.wait_ge(natm_ready, m)
                        if m > 1:
                            pool.wait_ge(hn_ready, c0 + m - 1)
                        z4 = heads4(natm[part][:, :, :], 4, 96)
                        for half in range(2):
                            a, b = (16 * half, 16 - 16 * half)
                            sine = mtab[int(what == "mk")][:, :, None, 96 + a:112 + a].to_broadcast([P, NT, 4, 16])
                            ins = nc.gpsimd.tensor_tensor(heads4(r2[:, :, :], 4, 32)[:, :, :, a:a + 16], z4[:, :, :, 64 + b:80 + b], sine, ALU.mult)
                        ins.then_inc(rot2_ready, 1)
                    pool.wait_ge(hss_done, c0 + n + 1)
                    inverse_rms(srs[:, n % 4, :], ssq2[:, n % 4, :], ssq[:, n % 4, :], width, cnt, hrs_ready)

            nc.gpsimd.memset(mhalf[:, :], -0.5).then_inc(pool_const, 1)
            pool.wait_ge(pool_const, 1)
            norm(0)
            norm(1)
            mixer0()
            for n in range(M0_OUT, M0_OUT + M0_POOL):
                split(U_M0 + n)
            norm(2)
            norm(3)
            norm(4)
            mixer1()
            pool.wait_ge(unit_done, U_M1 + M1_OUT)
            pool.wait_ge(hrs_ready, len(M0_CHAINS) + len(M1_CHAINS))
            key_zeros(kf_even[HD:P, :, :], kf_odd[0:HD, :, :])
            for n in range(M1_OUT, M1_OUT + M1_POOL):
                split(U_M1 + n)
            norm(5)

        @block.scalar
        def _(act):
            def split(u, size=UNIT, i=0):
                s = u % RAW
                act.wait_ge(raw_loaded[s], 32 * i + (16 * ((u - s) // RAW) + 16))
                if u >= SPLIT:
                    act.wait_ge(unit_done, 6 * i + (u - (SPLIT - 1)))
                nc.scalar.activation(w_hi[u % SPLIT][:, 0:size], raw[s][:, 0:size], ACT.Copy).then_inc(hi_ready, 1)

            def copy_half(u):
                act.wait_ge(raw_loaded[u % RAW], 16 * (u // RAW) + 16)
                act.wait_ge(unit_done, u - (SPLIT - 1))
                nc.scalar.activation(w_half0[u % SPLIT][:, :], raw[u % RAW][:, 0:UNIT // 2], ACT.Copy).then_inc(hi_ready, 1)

            def split_list(u0, sizes, n):
                if n < len(sizes):
                    split(u0 + n, sizes[n])
                elif u0 + n < U_END:
                    split(u0 + n)

            steps = [0]

            def link(ins):
                steps[0] += 1
                ins.then_inc(a_step, 1)
                act.wait_ge(a_step, steps[0])

            def norm(m):
                for i, (t, c0, c1) in enumerate(X_PARTS):
                    if m == 0:
                        act.wait_ge(x_loaded[t], 16)
                    else:
                        act.wait_ge(x_updated, N_PARTS * (m - 1) + i + 1)
                    nc.scalar.activation(xn[:, t, c0:c1], x[:, t, c0:c1], ACT.Square, scale=D ** -0.5,
                                         accum_out=ms[:, m, i:i + 1]).then_inc(sq_done, 1)
                if m == 0:
                    split(0)
                    act.wait_ge(par_loaded, 16)
                if m in (NORM_M0 + 1, NORM_M1 + 1):
                    split(after_mixer(m))
                for c in range(DC):
                    if c % 2 == 0:
                        act.wait_ge(xT_ready, 4 * m + c // 2 + 1)
                    src = ps[:, T_BANK[m] + c // 2, (c % 2) * SEQ:(c % 2 + 1) * SEQ]
                    nc.scalar.activation(h_hi[:, c, :], src, ACT.Copy, scale=gain_col(m, c)).then_inc(hhi_ready, 1)

            def ffn(f, last):
                u0 = U_FFN[f]

                def step(j, js):
                    def next_split(n):
                        us = u0 + 3 * js + 4 + n
                        if not isinstance(j, int):
                            split(us, i=j)
                        elif us < U_END:
                            split(us)

                    next_split(0)
                    next_split(1)
                    bank = 4 + 2 * (js % 2)
                    up = u0 + (3 * js + 1 if js else 2)
                    done = NSTEP * f + js + 1
                    if not isinstance(j, int):
                        up, done = 6 * j + up, 2 * j + done
                    act.wait_ge(unit_done, up)
                    nc.scalar.activation(sg[:, :].rearrange("p (b n) -> p b n", b=2), ps[:, bank:bank + 2, 0:SEQ],
                                         ACT.Silu).then_inc(silu_done, 1)
                    act.wait_ge(mul_done, done)
                    nc.scalar.activation(a_hi[:, js % 2, :, :].rearrange("p b n -> p (b n)"), act_v[:, :],
                                         ACT.Copy).then_inc(ahi_ready, 1)
                    next_split(2)

                step(0, 0)
                n_loop = (NSTEP - 1) // 2 - (1 if last else 0)
                with act.Fori(0, n_loop) as i:
                    for half in range(2):
                        step(i, 1 + half)
                if last:
                    step(NSTEP - 2, NSTEP - 2)
                    step(NSTEP - 1, NSTEP - 1)

            def att_exp(j):
                a, qt, hs = job_heads(j)
                kind, g = ATT[a]
                s = j % QK_RING
                act.wait_ge(nmax_ready, j + 1)
                if j >= QK_RING:
                    act.wait_ge(pt_done, j - QK_RING + 1)
                n, keys = (4, P) if qt == 0 else (2, SEQ)
                if kind == SWA:
                    nc.scalar.activation(esink[:, s, 0:n], zsink[:, s, 0:n], ACT.Exp).then_inc(esink_ready, 1)
                for i in range(n):
                    ins = nc.scalar.activation(prob[s][:, i * keys:(i + 1) * keys], ps[:, 2 + s, i * keys:(i + 1) * keys], ACT.Exp,
                                               bias=nmax[:, s, i:i + 1], accum_out=den[:, s, i:i + 1])
                ins.then_inc(exp_done, 1)

            def att_evac(j):
                act.wait_ge(pt_done, j + 1)
                if j >= PT_RING:
                    act.wait_ge(pv_done, j - PT_RING + 1)
                nc.scalar.activation(pT[j % PT_RING][:, :], ps[:, 6 + j % T_RING, :], ACT.Copy).then_inc(pT_ready, 1)

            def att_out(j):
                e = ends_output(j)
                if e is not None:
                    act.wait_ge(pv_done, j + 1)
                    nc.scalar.activation(o_parts(e)[0].rearrange("p c t -> p (c t)"), ps[:, e % 2, :], ACT.Copy).then_inc(ohi_ready, 1)

            def attention(a0, a1):
                j0, j1 = JOBS * a0, JOBS * a1
                for j in range(j0, j0 + 3):
                    att_exp(j)
                for j in range(j0, j1):
                    att_evac(j)
                    if j > j0:
                        att_out(j - 1)
                    if j + 3 < j1:
                        att_exp(j + 3)
                att_out(j1 - 1)

            def copy_keys(bank, even, odd):
                nc.scalar.activation(even[0:HD].rearrange("p c t -> p (c t)"), ps[0:HD, bank, :], ACT.Copy)
                nc.scalar.activation(odd[HD:P].rearrange("p c t -> p (c t)"), ps[HD:P, bank, :], ACT.Copy).then_inc(hT_ready, 1)

            def copy_T(job_bank, dst):
                nc.scalar.activation(dst, ps[:, job_bank, :], ACT.Copy).then_inc(hT_ready, 1)

            def mixer0():
                u0 = U_M0
                job_dst = [qrT[:, 0:2, :], qaT[:, 0:2, :], qrT[:, 2:4, :], qaT[:, 2:4, :], 0, 1,
                           qbT[:, 0:2, :], qbT[:, 2:4, :], 2]

                def t_evac(j):
                    act.wait_ge(hT_done, j + 1)
                    if isinstance(job_dst[j], int):
                        copy_keys(5 + j % 2, k_even[job_dst[j]][:, :, :], k_odd[job_dst[j]][:, :, :])
                    else:
                        copy_T(5 + j % 2, job_dst[j].rearrange("p c t -> p (c t)"))

                def rows_out(n):
                    u, bank, h, rope, value = M0_CHAINS[n]
                    act.wait_ge(unit_done, u0 + u + 1)
                    src = ps[:, bank, :].rearrange("p (t n) -> p t n", t=NT)
                    if n >= 2:
                        act.wait_ge(rot_ready, n - 1)
                    ins = nc.scalar.activation(nat[n % 2][:, :, 0:h * HD], src[:, :, 0:h * HD], ACT.Copy)
                    if value is not None:
                        ins = nc.scalar.activation(vN[value][:, :, :], src[:, :, P:2 * P], ACT.Copy)
                    ins.then_inc(nat_ready, 1)
                    act.wait_ge(nat_ready, n + 1)
                    nc.scalar.activation(src[:, :, 0:h * HD], src[:, :, 0:h * HD], ACT.Square).then_inc(hsq_done, 1)

                def w_split(n):
                    if n in M0_EXACT:
                        copy_half(u0 + n)
                    else:
                        split_list(u0, M0_SIZES, n)

                w_split(4)
                w_split(5)
                rows_out(0)
                w_split(6)
                rows_out(1)
                act.wait_ge(unit_done, u0 + 4)
                nc.scalar.activation(gateT[:, :], ps[0:24, 0, 0:SEQ], ACT.Copy).then_inc(gateT_ready, 1)
                t_evac(0)
                t_evac(1)
                w_split(7)
                w_split(8)
                rows_out(2)
                t_evac(2)
                t_evac(3)
                w_split(9)
                w_split(10)
                rows_out(3)
                t_evac(4)
                act.wait_ge(glog_ready, 1)
                nc.scalar.activation(gden1[:, :], glog[:, :], ACT.Exp, scale=-1.0).then_inc(gexp_ready, 1)
                w_split(11)
                act.wait_ge(unit_done, u0 + 10)
                nc.scalar.activation(hid[:, :, :, :].rearrange("p m b n -> p b m n"),
                                     ps[:, 2:4, 0:64].rearrange("p b (m n) -> p b m n", m=2)[:, :, :, 0:30], ACT.Silu).then_inc(hid_ready, 1)
                act.wait_ge(kcv_done, 1)
                nc.scalar.activation(kcv[:, :], ps[0:NCMP, 4, 0:256], ACT.Copy).then_inc(kcv_ready, 1)
                w_split(12)
                rows_out(4)
                t_evac(5)
                act.wait_ge(kcT_done, 1)
                nc.scalar.activation(kcT[:, :, 0:NCMP], ps[:, 7, 0:32].rearrange("p (g c) -> p g c", g=2)[:, :, 0:NCMP],
                                     ACT.Copy).then_inc(kcT_ready, 1)
                rows_out(5)
                act.wait_ge(lc_shift, 1)
                nc.scalar.activation(lc[:, :, :, 0:NCMP].rearrange("p t h c -> p (t h) c"),
                                     lc[:, :, :, 0:NCMP].rearrange("p t h c -> p (t h) c"), ACT.Exp).then_inc(lc_exp, 1)
                t_evac(6)
                rows_out(6)
                t_evac(7)
                for b in range(4):
                    act.wait_ge(pcT_done, b + 1)
                    nc.scalar.activation(pcT[:, 2 * b:2 * b + 2, :].rearrange("p h t -> p (h t)"), ps[0:NCMP, (4, 7)[b % 2], :], ACT.Copy)\
                        .then_inc(pcT_ready, 1)
                t_evac(8)
                attention(A_M0, A_M1)
                for n in range(M0_OUT + M0_POOL, M0_UNITS + LEAD - 1):
                    w_split(n)

            def mixer1():
                u0 = U_M1
                o0 = len(M0_TJOBS)
                c0 = len(M0_CHAINS)

                free = [0]

                def rows_out(n):
                    what, part, u = M1_CHAINS[n]
                    act.wait_ge(unit_done, u0 + u + 1)
                    if what in ("mq", "mk"):
                        z = natm[part]
                        if what == "mk":
                            act.wait_ge(mT_done, part + 1)
                            kv = ps[:, 4 + 2 * part:6 + 2 * part, :].rearrange("p t (h d) -> p t h d", d=P)
                            for t in range(NT):
                                nc.scalar.activation(heads4(z[:, :, :], 4, 96)[:, t, :, 0:HD], kv[:, t, :, 0:HD], ACT.Copy)
                                nc.scalar.activation(heads4(z[:, :, :], 4, 96)[:, t, :, HD:96], kr[:, t, None, :].to_broadcast([P, 4, 32]), ACT.Copy)
                                ins = nc.scalar.activation(vm[:, t, 4 * part:4 * part + 4, :], kv[:, t, :, HD:P], ACT.Copy)
                            src = z[:, :, :]
                        else:
                            src = ps[:, 4 + 2 * part:6 + 2 * part, 0:384]
                            ins = nc.scalar.activation(z[:, :, :], src, ACT.Copy)
                        ins.then_inc(natm_ready, 1)
                        act.wait_ge(natm_ready, 1 + [c for c in M1_CHAINS if c[0] in ("mq", "mk")].index(M1_CHAINS[n]))
                        act.wait_ge(hss_done, c0 + n)
                        nc.scalar.activation(sq1[:, :, :], src, ACT.Square).then_inc(hsq_done, 1)
                        return
                    b = M1_PROJ.index(u) % 2
                    if what == "cq":
                        src = ps[:, 1, :].rearrange("p (t n) -> p t n", t=NT)[:, :, 88:96]
                        nc.scalar.activation(nat1[3][:, :, 248:256], src, ACT.Copy)
                        nc.scalar.activation(sq1[:, :, 248:256], src, ACT.Square).then_inc(hsq_done, 1)
                        return
                    w = P if what == "ckv" else 256
                    at_ = 96 if what == "ckv" else 0
                    src = ps[:, b, :].rearrange("p (t n) -> p t n", t=NT)
                    dst = nat1[{"cq": 3, "ckv": 2, "q": part, "k": 2 + part}[what]]
                    if what == "k":
                        act.wait_ge(cT_done, 2 - part)
                    if what == "ckv":
                        nc.scalar.activation(kr[:, :, :], src[:, :, 224:256], ACT.Copy)
                    free[0] += 1
                    nc.scalar.activation(dst[:, :, 0:w], src[:, :, at_:at_ + w], ACT.Copy).then_inc(bank_free, 1)
                    act.wait_ge(bank_free, free[0])
                    act.wait_ge(hss_done, c0 + n)
                    nc.scalar.activation(sq1[:, :, 0:w], dst[:, :, 0:w], ACT.Square).then_inc(hsq_done, 1)

                def values_out(u):
                    act.wait_ge(unit_done, u0 + u + 1)
                    b = M1_PROJ.index(u) % 2
                    nc.scalar.activation(vf[:, :, (u - 8) * 256:(u - 7) * 256], ps[:, b, :].rearrange("p (t n) -> p t n", t=NT), ACT.Copy)\
                        .then_inc(nat_ready, 1)

                def c_hi(n):
                    act.wait_ge(cT_done, n + 1)
                    if n == 0:
                        c = COLS["l1_mla_q_a_norm"][0]
                        for k in range(2):
                            ins = nc.scalar.activation(cq_hi[:, k, :], ps[:, 2, k * SEQ:(k + 1) * SEQ], ACT.Copy, scale=cols[:, c + k:c + k + 1])
                    else:
                        c = COLS["l1_mla_kv_a_norm"][0]
                        ins = nc.scalar.activation(ckv_hi, ps[:, 3, 0:SEQ], ACT.Copy, scale=cols[:, c:c + 1])
                    ins.then_inc(chi_ready, 1)

                def m_evac(n):
                    act.wait_ge(mT_done, n + 1)
                    dst = (qmT if n < 2 else kmT)[:, 4 * (n % 2):4 * (n % 2) + 4, :]
                    nc.scalar.activation(dst.rearrange("p (b h) t -> p b (h t)", b=2), ps[0:96, 2:4, :], ACT.Copy).then_inc(mT_ready, 1)

                def w_split(n):
                    split_list(u0, M1_SIZES, n)

                w_split(4)
                act.wait_ge(unit_done, u0 + 1)
                src = ps[:, 0, :].rearrange("p (t n) -> p t n", t=NT)
                nc.scalar.activation(nat1[3][:, :, 0:248], src[:, :, 8:256], ACT.Copy)
                nc.scalar.activation(f_raw[:, :, :], src[:, :, 0:8], ACT.Copy)
                nc.scalar.activation(sq1[:, :, 0:248], src[:, :, 8:256], ACT.Square).then_inc(nat_ready, 1)
                w_split(5)
                act.wait_ge(f_abs, 1)
                link(nc.scalar.activation(fe[:, :], fa[:, :], ACT.Exp, scale=-1.0))
                nc.scalar.activation(fl[:, :], fe[:, :], ACT.Ln, bias=1.0).then_inc(f_ln, 1)
                rows_out(0)
                rows_out(1)
                w_split(6)
                c_hi(0)
                c_hi(1)
                rows_out(2)
                w_split(7)
                rows_out(3)
                rows_out(4)
                w_split(8)
                rows_out(5)
                w_split(9)
                rows_out(6)
                m_evac(0)
                rows_out(7)
                m_evac(1)
                rows_out(8)
                rows_out(9)
                m_evac(2)
                values_out(8)
                m_evac(3)
                values_out(9)
                for j in range(4):
                    act.wait_ge(hT_done, o0 + j + 1)
                    c = slice(2 * (j % 2), 2 * (j % 2) + 2)
                    if j < 2:
                        copy_T(FOX_T_BANK[j], qfT[:, c, :].rearrange("p c t -> p (c t)"))
                    else:
                        copy_keys(FOX_T_BANK[j], kf_even[:, c, :], kf_odd[:, c, :])
                attention(A_M1, A_END)
                for n in range(M1_OUT + M1_POOL, M1_UNITS + LEAD - 1):
                    w_split(n)

            act.dma_start(ident, A["shape_tables"][:, T_ID:T_ID + P]).then_inc(ident_loaded, 16)
            act.dma_start(par[:, :], A["columns"]).then_inc(par_loaded, 16)
            norm(0)
            act.dma_start(rows[:, :], A["rows"].partition_broadcast(P)).then_inc(rows_loaded, 16)
            act.dma_start(tab[:, P:T_COLS], A["shape_tables"][:, P:T_COLS]).then_inc(rows_loaded, 16)
            for n in range(1, LEAD):
                split(n)
            act.wait_ge(rows_loaded, 32)
            nc.scalar.activation(id_b[:, :], ident, ACT.Copy)
            nc.scalar.activation(mask0[:, :], tab[:, T_CAUSAL:T_CAUSAL + P], ACT.Copy)
            nc.scalar.activation(mask1[:, P:2 * P], tab[:, T_CAUSAL:T_CAUSAL + P], ACT.Copy)
            nc.scalar.activation(mask1w[:, P:2 * P], tab[:, T_CAUSAL:T_CAUSAL + P], ACT.Copy)
            nc.scalar.activation(mask1w[:, 0:P], tab[:, T_BAND:T_BAND + P], ACT.Copy).then_inc(cast_ready, 1)
            ffn(0, False)
            norm(1)
            mixer0()
            norm(2)
            ffn(1, False)
            norm(3)
            ffn(2, False)
            norm(4)
            mixer1()
            norm(5)
            ffn(3, True)

        @block.vector
        def _(dve):
            steps = [0]

            def link(ins):
                steps[0] += 1
                ins.then_inc(v_step, 1)
                dve.wait_ge(v_step, steps[0])

            def split(us, size=UNIT, more=0):
                dve.wait_ge(hi_ready, more + (before(us) + 1))
                nc.vector.tensor_tensor(w_lo[us % SPLIT][:, 0:size], raw[us % RAW][:, 0:size],
                                        w_hi[us % SPLIT][:, 0:size].bitcast(F32), ALU.subtract).then_inc(lo_ready, 1)

            def copy_half(u):
                dve.wait_ge(hi_ready, before(u) + 1)
                nc.vector.tensor_copy(w_half1[u % SPLIT][:, :], raw[u % RAW][:, UNIT // 2:UNIT]).then_inc(lo_ready, 1)

            def split_list(u0, sizes, n):
                if n < len(sizes):
                    split(u0 + n, sizes[n])
                elif u0 + n < U_END:
                    split(u0 + n)

            def norm_rows(m, t):
                dve.wait_ge(rstd_ready, NT * m + t + 1)
                for tile, c0, c1 in X_PARTS:
                    if tile == t:
                        nc.vector.tensor_scalar(xn[:, t, c0:c1], x[:, t, c0:c1], rstd[:, m, t:t + 1], None, ALU.mult).then_inc(xn_ready, 1)

            def norm(m):
                for c in range(DC):
                    dve.wait_ge(hhi_ready, DC * m + 2 * (c // 2) + 2)
                    src = ps[:, T_BANK[m] + c // 2, (c % 2) * SEQ:(c % 2 + 1) * SEQ]
                    nc.vector.scalar_tensor_tensor(out=h_lo[:, c, :], in0=src, scalar=gain_col(m, c), in1=h_hi[:, c, :].bitcast(F32),
                                                   op0=ALU.mult, op1=ALU.subtract).then_inc(hlo_ready, 1)
                if m in (NORM_M0 + 1, NORM_M1 + 1):
                    split(after_mixer(m))

            def add_to_x(m, bank, scale, last_unit):
                for i, (t, c0, c1) in enumerate(X_PARTS):
                    if i < N_PARTS - 1:
                        dve.wait_ge(acc_ready, (N_PARTS - 1) * m + i + 1)
                    else:
                        dve.wait_ge(unit_done, last_unit + 1)
                    b0, b1 = bank + 2 * t + c0 // 512, bank + 2 * t + c1 // 512
                    nc.vector.scalar_tensor_tensor(out=x[:, t, c0:c1], in0=ps[:, b0:b1, :].rearrange("p b n -> p (b n)"), scalar=scale,
                                                   in1=x[:, t, c0:c1], op0=ALU.mult, op1=ALU.add).then_inc(x_updated, 1)
                    if m < 5 and c1 == D:
                        norm_rows(m + 1, t)

            def ffn(f, last):
                u0 = U_FFN[f]

                def step(j, js):
                    loop = not isinstance(j, int)

                    def next_split(n):
                        us = u0 + 3 * js + 4 + n
                        if loop:
                            split(us, more=6 * j)
                        elif us < U_END:
                            split(us)

                    next_split(0)
                    next_split(1)
                    bank = 4 + 2 * (js % 2)
                    done = NSTEP * f + js + 1
                    if loop:
                        done = 2 * j + done
                    if loop or done > 1:
                        dve.wait_ge(alo_ready, done - 1)
                    dve.wait_ge(silu_done, done)
                    nc.vector.tensor_tensor(act_v[:, :].rearrange("p (b n) -> p b n", b=2), sg[:, :].rearrange("p (b n) -> p b n", b=2),
                                            ps[:, bank:bank + 2, SEQ:2 * SEQ], ALU.mult).then_inc(mul_done, 1)
                    dve.wait_ge(ahi_ready, done)
                    nc.vector.tensor_tensor(a_lo[:, js % 2, :, :].rearrange("p b n -> p (b n)"), act_v[:, :],
                                            a_hi[:, js % 2, :, :].rearrange("p b n -> p (b n)").bitcast(F32),
                                            ALU.subtract).then_inc(alo_ready, 1)
                    next_split(2)

                step(0, 0)
                with dve.Fori(0, (NSTEP - 1) // 2 - (1 if last else 0)) as i:
                    for half in range(2):
                        step(i, 1 + half)
                if last:
                    step(NSTEP - 2, NSTEP - 2)
                    step(NSTEP - 1, NSTEP - 1)
                add_to_x(NORM_FFN[f], 0, 0.5, u0 + FFN_UNITS - 1)

            def att_max(j):
                a, qt, hs = job_heads(j)
                kind, g = ATT[a]
                s = j % QK_RING
                n = 4 if qt == 0 else 2
                dve.wait_ge(qk_done, j + 1)
                if j >= QK_RING:
                    dve.wait_ge(exp_done, j - QK_RING + 1)
                first = nmax2 if kind in (SWA, FOX) else nmax
                ins = nc.vector.tensor_reduce(first[:, s, 0:n], ps[:, 2 + s, :].rearrange("p (h k) -> p h k", h=n), AX.X, ALU.max, negate=True)
                if kind in (SLC, WIN, MLA):
                    ins.then_inc(nmax_ready, 1)
                    return
                link(ins)
                if kind == SWA:
                    sinks = row("l0_swa_sinks")[:, of_heads(hs, g)]
                    link(nc.vector.tensor_tensor(nmax[:, s, 0:n], nmax2[:, s, 0:n], nsink[:, of_heads(hs, g)], ALU.min))
                    nc.vector.tensor_tensor(zsink[:, s, 0:n], nmax[:, s, 0:n], sinks, ALU.add).then_inc(nmax_ready, 1)
                else:
                    dn = dnat[:, qt, of_heads(hs, g)]
                    link(nc.vector.tensor_tensor(nmax2[:, s, 0:n], nmax2[:, s, 0:n], dn, ALU.subtract))
                    nc.vector.tensor_tensor(nmax[:, s, 0:n], nmax2[:, s, 0:n], dn, ALU.add).then_inc(nmax_ready, 1)

            def att_scale(j):
                a, qt, hs = job_heads(j)
                kind, g = ATT[a]
                s = j % QK_RING
                n = 4 if qt == 0 else 2
                dve.wait_ge(exp_done, j + 1)
                d = den
                if kind == SWA:
                    dve.wait_ge(esink_ready, j - 4 * JOBS + 1)
                    link(nc.vector.tensor_tensor(den2[:, s, 0:n], den[:, s, 0:n], esink[:, s, 0:n], ALU.add))
                    d = den2
                link(nc.vector.reciprocal(rden[:, s, 0:n], d[:, s, 0:n]))
                r = rden
                if kind in (SLC, WIN):
                    gv = gate[:, :].rearrange("p (t h b) -> p t h b", t=NT, b=3)[:, qt, of_heads(hs, g), 1 if kind == SLC else 2]
                    link(nc.vector.tensor_tensor(gden[:, s, 0:n], rden[:, s, 0:n], gv, ALU.mult))
                    r = gden
                pr = prob[s][:, :].rearrange("p (h k) -> p h k", h=n)
                nc.vector.tensor_tensor(pr, pr, r[:, s, 0:n, None].to_broadcast([P, n, 512 // n]), ALU.mult).then_inc(ps_ready, 1)

            def att_out(j):
                e = ends_output(j)
                if e is not None:
                    dve.wait_ge(ohi_ready, e + 1)
                    hi, lo = o_parts(e)
                    nc.vector.tensor_tensor(lo.rearrange("p c t -> p (c t)"), ps[:, e % 2, :],
                                            hi.rearrange("p c t -> p (c t)").bitcast(F32), ALU.subtract).then_inc(olo_ready, 1)

            def attention(a0, a1):
                j0, j1 = JOBS * a0, JOBS * a1
                for j in range(j0, j0 + 3):
                    att_max(j)
                for j in range(j0, j1):
                    att_scale(j)
                    if j + 3 < j1:
                        att_max(j + 3)
                    if j > j0 + 1:
                        att_out(j - 2)
                att_out(j1 - 2)
                att_out(j1 - 1)

            def mixer0():
                u0 = U_M0
                dve.wait_ge(rows_loaded, 32)
                link(nc.vector.tensor_scalar(row("l0_nsa_q_norm"), row("l0_nsa_q_norm"), 0.125, None, ALU.mult))
                r64 = tab[:, T_R64:T_R64 + 256].rearrange("p (t c) -> p t c", t=NT)
                for i, (name, scale) in enumerate((("l0_nsa_q_norm", 1.0), ("l0_nsa_ks_norm", 1.0), ("l0_nsa_kw_norm", 1.0),
                                                   ("l0_swa_q_norm", 0.125), ("l0_swa_k_norm", 1.0))):
                    g = row(name)
                    for a, b in ((0, 0), (HD, 32), (HD + 32, 0)):
                        w = HD if a == 0 else 32
                        nc.vector.scalar_tensor_tensor(out=rope_q[i][:, :, a:a + w], in0=g[:, None, b:b + w].to_broadcast([P, NT, w]), scalar=scale,
                                                       in1=r64[:, :, a:a + w], op0=ALU.mult, op1=ALU.mult)
                link(nc.vector.tensor_scalar(nsink[:, :], row("l0_swa_sinks"), -1.0, None, ALU.mult))

                def build_flat():
                    dve.wait_ge(unit_done, u0 + 1)
                    for m, name in enumerate(("l0_cmp_pos_k", "l0_cmp_pos_v")):
                        c0 = COLS[name][0]
                        for g in range(2):
                            tok = ps[g * HD:(g + 1) * HD, 4, m * SEQ:(m + 1) * SEQ].rearrange("p (b j) -> p j b", j=CS)
                            for jj in range(2):
                                for b0 in range(2):
                                    src = tok[:, jj:CS:2, b0:b0 + NCMP]
                                    pos = cols[jj * HD:(jj + 1) * HD, c0 + 8 * b0:c0 + 8 * b0 + 8]
                                    ins = nc.vector.tensor_tensor(flat[jj * HD:(jj + 1) * HD, m, 8 * b0:8 * b0 + 8, g * NCMP:(g + 1) * NCMP],
                                                                  src, pos[:, :, None].to_broadcast([HD, 8, NCMP]), ALU.add)
                    ins.then_inc(flat_built, 1)

                def chain(n):
                    u, bank, h, rope, value = M0_CHAINS[n]
                    w = h * HD
                    dve.wait_ge(hsq_done, n + 1)
                    squares = ps[:, bank, :].rearrange("p (t n) -> p t n", t=NT)
                    nc.vector.tensor_reduce(ssq[:, n % 4, 0:NT * h].rearrange("p (t h) -> p t h", t=NT), heads4(squares, h, HD), AX.X, ALU.add)\
                        .then_inc(hss_done, 1)
                    rs = srs[:, n % 4, 0:NT * h].rearrange("p (t h) -> p t h", t=NT)[:, :, :, None].to_broadcast([P, NT, h, HD])
                    z = heads4(nat[n % 2][:, :, :], h, HD)
                    dst = heads4(t1[n % 2][:, :, :], h, HD)
                    cosine = rope_q[rope][:, :, None, 0:HD].to_broadcast([P, NT, h, HD])
                    if n >= 2:
                        dve.wait_ge(hT_done, {2: 2, 3: 4, 4: 5, 5: 6, 6: 7}[n])
                    if n < 2:
                        dve.wait_ge(hrs_ready, n + 1)
                        nc.vector.tensor_tensor(z, z, rs, ALU.mult).then_inc(hn_ready, 1)
                        dve.wait_ge(hn_ready, n + 1)
                        link(nc.vector.tensor_tensor(dst, z, cosine, ALU.mult))
                        if n == 1:
                            dve.wait_ge(hT_done, 2)
                        link(nc.vector.tensor_tensor(heads4(qg[:, :, :], h, HD), z,
                                                     row("l0_nsa_q_norm")[:, None, None, :].to_broadcast([P, NT, h, HD]), ALU.mult))
                        dve.wait_ge(rot2_ready, n + 1)
                        nc.vector.tensor_tensor(t1[n % 2][:, :, 0:w], t1[n % 2][:, :, 0:w], t2[:, :, 0:w], ALU.add).then_inc(rot_ready, 1)
                        return
                    link(nc.vector.tensor_tensor(dst, z, cosine, ALU.mult))
                    dve.wait_ge(rot2_ready, n + 1)
                    nc.vector.tensor_tensor(t1[n % 2][:, :, 0:w], t1[n % 2][:, :, 0:w], t2[:, :, 0:w], ALU.add).then_inc(hn_ready, 1)
                    dve.wait_ge(hn_ready, n + 1)
                    dve.wait_ge(hrs_ready, n + 1)
                    if h == 4:
                        nc.vector.tensor_tensor(dst, dst, rs, ALU.mult).then_inc(rot_ready, 1)
                        return
                    dve.wait_ge(hT_done, {2: 4, 3: 5, 6: 6}[n])
                    for t in range(NT):
                        twice = dst[:, t, :, None, :].to_broadcast([P, 2, 2, HD])
                        factor = srs[:, n % 4, t * h:(t + 1) * h, None, None].to_broadcast([P, 2, 2, HD])
                        ins = nc.vector.tensor_tensor(qg[:, t, :].rearrange("p (g two d) -> p g two d", g=2, two=2), twice, factor, ALU.mult)
                    ins.then_inc(rot_ready, 1)

                def compressed_keys():
                    dve.wait_ge(ksq_done, 1)
                    nc.vector.tensor_reduce(ssq[0:NCMP, 3, 0:2], kc2[:, :].rearrange("p (g d) -> p g d", g=2), AX.X, ALU.add).then_inc(kss_done, 1)
                    dve.wait_ge(krs_ready, 1)
                    kn = kcv[:, 0:P].rearrange("p (g d) -> p g d", g=2)
                    link(nc.vector.tensor_tensor(kn, kn, srs[0:NCMP, 3, 0:2, None].to_broadcast([NCMP, 2, HD]), ALU.mult))
                    c = ROWS["l0_nsa_kc_norm"][0]
                    nc.vector.tensor_tensor(kcd[:, :].rearrange("p (g two d) -> p g two d", g=2, two=2),
                                            kn[:, :, None, :].to_broadcast([NCMP, 2, 2, HD]),
                                            rows[0:NCMP, None, None, c:c + HD].to_broadcast([NCMP, 2, 2, HD]), ALU.mult).then_inc(kcn_ready, 1)

                lc4 = lc[:, :, :, 0:NCMP]
                lc3 = lc4.rearrange("p t h c -> p (t h) c")

                def block_table(c0, heads):
                    return tab[:, c0:c0 + 30].rearrange("p (t c) -> p t c", t=NT)[:, :, None, :].to_broadcast([P, NT, heads, NCMP])

                def compressed_shift():
                    dve.wait_ge(lc_done, 1)
                    for par, bank in enumerate((4, 7)):
                        sc = ps[:, bank, 0:128].rearrange("p (t h c) -> p t h c", t=NT, h=4)[:, :, :, 0:NCMP]
                        link(nc.vector.tensor_tensor(lc4[:, :, par:8:2, :], sc, block_table(T_CNEG, 4), ALU.add))
                    link(nc.vector.tensor_reduce(lc_n[:, :], lc3, AX.X, ALU.max, negate=True))
                    nc.vector.tensor_tensor(lc3, lc3, lc_n[:, :, None].to_broadcast([P, 16, NCMP]), ALU.add).then_inc(lc_shift, 1)

                def compressed_probabilities():
                    dve.wait_ge(lc_exp, 1)
                    link(nc.vector.tensor_tensor(lc4, lc4, block_table(T_C01, 8), ALU.mult))
                    link(nc.vector.tensor_reduce(lc_d[:, :], lc3, AX.X, ALU.add))
                    link(nc.vector.tensor_scalar(lc_d[:, :], lc_d[:, :], 1e-30, None, ALU.max))
                    link(nc.vector.reciprocal(lc_r[:, :], lc_d[:, :]))
                    g0 = gate[:, :].rearrange("p (t h b) -> p (t h) b", t=NT, b=3)[:, :, 0]
                    link(nc.vector.tensor_tensor(lc_r[:, :], lc_r[:, :], g0, ALU.mult))
                    nc.vector.tensor_tensor(lc3, lc3, lc_r[:, :, None].to_broadcast([P, 16, NCMP]), ALU.mult).then_inc(pc_ready, 1)

                def w_split(n):
                    if n in M0_EXACT:
                        copy_half(u0 + n)
                    else:
                        split_list(u0, M0_SIZES, n)

                w_split(4)
                build_flat()
                w_split(5)
                chain(0)
                w_split(6)
                chain(1)
                w_split(7)
                dve.wait_ge(gate_done, 1)
                gb = row("l0_nsa_gate_b")[:, None, :].to_broadcast([P, NT, 24])
                nc.vector.tensor_tensor(glog[:, :].rearrange("p (t c) -> p t c", t=NT),
                                        ps[:, 0, SEQ:SEQ + 48].rearrange("p (t n) -> p t n", t=NT), gb, ALU.add).then_inc(glog_ready, 1)
                w_split(8)
                chain(2)
                w_split(9)
                w_split(10)
                chain(3)
                dve.wait_ge(gexp_ready, 1)
                link(nc.vector.tensor_scalar(gden1[:, :], gden1[:, :], 1.0, None, ALU.add))
                link(nc.vector.reciprocal(gate[:, :], gden1[:, :]))
                w_split(11)
                compressed_keys()
                w_split(12)
                chain(4)
                compressed_shift()
                chain(5)
                compressed_probabilities()
                chain(6)
                attention(A_M0, A_M1)
                for n in range(M0_OUT + M0_POOL, M0_UNITS + LEAD - 1):
                    w_split(n)
                add_to_x(NORM_M0, 4, 1.0, u0 + M0_UNITS - 1)

            def mixer1():
                u0 = U_M1
                c0 = len(M0_CHAINS)
                nc.vector.tensor_scalar(fgain[:, :], row("l1_fox_q_norm"), 0.125, None, ALU.mult)
                r32 = tab[:, T_R32:T_R32 + 128].rearrange("p (t c) -> p t c", t=NT)
                for i, (name, scale) in enumerate((("l1_mla_q_norm", 96.0 ** -0.5), ("l1_mla_k_norm", 1.0))):
                    g = row(name)
                    ins = nc.vector.tensor_scalar(mtab[i][:, :, 0:HD], g[:, None, 0:HD].to_broadcast([P, NT, HD]), scale, None, ALU.mult)
                    for a, b, w, r in ((HD, HD, 32, 0), (96, HD + 16, 16, 32), (112, HD, 16, 48)):
                        ins = nc.vector.scalar_tensor_tensor(out=mtab[i][:, :, a:a + w], in0=g[:, None, b:b + w].to_broadcast([P, NT, w]), scalar=scale,
                                                             in1=r32[:, :, r:r + w], op0=ALU.mult, op1=ALU.mult)
                link(ins)

                def chain_rows(n):
                    what, part, _ = M1_CHAINS[n]
                    return (natm[part] if what in ("mq", "mk") else nat1[{"cq": 3, "ckv": 2, "q": part, "k": 2 + part}[what]])

                def sums(n):
                    what, part, _ = M1_CHAINS[n]
                    dve.wait_ge(hsq_done, c0 + n + 1)
                    if what in ("cq", "ckv"):
                        w = 256 if what == "cq" else P
                        dst, src = ssq[:, n % 4, 0:NT], sq1[:, :, 0:w]
                    else:
                        w = 96 if what in ("mq", "mk") else HD
                        dst, src = ssq[:, n % 4, :].rearrange("p (t h) -> p t h", t=NT), heads4(sq1[:, :, 0:4 * w], 4, w)
                    nc.vector.tensor_reduce(dst, src, AX.X, ALU.add).then_inc(hss_done, 1)

                def scaled(n):
                    what, part, _ = M1_CHAINS[n]
                    dve.wait_ge(hrs_ready, c0 + n + 1)
                    if what in ("cq", "ckv"):
                        w = 256 if what == "cq" else P
                        z = chain_rows(n)[:, :, 0:w]
                        nc.vector.tensor_tensor(z, z, srs[:, n % 4, 0:NT, None].to_broadcast([P, NT, w]), ALU.mult).then_inc(rot_ready, 1)
                        return
                    w = 96 if what in ("mq", "mk") else HD
                    z = heads4(chain_rows(n)[:, :, :], 4, w)
                    rs = srs[:, n % 4, :].rearrange("p (t h) -> p t h", t=NT)[:, :, :, None].to_broadcast([P, NT, 4, w])
                    ins = nc.vector.tensor_tensor(z, z, rs, ALU.mult)
                    if w == 96:
                        ins.then_inc(mrot_ready, 1)
                        return
                    link(ins)
                    g = fgain[:, :] if what == "q" else row("l1_fox_k_norm")
                    nc.vector.tensor_tensor(z, z, g[:, None, None, :].to_broadcast([P, NT, 4, HD]), ALU.mult).then_inc(rot_ready, 1)

                def rotated(n, m):
                    what, part, _ = M1_CHAINS[n]
                    z = heads4(natm[part][:, :, :], 4, 96)
                    dve.wait_ge(rot2_ready, c0 + m + 1)
                    link(nc.vector.tensor_tensor(z, z, mtab[int(what == "mk")][:, :, None, 0:96].to_broadcast([P, NT, 4, 96]), ALU.mult))
                    nc.vector.tensor_tensor(z[:, :, :, HD:96], z[:, :, :, HD:96], heads4(r2[:, :, :], 4, 32), ALU.add).then_inc(hn_ready, 1)
                    dve.wait_ge(hn_ready, c0 + m + 1)

                def c_lo(n):
                    dve.wait_ge(chi_ready, n + 1)
                    if n == 0:
                        cc = COLS["l1_mla_q_a_norm"][0]
                        for k in range(2):
                            ins = nc.vector.scalar_tensor_tensor(out=cq_lo[:, k, :], in0=ps[:, 2, k * SEQ:(k + 1) * SEQ], scalar=cols[:, cc + k:cc + k + 1],
                                                                 in1=cq_hi[:, k, :].bitcast(F32), op0=ALU.mult, op1=ALU.subtract)
                    else:
                        cc = COLS["l1_mla_kv_a_norm"][0]
                        ins = nc.vector.scalar_tensor_tensor(out=ckv_lo, in0=ps[:, 3, 0:SEQ], scalar=cols[:, cc:cc + 1],
                                                             in1=ckv_hi.bitcast(F32), op0=ALU.mult, op1=ALU.subtract)
                    ins.then_inc(clo_ready, 1)

                def w_split(n):
                    split_list(u0, M1_SIZES, n)

                w_split(4)
                dve.wait_ge(nat_ready, c0 + 1)
                fb = row("l1_fox_f_bias")[:, None, :].to_broadcast([P, NT, 8])
                link(nc.vector.tensor_tensor(fz[:, :].rearrange("p (t h) -> p t h", t=NT), f_raw[:, :, :], fb, ALU.add))
                nc.vector.scalar_tensor_tensor(out=fa[:, :], in0=fz[:, :], scalar=-1.0, in1=fz[:, :], op0=ALU.mult, op1=ALU.max).then_inc(f_abs, 1)
                w_split(5)
                dve.wait_ge(f_ln, 1)
                nc.vector.scalar_tensor_tensor(out=lf[:, :, :].rearrange("p t h -> p (t h)"), in0=fz[:, :], scalar=0.0, in1=fl[:, :],
                                               op0=ALU.min, op1=ALU.subtract).then_inc(lf_ready, 1)
                sums(0)
                scaled(0)
                sums(1)
                scaled(1)
                c_lo(0)
                w_split(6)
                c_lo(1)
                sums(2)
                scaled(2)
                w_split(7)
                sums(3)
                rotated(3, 0)
                scaled(3)
                sums(4)
                rotated(4, 1)
                w_split(8)
                scaled(4)
                sums(5)
                w_split(9)
                scaled(5)
                sums(6)
                rotated(6, 2)
                scaled(6)
                sums(7)
                scaled(7)
                sums(8)
                rotated(8, 3)
                scaled(8)
                sums(9)
                scaled(9)
                dve.wait_ge(dt_done, 1)
                nc.vector.tensor_scalar(negDT[:, :], ps[0:8, 0, 0:SEQ], -1.0, None, ALU.mult)
                nc.vector.tensor_copy(dnat[:, :, :].rearrange("p t h -> p (t h)"), ps[:, 0, SEQ:SEQ + 16]).then_inc(dt_ready, 1)
                attention(A_M1, A_END)
                for n in range(M1_OUT + M1_POOL, M1_UNITS + LEAD - 1):
                    w_split(n)
                add_to_x(NORM_M1, 4, 1.0, u0 + M1_UNITS - 1)

            nc.vector.memset(zero_b[:, :], 0.0)
            nc.vector.memset(mask1[:, 0:P], 0.0).then_inc(const_ready, 1)
            for t in range(NT):
                norm_rows(0, t)
            split(0)
            norm(0)
            for n in range(1, LEAD):
                split(n)
            ffn(0, False)
            norm(1)
            mixer0()
            norm(2)
            ffn(1, False)
            norm(3)
            ffn(2, False)
            norm(4)
            mixer1()
            norm(5)
            ffn(3, True)

        @block.tensor
        def _(pe):
            def passes(dst, lhs, rhs, start, stop):
                nc.tensor.matmul(dst, lhs[0], rhs[0], start=start, stop=False)
                nc.tensor.matmul(dst, lhs[0], rhs[1], start=False, stop=False)
                return nc.tensor.matmul(dst, lhs[1], rhs[0], start=False, stop=stop)

            def wslot(us, size, inner):
                return tuple(w[us % SPLIT][:, 0:size].rearrange("p (a b) -> p a b", b=inner) for w in (w_hi, w_lo))

            def norm(m):
                for i, (t, c0, c1) in enumerate(X_PARTS):
                    pe.wait_ge(xn_ready, N_PARTS * m + i + 1)
                    for q in range(c0 // (2 * P), c1 // (2 * P)):
                        for c in range(2):
                            ins = nc.tensor.transpose(ps[:, T_BANK[m] + q, c * SEQ + t * P:c * SEQ + (t + 1) * P],
                                                      xn[:, t, (2 * q + c) * P:(2 * q + c + 1) * P], ident)
                        if t == NT - 1:
                            ins.then_inc(xT_ready, 1)

            def down_tile(us, lhs, bank, t, start=False, stop=False):
                w = wslot(us, UNIT, D)
                for half in range(2):
                    for c in range(2):
                        ins = passes(ps[:, bank + 2 * t + half, :], tuple(v[:, c, t * P:(t + 1) * P] for v in lhs),
                                     tuple(v[:, c, half * 512:(half + 1) * 512] for v in w),
                                     start and c == 0, stop and c == 1)
                    if stop and (t, half) in ((0, 1), (1, 0)):
                        ins.then_inc(acc_ready, 1)
                return ins

            def down(us, lhs, bank, start=False):
                down_tile(us, lhs, bank, 0, start)
                down_tile(us, lhs, bank, 1, start).then_inc(unit_done, 1)

            def down_last(us, lhs_a, lhs_b, bank, before_b):
                wait_unit(pe, us)
                down_tile(us, lhs_a, bank, 0)
                wait_unit(pe, us + 1)
                before_b()
                down_tile(us + 1, lhs_b, bank, 0, stop=True)
                down_tile(us, lhs_a, bank, 1).then_inc(unit_done, 1)
                down_tile(us + 1, lhs_b, bank, 1, stop=True).then_inc(unit_done, 1)

            def ffn(f):
                u0 = U_FFN[f]
                m = NORM_FFN[f]

                def gate_up(j, js):
                    bank = 4 + 2 * (js % 2)
                    u = u0 + (3 * js - 1 if js else 0)
                    loop = not isinstance(j, int)
                    if loop:
                        pe.wait_ge(mul_done, 2 * j + (NSTEP * f + js - 1))
                    elif js > 1:
                        pe.wait_ge(mul_done, NSTEP * f + js - 1)
                    for n in range(2):
                        us = u + n
                        wait_unit(pe, us, 6 * j if loop else 0)
                        w = wslot(us, UNIT, STEP)
                        for b in range(2):
                            for k in range(DC):
                                if js == 0 and n == 0:
                                    pe.wait_ge(hlo_ready, DC * m + max(k + 1, 2 * b + 2))
                                ins = passes(ps[:, bank + b, n * SEQ:(n + 1) * SEQ], tuple(v[:, k, b * P:(b + 1) * P] for v in w),
                                             (h_hi[:, k, :], h_lo[:, k, :]), k == 0, k == DC - 1)
                        ins.then_inc(unit_done, 1)

                def activations(js):
                    return a_hi[:, js % 2, :, :], a_lo[:, js % 2, :, :]

                def down_step(j, js):
                    us = u0 + down_index(js)
                    loop = not isinstance(j, int)
                    wait_unit(pe, us, 6 * j if loop else 0)
                    pe.wait_ge(alo_ready, (2 * j if loop else 0) + (NSTEP * f + js + 1))
                    down(us, activations(js), 0)

                gate_up(0, 0)
                for b in range(4):
                    nc.tensor.matmul(ps[:, b, :], zero_b[:, :], zero_b[:, 0:1].to_broadcast([P, 512]), start=True, stop=False)
                if f == 0:
                    for js in (1, 2):
                        gate_up(js, js)
                        down_step(js - 1, js - 1)
                with pe.Fori(int(f == 0), (NSTEP - 3) // 2) as i:
                    for half in range(2):
                        gate_up(i, 1 + half)
                        down_step(i, half)
                gate_up(NSTEP - 2, NSTEP - 2)
                down_step(NSTEP - 3, NSTEP - 3)
                gate_up(NSTEP - 1, NSTEP - 1)
                pe.wait_ge(alo_ready, NSTEP * f + NSTEP - 1)
                down_last(u0 + down_index(NSTEP - 2), activations(NSTEP - 2), activations(NSTEP - 1), 0,
                          lambda: pe.wait_ge(alo_ready, NSTEP * (f + 1)))

            def att_qk(j):
                a, qt, hs = job_heads(j)
                kind, g = ATT[a]
                if j >= QK_RING:
                    pe.wait_ge(exp_done, j - QK_RING + 1)
                mk = mask0 if qt == 0 else mask1w if kind == SWA else mask1
                n = 4 if qt == 0 else 2
                keys = P * (qt + 1)
                nc.tensor.matmul(ps[:, 2 + j % QK_RING, :], id_b[:, :], mk[:, None, :].to_broadcast([P, n, 512 // n]), start=True, stop=False)
                for n, i in enumerate(range(4)[hs]):
                    h = 4 * g + i
                    dst = ps[:, 2 + j % QK_RING, n * keys:(n + 1) * keys]
                    if kind == MLA:
                        q, k = qmT[:, h, qt * P:(qt + 1) * P], kmT[:, h, 0:keys]
                    elif kind == FOX:
                        q, k = qfT[:, h // 2, qt * P:(qt + 1) * P], (kf_even, kf_odd)[h % 2][:, h // 2, 0:keys]
                    else:
                        q = (qbT if kind == SWA else qrT)[:, h // 2, qt * P:(qt + 1) * P]
                        k = (k_even, k_odd)[h % 2][{SLC: 0, WIN: 1, SWA: 2}[kind]][:, g, 0:keys]
                    if kind == FOX:
                        nc.tensor.matmul(dst, ident[0:8, h:h + 1].to_broadcast([8, P]), negDT[:, 0:keys], start=False, stop=False)
                    ins = nc.tensor.matmul(dst, q, k, start=False, stop=i == range(4)[hs][-1])
                ins.then_inc(qk_done, 1)

            def att_pT(j):
                pe.wait_ge(ps_ready, j + 1)
                if j >= T_RING:
                    pe.wait_ge(pT_ready, j - T_RING + 1)
                for c in range(4):
                    ins = nc.tensor.transpose(ps[:, 6 + j % T_RING, c * P:(c + 1) * P], prob[j % QK_RING][:, c * P:(c + 1) * P], ident)
                ins.then_inc(pt_done, 1)

            def att_pv(j):
                a, qt, hs = job_heads(j)
                kind, g = ATT[a]
                pe.wait_ge(pT_ready, j + 1)
                if a in (4, 5, 8, 9) and j % JOBS == 0:
                    pe.wait_ge(olo_ready, a - 3)
                bank = ps[:, g, :].rearrange("p (c t) -> p c t", c=2)
                pt = pT[j % PT_RING][:, :].rearrange("p (h q) -> p h q", h=4) if qt == 0 else \
                    pT[j % PT_RING][:, :].rearrange("p (h k q) -> p k h q", h=2, k=2)
                fresh = kind in (SWA, FOX, MLA)
                if kind in (SLC, WIN, SWA):
                    v = vN[{SLC: 0, WIN: 1, SWA: 2}[kind]]
                    if qt == 0:
                        for par in range(2):
                            r = slice(par * HD, (par + 1) * HD)
                            ins = nc.tensor.matmul(bank[r, :, 0:P], v[:, 0, g * HD:(g + 1) * HD], pt[:, par:4:2, :], start=fresh, stop=fresh)
                    else:
                        r = slice(hs.start * HD, (hs.start + 1) * HD)
                        for kc in range(2):
                            ins = nc.tensor.matmul(bank[r, :, P:SEQ], v[:, kc, g * HD:(g + 1) * HD], pt[:, kc, :, :], start=fresh and kc == 0,
                                                   stop=kind != SLC and kc == 1)
                else:
                    for n, i in enumerate(range(4)[hs]):
                        h = 4 * g + i
                        r = slice((h % 2) * HD, (h % 2 + 1) * HD)
                        for kc in range(qt + 1):
                            v = vf[:, kc, h * HD:(h + 1) * HD] if kind == FOX else vm[:, kc, h, :]
                            ins = nc.tensor.matmul(bank[r, i // 2, qt * P:(qt + 1) * P], v, pt[:, n, :] if qt == 0 else pt[:, kc, n, :],
                                                   start=kc == 0, stop=kc == qt)
                ins.then_inc(pv_done, 1)

            def attention(a0, a1, before_last, before_loop=None):
                j0, j1 = JOBS * a0, JOBS * a1
                for j in range(j0, j0 + 3):
                    att_qk(j)
                if before_loop:
                    before_loop()
                for j in range(j0, j1):
                    if j + 3 < j1:
                        att_qk(j + 3)
                    if j == j1 - 1:
                        before_last()
                    att_pT(j)
                    if j > j0:
                        att_pv(j - 1)
                att_pv(j1 - 1)

            def project(u0, n, width, bank, between=None):
                us = u0 + n
                wait_unit(pe, us)
                w = wslot(us, DC * width, width)
                for t in range(NT):
                    if t and between:
                        between()
                    for k in range(DC):
                        if us == U_M1 and t == 0:
                            pe.wait_ge(hlo_ready, DC * NORM_M1 + k + 1)
                        ins = passes(ps[:, bank, t * 256:t * 256 + width], tuple(v[:, k, t * P:(t + 1) * P] for v in (h_hi, h_lo)),
                                     tuple(v[:, k, :] for v in w), k == 0, k == DC - 1)
                ins.then_inc(unit_done, 1)

            def out_proj_first(us, e0, part, last_job):
                wait_unit(pe, us)
                pe.wait_ge(olo_ready, e0 + 1)
                pe.wait_ge(exp_done, last_job - 1)
                down_tile(us, part, 4, 0, start=True)

            def out_proj(us, e0, parts):
                down_tile(us, parts(0), 4, 1, start=True).then_inc(unit_done, 1)
                wait_unit(pe, us + 1)
                pe.wait_ge(olo_ready, e0 + 2)
                down(us + 1, parts(1), 4)
                pe.wait_ge(olo_ready, e0 + 4)
                down_last(us + 2, parts(2), parts(3), 4, lambda: None)

            def mixer0():
                u0 = U_M0

                def tjob(j):
                    n, what = M0_TJOBS[j]
                    pe.wait_ge(rot_ready, n + 1)
                    if j >= 2:
                        pe.wait_ge(hT_ready, j - 1)
                    src = t1[n % 2] if what == "rot" and M0_CHAINS[n][2] == 4 else qg
                    for c in range(2):
                        for t in range(NT):
                            ins = nc.tensor.transpose(ps[:, 5 + j % 2, c * SEQ + t * P:c * SEQ + (t + 1) * P],
                                                      src[:, t, c * P:(c + 1) * P], ident)
                    ins.then_inc(hT_done, 1)

                def proj(u, between=None):
                    if u == 5:
                        pe.wait_ge(hss_done, 2)
                    if u == 7:
                        pe.wait_ge(glog_ready, 1)
                    if u == 10:
                        pe.wait_ge(hid_ready, 1)
                    if u == 12:
                        pe.wait_ge(hss_done, 3)
                    bank = [c[1] for c in M0_CHAINS if c[0] == u][0]
                    project(u0, u, M0_COLS[M0_PROJ.index(u)][1], bank, between)

                def hidden(u):
                    m, n = divmod(M0_EXACT.index(u), 2)
                    pe.wait_ge(flat_built, 1)
                    wait_unit(pe, u0 + u)
                    w = tuple(v[(u0 + u) % SPLIT][:, :].rearrange("p (c n) -> p c n", n=CMPH) for v in (w_half0, w_half1))
                    for half in range(2):
                        for c in range(8):
                            ins = nc.tensor.matmul(ps[:, 2 + half, m * 32:m * 32 + 30], w[c // 4][:, c % 4, half * P:(half + 1) * P],
                                                   flat[:, m, 8 * n + c, :], start=n == 0 and c == 0, stop=n == 1 and c == 7)
                    ins.then_inc(unit_done, 1)

                pe.wait_ge(cast_ready, 1)
                wait_unit(pe, u0 + 0)
                w = wslot(u0, UNIT, 256)
                for m in range(2):
                    for k in range(DC):
                        pe.wait_ge(hlo_ready, DC * NORM_M0 + max(k + 1, 2))
                        ins = passes(ps[:, 4, m * SEQ:(m + 1) * SEQ], tuple(v[:, k, m * P:(m + 1) * P] for v in w),
                                     (h_hi[:, k, :], h_lo[:, k, :]), k == 0, k == DC - 1)
                ins.then_inc(unit_done, 1)
                proj(1)
                proj(2)
                pe.wait_ge(hss_done, 1)
                wait_unit(pe, u0 + 3)
                w = wslot(u0 + 3, DC * P, P)
                for k in range(DC):
                    ins = passes(ps[:, 0, 0:SEQ], tuple(v[:, k, :] for v in w), (h_hi[:, k, :], h_lo[:, k, :]), k == 0, k == DC - 1)
                ins.then_inc(unit_done, 1)
                tjob(0)
                tjob(1)
                pe.wait_ge(gateT_ready, 1)
                for t in range(NT):
                    ins = nc.tensor.transpose(ps[:, 0, SEQ + 24 * t:SEQ + 24 * (t + 1)], gateT[:, t * P:(t + 1) * P], ident[0:24, 0:24])
                ins.then_inc(gate_done, 1)
                proj(5, lambda: hidden(4))
                tjob(2)
                tjob(3)
                proj(7, lambda: hidden(6))
                tjob(4)
                hidden(8)
                hidden(9)
                pe.wait_ge(hid_ready, 1)
                for m in range(2):
                    for g in range(2):
                        for half in range(2):
                            ins = nc.tensor.matmul(ps[0:NCMP, 4, m * P + g * HD:m * P + (g + 1) * HD], hid[:, m, half, g * NCMP:(g + 1) * NCMP],
                                                   w2[:, m, half, :], start=half == 0, stop=half == 1)
                ins.then_inc(kcv_done, 1)
                proj(10)
                tjob(5)
                pe.wait_ge(kcn_ready, 1)
                for g in range(2):
                    ins = nc.tensor.transpose(ps[:, 7, g * 16:g * 16 + NCMP], kcd[:, g * P:(g + 1) * P], ident[0:NCMP, 0:NCMP])
                ins.then_inc(kcT_done, 1)

                def compressed_scores():
                    pe.wait_ge(kcT_ready, 1)
                    pe.wait_ge(hT_ready, 4)
                    for t in range(NT):
                        for h in range(8):
                            r = slice((h % 2) * HD, (h % 2 + 1) * HD)
                            c = (t * 4 + h // 2) * 16
                            ins = nc.tensor.matmul(ps[:, (4, 7)[h % 2], c:c + NCMP], qaT[r, h // 2, t * P:(t + 1) * P],
                                                   kcT[r, h // 4, 0:NCMP], start=True, stop=True)
                    ins.then_inc(lc_done, 1)

                proj(11, compressed_scores)
                tjob(6)
                proj(12)
                tjob(7)
                pe.wait_ge(pc_ready, 1)
                for b in range(4):
                    if b >= 2:
                        pe.wait_ge(pcT_ready, b - 1)
                    for h in (2 * b, 2 * b + 1):
                        for t in range(NT):
                            ins = nc.tensor.transpose(ps[0:NCMP, (4, 7)[b % 2], (h % 2) * SEQ + t * P:(h % 2) * SEQ + (t + 1) * P],
                                                      lc[:, t, h, 0:NCMP], ident)
                    ins.then_inc(pcT_done, 1)

                def compressed_values():
                    tjob(8)
                    pe.wait_ge(hss_done, len(M0_CHAINS))
                    pe.wait_ge(pcT_ready, 4)
                    for g in range(2):
                        for par in range(2):
                            nc.tensor.matmul(ps[par * HD:(par + 1) * HD, g, :].rearrange("p (c t) -> p c t", c=2), kcv[:, P + g * HD:P + (g + 1) * HD],
                                             pcT[:, 4 * g + par:4 * g + 4:2, :], start=True, stop=False)
                    pe.wait_ge(hT_ready, len(M0_TJOBS))

                compressed_values()
                pe.wait_ge(zeros_ready, 6)
                attention(A_M0, A_M1, lambda: out_proj_first(u0 + M0_OUT, 0, o_parts(0), JOBS * A_M1 - 1))
                out_proj(u0 + M0_OUT, 0, o_parts)

            def mixer1():
                u0 = U_M1
                c0 = len(M0_CHAINS)
                o0 = len(M0_TJOBS)

                def proj(u, between=None):
                    i = M1_PROJ.index(u)
                    if u == 2:
                        pe.wait_ge(nat_ready, c0 + 1)
                    elif i >= 2:
                        pe.wait_ge(bank_free, i - 2)
                    project(u0, u, M1_COLS[i][1], i % 2, between)

                def c_T(n):
                    pe.wait_ge(rot_ready, c0 + n + 1)
                    for c in range(2 - n):
                        for t in range(NT):
                            ins = nc.tensor.transpose(ps[:, 2 + n, c * SEQ + t * P:c * SEQ + (t + 1) * P], nat1[3 - n][:, t, c * P:(c + 1) * P], ident)
                    ins.then_inc(cT_done, 1)

                def m_T(n):
                    pe.wait_ge(mrot_ready, n + 1)
                    if n:
                        pe.wait_ge(mT_ready, n)
                    for h in range(4):
                        for t in range(NT):
                            ins = nc.tensor.transpose(ps[0:96, 2 + h // 2, (h % 2) * SEQ + t * P:(h % 2) * SEQ + (t + 1) * P],
                                                      natm[n % 2][:, t, h * 96:(h + 1) * 96], ident)
                    ins.then_inc(mT_done, 1)

                proj(0)
                proj(1)
                proj(2, lambda: c_T(0))
                c_T(1)
                pe.wait_ge(clo_ready, 1)
                wait_unit(pe, u0 + 3)
                w = wslot(u0 + 3, 1536, 768)
                for half in range(2):
                    for t in range(NT):
                        for c in range(2):
                            ins = passes(ps[:, 4 + 2 * half + t, 0:384], tuple(v[:, c, t * P:(t + 1) * P] for v in (cq_hi, cq_lo)),
                                         tuple(v[:, c, half * 384:(half + 1) * 384] for v in w), c == 0, c == 1)
                ins.then_inc(unit_done, 1)
                proj(4)
                pe.wait_ge(clo_ready, 2)
                pe.wait_ge(hsq_done, c0 + 5)
                wait_unit(pe, u0 + 5)
                w = wslot(u0 + 5, 1024, 1024)
                for half in range(2):
                    for t in range(NT):
                        ins = passes(ps[:, 4 + 2 * half + t, :], (ckv_hi[:, t * P:(t + 1) * P], ckv_lo[:, t * P:(t + 1) * P]),
                                     tuple(v[:, 0, half * 512:(half + 1) * 512] for v in w), True, True)
                ins.then_inc(unit_done, 1)
                proj(6, lambda: m_T(0))
                proj(7, lambda: m_T(1))
                proj(8, lambda: m_T(2))
                proj(9, lambda: m_T(3))
                for j in range(4):
                    pe.wait_ge(rot_ready, c0 + 2 + j + 1)

                    if j == 2:
                        pe.wait_ge(nat_ready, c0 + 3)
                    if j == 3:
                        pe.wait_ge(mT_ready, 4)
                    for c in range(2):
                        for t in range(NT):
                            ins = nc.tensor.transpose(ps[:, FOX_T_BANK[j], c * SEQ + t * P:c * SEQ + (t + 1) * P],
                                                      nat1[j][:, t, c * P:(c + 1) * P], ident)
                    ins.then_inc(hT_done, 1)
                pe.wait_ge(lf_ready, 1)
                pe.wait_ge(nat_ready, c0 + 2)
                tri, ones = tab[:, T_TRI:T_TRI + P], tab[:, T_TRI + P:T_TRI + 2 * P]
                nc.tensor.matmul(ps[0:8, 0, 0:SEQ], lf[:, 0, :], tab[:, T_TRI:T_TRI + SEQ], start=True, stop=False)
                nc.tensor.matmul(ps[0:8, 0, P:SEQ], lf[:, 1, :], tri, start=False, stop=True)
                nc.tensor.matmul(ps[:, 0, SEQ:SEQ + 8], tri, lf[:, 0, :], start=True, stop=True)
                nc.tensor.matmul(ps[:, 0, SEQ + 8:SEQ + 16], ones, lf[:, 0, :], start=True, stop=False)
                nc.tensor.matmul(ps[:, 0, SEQ + 8:SEQ + 16], tri, lf[:, 1, :], start=False, stop=True).then_inc(dt_done, 1)

                def banks_free():
                    pe.wait_ge(hT_ready, o0 + 4)
                    pe.wait_ge(dt_ready, 1)
                    pe.wait_ge(zeros_ready, 8)

                pe.wait_ge(mT_ready, 4)
                attention(A_M1, A_END, lambda: out_proj_first(u0 + M1_OUT, 4, o_parts(4), JOBS * A_END - 1), banks_free)
                out_proj(u0 + M1_OUT, 4, lambda e: o_parts(4 + e))

            pe.wait_ge(ident_loaded, 16)
            pe.wait_ge(const_ready, 1)
            norm(0)
            ffn(0)
            norm(1)
            mixer0()
            norm(2)
            ffn(1)
            norm(3)
            ffn(2)
            norm(4)
            mixer1()
            norm(5)
            ffn(3)


def shape_tables():
    i = np.arange(P)
    t = np.zeros((P, T_COLS), np.float32)
    t[:, T_ID:T_ID + P] = np.eye(P)
    t[:, T_TRI:T_TRI + P] = i[None, :] >= i[:, None]
    t[:, T_TRI + P:T_TRI + 2 * P] = 1.0
    t[:, T_CAUSAL:T_CAUSAL + P] = np.where(i[None, :] <= i[:, None], 0.0, -BIG)
    t[:, T_BAND:T_BAND + P] = np.where(i[None, :] > i[:, None], 0.0, -BIG)
    for tile in range(NT):
        pos = (tile * P + i).astype(np.float32)[:, None]
        for at_, dim in ((T_R64 + tile * P, 64), (T_R32 + tile * 64, 32)):
            inv = (1.0 / (np.float32(10000.0) ** (np.arange(0, dim, 2, dtype=np.float32) / np.float32(dim)))).astype(np.float32)
            ang = (pos * inv[None, :]).astype(np.float32)
            c, s = np.cos(ang), np.sin(ang)
            t[:, at_:at_ + 2 * dim] = np.concatenate([c, c, -s, s], 1)
        seen = (np.arange(NCMP) * CS + CB - 1)[None, :] <= pos
        t[:, T_CNEG + tile * NCMP:T_CNEG + (tile + 1) * NCMP] = np.where(seen, 0.0, -BIG)
        t[:, T_C01 + tile * NCMP:T_C01 + (tile + 1) * NCMP] = seen
    return t


def kernel(**inputs):
    import concourse.bacc as bacc
    from concourse.bass_utils import run_bass_kernel_spmd

    nc = bacc.Bacc("TRN2", target_bir_lowering=False, num_devices=1)
    arrays = {name: np.ascontiguousarray(a) for name, a in inputs.items()}
    by_column = [arrays.pop(name).reshape(w, P).T for name, (_, w) in COLS.items()]
    by_column += [arrays.pop(name).reshape(2, P, HD).transpose(1, 0, 2).reshape(P, 2 * HD) for name in ("l0_cmpk_w2", "l0_cmpv_w2")]
    arrays["columns"] = np.ascontiguousarray(np.concatenate(by_column, 1))
    arrays["rows"] = np.concatenate([arrays.pop(name) for name in ROWS])
    arrays["shape_tables"] = shape_tables()
    A = {}
    for name, a in arrays.items():
        A[name] = nc.dram_tensor(name, a.shape, mybir.dt.from_np(a.dtype), kind="ExternalInput").ap()
    out = nc.dram_tensor("out", (1, SEQ, D), F32, kind="ExternalOutput").ap()
    trunk(nc, A, out)
    r = run_bass_kernel_spmd(nc, [arrays], core_ids=[0])
    return r.results[0]["out"]
```
